# Optimizing a Trainium2 kernel written in Bass

```python
import jax, jax.numpy as jnp
from jax import lax
import numpy as np
import math
import jax
import jax.numpy as jnp

D_MODEL = 1024
BATCH = 1
SEQ = 256
DEPTH = 1

FOURIER_GROUPS = 4
FOURIER_GROUP_DIM = 128
D_FOURIER = FOURIER_GROUPS * FOURIER_GROUP_DIM
D_CONV = D_MODEL
CONV_WIDTH = 3
N_BRANCHES = 2
D_IN_PROJ = D_FOURIER + 3 * D_CONV + N_BRANCHES * D_MODEL
N_EXPERTS = 16
EC_CAPACITY = 2
D_EXPERT = 2048
N_MOD = 6
RMS_EPS = 1e-6


def rms_norm(x, g):
    xf = x.astype(jnp.float32)
    y = xf * lax.rsqrt(jnp.mean(xf * xf, axis=-1, keepdims=True) + RMS_EPS)
    return (y * g.astype(jnp.float32)).astype(x.dtype)

def modulate(h, shift, scale):
    return h * (1 + scale[:, None, :]) + shift[:, None, :]

def fourier_mix(u):
    b, s, _ = u.shape
    ug = u.reshape(b, s, FOURIER_GROUPS, FOURIER_GROUP_DIM).astype(jnp.float32)
    f = jnp.fft.fftn(ug, axes=(1, 3), norm="ortho")
    return jnp.real(f).reshape(b, s, D_FOURIER).astype(u.dtype)

def centred_conv3(u, w):
    s = u.shape[1]
    up = jnp.pad(u, ((0, 0), (1, 1), (0, 0)))
    return up[:, 0:s] * w[0] + up[:, 1:s + 1] * w[1] + up[:, 2:s + 2] * w[2]

def expert_choice_moe(h, w_router, b_router, w_gate_e, w_up_e, w_down_e):
    b, s, d = h.shape
    cap = EC_CAPACITY * s // N_EXPERTS
    logits = jnp.einsum('bsd,de->bse', h, w_router).astype(jnp.float32) + b_router.astype(jnp.float32)
    probs = jax.nn.softmax(logits, axis=-1)
    vals, idx = lax.top_k(jnp.swapaxes(probs, 1, 2), cap)
    xe = jax.vmap(lambda hb, ib: hb[ib])(h, idx)
    a = jnp.einsum('becd,edf->becf', xe, w_gate_e)
    u = jnp.einsum('becd,edf->becf', xe, w_up_e)
    y = jnp.einsum('becf,efd->becd', jax.nn.silu(a) * u, w_down_e)
    y = y * vals[..., None].astype(y.dtype)
    return jax.vmap(lambda yb, ib: jnp.zeros((s, d), yb.dtype).at[ib.reshape(-1)].add(yb.reshape(-1, d)))(y, idx)

def first_inputs(seed: int = 0) -> dict:
    key = jax.random.key(seed)
    ks = jax.random.split(key, 20)
    f32 = jnp.float32
    nrm = lambda k, shape, scale: (jax.random.normal(k, shape, f32) * scale).astype(f32)
    D = D_MODEL
    return {
        "x": nrm(ks[0], (BATCH, SEQ, D), 1.0),
        "c": nrm(ks[1], (BATCH, D), 1.0),
        "w_ada": nrm(ks[2], (DEPTH, D, N_MOD * D), 0.5 * D ** -0.5),
        "b_ada": nrm(ks[3], (DEPTH, N_MOD * D), 0.02),
        "g_norm_mix": 1.0 + nrm(ks[4], (DEPTH, D), 0.02),
        "w_in": nrm(ks[5], (DEPTH, D, D_IN_PROJ), D ** -0.5),
        "b_gate": nrm(ks[6], (DEPTH, N_BRANCHES * D), 0.02),
        "w_fourier": nrm(ks[7], (DEPTH, D_FOURIER, D), D_FOURIER ** -0.5),
        "w_conv": nrm(ks[8], (DEPTH, CONV_WIDTH, D_CONV), CONV_WIDTH ** -0.5),
        "w_conv_out": nrm(ks[9], (DEPTH, D_CONV, D), D_CONV ** -0.5),
        "w_o": nrm(ks[10], (DEPTH, D, D), D ** -0.5),
        "g_norm_moe": 1.0 + nrm(ks[11], (DEPTH, D), 0.02),
        "w_router": nrm(ks[12], (DEPTH, D, N_EXPERTS), D ** -0.5),
        "b_router": nrm(ks[13], (DEPTH, N_EXPERTS), 0.01),
        "w_gate_e": nrm(ks[14], (DEPTH, N_EXPERTS, D, D_EXPERT), D ** -0.5),
        "w_up_e": nrm(ks[15], (DEPTH, N_EXPERTS, D, D_EXPERT), D ** -0.5),
        "w_down_e": nrm(ks[16], (DEPTH, N_EXPERTS, D_EXPERT, D), D_EXPERT ** -0.5),
        "g_final": 1.0 + nrm(ks[17], (D,), 0.02),
    }

def first_block(x, c, w_ada, b_ada, g_norm_mix, w_in, b_gate, w_fourier, w_conv, w_conv_out, w_o,
              g_norm_moe, w_router, b_router, w_gate_e, w_up_e, w_down_e, g_final):
    D = D_MODEL
    c_act = jax.nn.silu(c)
    for l in range(DEPTH):
        mod = jnp.einsum('bd,dm->bm', c_act, w_ada[l]) + b_ada[l]
        shift_m, scale_m, gate_m, shift_f, scale_f, gate_f = jnp.split(mod, N_MOD, axis=-1)

        h = modulate(rms_norm(x, g_norm_mix[l]), shift_m, scale_m)
        p = jnp.einsum('bsd,dk->bsk', h, w_in[l])
        o1 = D_FOURIER
        o2 = o1 + D_CONV
        o3 = o2 + D_CONV
        o4 = o3 + D_CONV
        u_f = p[..., :o1]
        v, b_g, c_g = p[..., o1:o2], p[..., o2:o3], p[..., o3:o4]
        g_logits = p[..., o4:] + b_gate[l]
        gate_a = jax.nn.sigmoid(g_logits[..., :D])
        gate_b = jax.nn.sigmoid(g_logits[..., D:])
        y_a = jnp.einsum('bsk,kd->bsd', fourier_mix(u_f), w_fourier[l])
        y_b = jnp.einsum('bsk,kd->bsd', b_g * centred_conv3(c_g * v, w_conv[l]), w_conv_out[l])
        z = gate_a * y_a + gate_b * y_b
        mix_out = jnp.einsum('bsd,de->bse', z, w_o[l])
        x = x + gate_m[:, None, :] * mix_out

        h2 = modulate(rms_norm(x, g_norm_moe[l]), shift_f, scale_f)
        moe_out = expert_choice_moe(h2, w_router[l], b_router[l], w_gate_e[l], w_up_e[l], w_down_e[l])
        x = x + gate_f[:, None, :] * moe_out
    return rms_norm(x, g_final)


PLE_DIM = 256
EPS = 1e-6

LRU_WIDTH = 1024
LRU_BLOCKS = 8
LRU_BLOCK = LRU_WIDTH // LRU_BLOCKS
LRU_CONV = 4
LRU_C = 8.0

N_HEADS = 8
HEAD_DIM = 128
N_KV_HEADS = 2
GROUP = N_HEADS // N_KV_HEADS
ATTN_WIDTH = N_HEADS * HEAD_DIM
KV_WIDTH = N_KV_HEADS * HEAD_DIM
IDX_HEADS = 8
IDX_DIM = 64
TOPK_MAX = 256
Q_BLOCK = 128

N_BUCKETS = 32
MAX_DISTANCE = 128

D_FF = 3072
FFN_CONV = 3

IN_SPLITS = (LRU_WIDTH, LRU_WIDTH, ATTN_WIDTH, KV_WIDTH, KV_WIDTH,
             IDX_HEADS * IDX_DIM, IDX_DIM, IDX_HEADS, D_MODEL, D_MODEL)
IN_WIDTH = sum(IN_SPLITS)


def _rmsnorm(x, g):
    x32 = x.astype(jnp.float32)
    y = x32 * lax.rsqrt(jnp.mean(x32 * x32, axis=-1, keepdims=True) + EPS)
    return (y * g.astype(jnp.float32)).astype(x.dtype)

def _split_cols(h):
    parts = []
    start = 0
    for n in IN_SPLITS:
        parts.append(h[..., start:start + n])
        start += n
    return parts

def _causal_dwconv(x, w, b):
    width = w.shape[0]
    s = x.shape[1]
    xp = jnp.pad(x, ((0, 0), (width - 1, 0), (0, 0)))
    y = b
    for j in range(width):
        y = y + xp[:, j:j + s] * w[j]
    return y

def _rg_lru(x, wa, ba, wx, bx, lam):
    b, s, _ = x.shape
    xb = x.reshape(b, s, LRU_BLOCKS, LRU_BLOCK)
    r = jax.nn.sigmoid(jnp.einsum('bsnc,ncd->bsnd', xb, wa).reshape(b, s, LRU_WIDTH) + ba)
    i = jax.nn.sigmoid(jnp.einsum('bsnc,ncd->bsnd', xb, wx).reshape(b, s, LRU_WIDTH) + bx)
    log_a = -LRU_C * r.astype(jnp.float32) * jax.nn.softplus(-lam.astype(jnp.float32))
    a = jnp.exp(log_a)
    mult = jnp.sqrt(-jnp.expm1(2.0 * log_a))
    u = mult * (i * x).astype(jnp.float32)

    def combine(left, right):
        a1, b1 = left
        a2, b2 = right
        return a1 * a2, a2 * b1 + b2

    _, h = lax.associative_scan(combine, (a, u), axis=1)
    return h.astype(x.dtype)

def _t5_bucket(dist):
    max_exact = N_BUCKETS // 2
    d_f = jnp.maximum(dist, 1).astype(jnp.float32)
    large = max_exact + (jnp.log(d_f / max_exact) / math.log(MAX_DISTANCE / max_exact)
                         * (N_BUCKETS - max_exact)).astype(jnp.int32)
    large = jnp.minimum(large, N_BUCKETS - 1)
    return jnp.where(dist < max_exact, dist, large)

def _dsa_attention(q, k, v, qi, ki, wi, rel_bias):
    b, s = q.shape[0], q.shape[1]
    n_blk = s // Q_BLOCK
    top_k = min(TOPK_MAX, s // 4)
    key_pos = jnp.arange(s, dtype=jnp.int32)
    q_pos = key_pos.reshape(n_blk, Q_BLOCK)
    ki32 = ki.astype(jnp.float32)

    def blockify(a):
        return jnp.moveaxis(a.reshape((b, n_blk, Q_BLOCK) + a.shape[2:]), 1, 0)

    def one_block(args):
        qb, qib, wib, tpos = args
        dots = jnp.einsum('bthd,bsd->bths', qib.astype(jnp.float32), ki32) * (IDX_DIM ** -0.5)
        score = jnp.einsum('bth,bths->bts', wib.astype(jnp.float32), jax.nn.relu(dots))
        causal = key_pos[None, :] <= tpos[:, None]
        score = jnp.where(causal[None], score, -jnp.inf)
        _, sel = lax.top_k(score, top_k)
        k_sel = jax.vmap(lambda kb, ib: kb[ib])(k, sel)
        v_sel = jax.vmap(lambda vb, ib: vb[ib])(v, sel)
        qg = qb.reshape(b, Q_BLOCK, N_KV_HEADS, GROUP, HEAD_DIM)
        logits = jnp.einsum('btngd,btknd->btngk', qg, k_sel).astype(jnp.float32) * (HEAD_DIM ** -0.5)
        dist = tpos[None, :, None] - sel
        bias = rel_bias[_t5_bucket(jnp.maximum(dist, 0))]
        bias = bias.reshape(b, Q_BLOCK, top_k, N_KV_HEADS, GROUP).transpose(0, 1, 3, 4, 2)
        logits = logits + bias.astype(jnp.float32)
        logits = jnp.where((dist >= 0)[:, :, None, None, :], logits, -jnp.inf)
        probs = jax.nn.softmax(logits, axis=-1).astype(v.dtype)
        o = jnp.einsum('btngk,btknd->btngd', probs, v_sel)
        return o.reshape(b, Q_BLOCK, N_HEADS, HEAD_DIM)

    out = lax.map(one_block, (blockify(q), blockify(qi), blockify(wi), q_pos))
    return jnp.moveaxis(out, 0, 1).reshape(b, s, ATTN_WIDTH)

def second_inputs(seed: int = 0) -> dict:
    key = jax.random.key(seed)
    ks = jax.random.split(key, 32)
    f32 = jnp.float32

    def nrm(k, shape, fan_in):
        return jax.random.normal(k, shape, f32) * (fan_in ** -0.5)

    def gain(k, shape):
        return 1.0 + 0.05 * jax.random.normal(k, shape, f32)

    def small(k, shape):
        return 0.01 * jax.random.normal(k, shape, f32)

    u = jax.random.uniform(ks[10], (DEPTH, LRU_WIDTH), f32, 0.9, 0.999)
    sa = u ** (1.0 / LRU_C)
    lru_lambda = jnp.log(sa) - jnp.log1p(-sa)

    return {
        'x': jax.random.normal(ks[0], (BATCH, SEQ, D_MODEL), f32),
        'p': jax.random.normal(ks[1], (DEPTH, BATCH, SEQ, PLE_DIM), f32),
        'mix_norm': gain(ks[2], (DEPTH, D_MODEL)),
        'w_in': nrm(ks[3], (DEPTH, D_MODEL, IN_WIDTH), D_MODEL),
        'lru_conv_w': nrm(ks[4], (DEPTH, LRU_CONV, LRU_WIDTH), LRU_CONV),
        'lru_conv_b': small(ks[5], (DEPTH, LRU_WIDTH)),
        'lru_wa': nrm(ks[6], (DEPTH, LRU_BLOCKS, LRU_BLOCK, LRU_BLOCK), LRU_BLOCK),
        'lru_ba': small(ks[7], (DEPTH, LRU_WIDTH)),
        'lru_wx': nrm(ks[8], (DEPTH, LRU_BLOCKS, LRU_BLOCK, LRU_BLOCK), LRU_BLOCK),
        'lru_bx': small(ks[9], (DEPTH, LRU_WIDTH)),
        'lru_lambda': lru_lambda,
        'q_norm': gain(ks[11], (DEPTH, HEAD_DIM)),
        'k_norm': gain(ks[12], (DEPTH, HEAD_DIM)),
        'rel_bias': 0.5 * jax.random.normal(ks[13], (N_BUCKETS, N_HEADS), f32),
        'w_lru_br': nrm(ks[14], (DEPTH, LRU_WIDTH, D_MODEL), LRU_WIDTH),
        'w_attn_br': nrm(ks[15], (DEPTH, ATTN_WIDTH, D_MODEL), ATTN_WIDTH),
        'w_out': nrm(ks[16], (DEPTH, D_MODEL, D_MODEL), D_MODEL),
        'ffn_norm': gain(ks[17], (DEPTH, D_MODEL)),
        'w_up': nrm(ks[18], (DEPTH, D_MODEL, 2 * D_FF), D_MODEL),
        'ffn_conv_w': nrm(ks[19], (DEPTH, FFN_CONV, D_FF), FFN_CONV),
        'ffn_conv_b': small(ks[20], (DEPTH, D_FF)),
        'w_down': nrm(ks[21], (DEPTH, D_FF, D_MODEL), D_FF),
        'ple_norm': gain(ks[22], (DEPTH, D_MODEL)),
        'w_ple_gate': nrm(ks[23], (DEPTH, D_MODEL, D_MODEL), D_MODEL),
        'w_ple_proj': nrm(ks[24], (DEPTH, PLE_DIM, D_MODEL), PLE_DIM),
    }

def second_block(x, p, mix_norm, w_in, lru_conv_w, lru_conv_b, lru_wa, lru_ba, lru_wx, lru_bx,
              lru_lambda, q_norm, k_norm, rel_bias, w_lru_br, w_attn_br, w_out, ffn_norm,
              w_up, ffn_conv_w, ffn_conv_b, w_down, ple_norm, w_ple_gate, w_ple_proj):
    b, s, _ = x.shape
    for l in range(DEPTH):
        xn = _rmsnorm(x, mix_norm[l])
        h = xn @ w_in[l]
        lru_x, lru_gate, q, k, v, qi, ki, wi, gate_a, gate_b = _split_cols(h)

        ua = _causal_dwconv(lru_x, lru_conv_w[l], lru_conv_b[l])
        ya = _rg_lru(ua, lru_wa[l], lru_ba[l], lru_wx[l], lru_bx[l], lru_lambda[l])
        ya = (ya * jax.nn.gelu(lru_gate)) @ w_lru_br[l]

        qh = _rmsnorm(q.reshape(b, s, N_HEADS, HEAD_DIM), q_norm[l])
        kh = _rmsnorm(k.reshape(b, s, N_KV_HEADS, HEAD_DIM), k_norm[l])
        vh = v.reshape(b, s, N_KV_HEADS, HEAD_DIM)
        qih = qi.reshape(b, s, IDX_HEADS, IDX_DIM)
        wih = wi * (IDX_HEADS ** -0.5)
        yb = _dsa_attention(qh, kh, vh, qih, ki, wih, rel_bias) @ w_attn_br[l]

        merged = jax.nn.sigmoid(gate_a) * ya + jax.nn.sigmoid(gate_b) * yb
        x = x + merged @ w_out[l]

        xn = _rmsnorm(x, ffn_norm[l])
        up = xn @ w_up[l]
        g_ffn = _causal_dwconv(up[..., :D_FF], ffn_conv_w[l], ffn_conv_b[l])
        x = x + (jax.nn.gelu(g_ffn) * up[..., D_FF:]) @ w_down[l]

        g_ple = jax.nn.sigmoid(_rmsnorm(x, ple_norm[l]) @ w_ple_gate[l])
        x = x + g_ple * (p[l] @ w_ple_proj[l])
    return x


DEPTH_3 = 2

N_MIXERS = 3
HEAD_DIM_3 = 64
N_HEADS_3 = D_MODEL // HEAD_DIM_3
D_FF_3 = 2816
ROPE_THETA = 10000.0
BLOCK_Q = 128
NEG = -1e30

NSA_GROUPS = 4
NSA_REP = N_HEADS_3 // NSA_GROUPS
NSA_CMP_LEN = 32
NSA_CMP_STRIDE = 16
NSA_CMP_HIDDEN = 2 * HEAD_DIM_3
NSA_SLC_LEN = 64
NSA_TOPK = 16
NSA_WINDOW = 512
NSA_SLC_QBLOCK = 32
NSA_FORCE_BONUS = 1e4

SWA_KV_HEADS = 2
SWA_REP = N_HEADS_3 // SWA_KV_HEADS
SWA_WINDOW = 128

FOX_HEADS = N_HEADS_3

N_A = len(range(0, DEPTH_3, N_MIXERS))
N_B = len(range(1, DEPTH_3, N_MIXERS))
N_C = len(range(2, DEPTH_3, N_MIXERS))

Q_WIDTH = N_HEADS_3 * HEAD_DIM_3
NSA_KV_WIDTH = 3 * 2 * NSA_GROUPS * HEAD_DIM_3
NSA_IN = Q_WIDTH + NSA_KV_WIDTH + 3 * N_HEADS_3
SWA_IN = Q_WIDTH + 2 * SWA_KV_HEADS * HEAD_DIM_3
FOX_IN = 3 * FOX_HEADS * HEAD_DIM_3 + FOX_HEADS


def rmsnorm(x, g):
    xf = x.astype(jnp.float32)
    y = xf * lax.rsqrt(jnp.mean(xf * xf, axis=-1, keepdims=True) + RMS_EPS)
    return (y * g.astype(jnp.float32)).astype(x.dtype)

def swiglu(x, w_gu, w_down):
    g, u = jnp.split(x @ w_gu, 2, axis=-1)
    return (jax.nn.silu(g) * u) @ w_down

def rope_tables(S):
    inv = ROPE_THETA ** (-jnp.arange(0, HEAD_DIM_3, 2, dtype=jnp.float32) / HEAD_DIM_3)
    ang = jnp.arange(S, dtype=jnp.float32)[:, None] * inv[None, :]
    return jnp.cos(ang), jnp.sin(ang)

def apply_rope(x, cos, sin):
    x1, x2 = jnp.split(x.astype(jnp.float32), 2, axis=-1)
    c = cos[None, :, None, :]
    s = sin[None, :, None, :]
    return jnp.concatenate([x1 * c - x2 * s, x2 * c + x1 * s], axis=-1).astype(x.dtype)

def banded_attention(q, k, v, window, sinks=None):
    B, S, G, R, dh = q.shape
    span = window + BLOCK_Q
    kp = jnp.pad(k, ((0, 0), (window, 0), (0, 0), (0, 0)))
    vp = jnp.pad(v, ((0, 0), (window, 0), (0, 0), (0, 0)))
    scale = dh ** -0.5

    def step(i):
        start = i * BLOCK_Q
        qi = lax.dynamic_slice_in_dim(q, start, BLOCK_Q, axis=1)
        ki = lax.dynamic_slice_in_dim(kp, start, span, axis=1)
        vi = lax.dynamic_slice_in_dim(vp, start, span, axis=1)
        s = jnp.einsum('bqgrd,bkgd->bgrqk', qi, ki).astype(jnp.float32) * scale
        qpos = start + jnp.arange(BLOCK_Q)
        kpos = start - window + jnp.arange(span)
        diff = qpos[:, None] - kpos[None, :]
        mask = (diff >= 0) & (diff < window) & (kpos[None, :] >= 0)
        s = jnp.where(mask, s, NEG)
        if sinks is None:
            p = jax.nn.softmax(s, axis=-1)
        else:
            sk = sinks.astype(jnp.float32)[None, :, :, None, None]
            m = jnp.maximum(jnp.max(s, axis=-1, keepdims=True), sk)
            e = jnp.exp(s - m)
            p = e / (jnp.sum(e, axis=-1, keepdims=True) + jnp.exp(sk - m))
        return jnp.einsum('bgrqk,bkgd->bqgrd', p.astype(vi.dtype), vi)

    o = lax.map(step, jnp.arange(S // BLOCK_Q))
    return jnp.moveaxis(o, 0, 1).reshape(B, S, G, R, dh)

def compress_blocks(x, blk_idx, pe, w1, w2):
    B, _, G, dh = x.shape
    n_cmp, L = blk_idx.shape
    xb = x[:, blk_idx] + pe[:, None, :]
    xb = xb.transpose(0, 1, 3, 2, 4).reshape(B, n_cmp, G, L * dh)
    return jax.nn.gelu(xb @ w1) @ w2

def cmp_to_slc_overlap(n_cmp, n_slc):
    cs = np.arange(n_cmp) * NSA_CMP_STRIDE
    ce = cs + NSA_CMP_LEN
    ss = np.arange(n_slc) * NSA_SLC_LEN
    se = ss + NSA_SLC_LEN
    ov = np.clip(np.minimum(ce[:, None], se[None, :]) - np.maximum(cs[:, None], ss[None, :]), 0, None)
    return jnp.asarray(ov / NSA_CMP_LEN, dtype=jnp.float32)

def selected_block_attention(q, k, v, sel):
    B, S, G, R, dh = q.shape
    n_sel = sel.shape[-1]
    n_slc = S // NSA_SLC_LEN
    m = n_sel * NSA_SLC_LEN
    kblk = k.reshape(B, n_slc, NSA_SLC_LEN, G, dh).transpose(0, 3, 1, 2, 4)
    vblk = v.reshape(B, n_slc, NSA_SLC_LEN, G, dh).transpose(0, 3, 1, 2, 4)
    gather = jax.vmap(jax.vmap(lambda blocks, ids: blocks[ids]))
    offs = jnp.arange(NSA_SLC_LEN)
    scale = dh ** -0.5

    def step(i):
        start = i * NSA_SLC_QBLOCK
        qi = lax.dynamic_slice_in_dim(q, start, NSA_SLC_QBLOCK, axis=1)
        ids = lax.dynamic_slice_in_dim(sel, start, NSA_SLC_QBLOCK, axis=2)
        kg = gather(kblk, ids).reshape(B, G, NSA_SLC_QBLOCK, m, dh)
        vg = gather(vblk, ids).reshape(B, G, NSA_SLC_QBLOCK, m, dh)
        kpos = (ids[..., None] * NSA_SLC_LEN + offs).reshape(B, G, NSA_SLC_QBLOCK, m)
        qpos = start + jnp.arange(NSA_SLC_QBLOCK)
        mask = (kpos <= qpos[:, None])[:, :, None]
        s = jnp.einsum('bqgrd,bgqmd->bgrqm', qi, kg).astype(jnp.float32) * scale
        p = jax.nn.softmax(jnp.where(mask, s, NEG), axis=-1)
        return jnp.einsum('bgrqm,bgqmd->bqgrd', p.astype(vg.dtype), vg)

    o = lax.map(step, jnp.arange(S // NSA_SLC_QBLOCK))
    return jnp.moveaxis(o, 0, 1).reshape(B, S, G, R, dh)

def nsa_mixer(h, cos, sin, w_in, ck_pe, ck_w1, ck_w2, cv_pe, cv_w1, cv_w2, w_out):
    B, S, _ = h.shape
    G, R, dh = NSA_GROUPS, NSA_REP, HEAD_DIM_3
    scale = dh ** -0.5
    proj = h @ w_in
    q = apply_rope(proj[..., :Q_WIDTH].reshape(B, S, N_HEADS_3, dh), cos, sin).reshape(B, S, G, R, dh)
    kv = proj[..., Q_WIDTH:Q_WIDTH + NSA_KV_WIDTH].reshape(B, S, 3, 2, G, dh)
    gates = jax.nn.sigmoid(proj[..., Q_WIDTH + NSA_KV_WIDTH:].astype(jnp.float32)).reshape(B, S, 3, G, R, 1)
    k = apply_rope(kv[:, :, :, 0].reshape(B, S, 3 * G, dh), cos, sin).reshape(B, S, 3, G, dh)
    v = kv[:, :, :, 1]
    t = jnp.arange(S)

    n_cmp = (S - NSA_CMP_LEN) // NSA_CMP_STRIDE + 1
    blk_idx = jnp.arange(n_cmp)[:, None] * NSA_CMP_STRIDE + jnp.arange(NSA_CMP_LEN)[None, :]
    k_cmp = compress_blocks(k[:, :, 0], blk_idx, ck_pe, ck_w1, ck_w2)
    v_cmp = compress_blocks(v[:, :, 0], blk_idx, cv_pe, cv_w1, cv_w2)
    s_cmp = jnp.einsum('bsgrd,bngd->bgrsn', q, k_cmp).astype(jnp.float32) * scale
    cmp_valid = (jnp.arange(n_cmp) * NSA_CMP_STRIDE + NSA_CMP_LEN - 1)[None, :] <= t[:, None]
    p_cmp = jax.nn.softmax(jnp.where(cmp_valid, s_cmp, NEG), axis=-1) * cmp_valid
    o_cmp = jnp.einsum('bgrsn,bngd->bsgrd', p_cmp.astype(v_cmp.dtype), v_cmp)

    n_slc = S // NSA_SLC_LEN
    k_sel = min(NSA_TOPK, n_slc)
    imp = jnp.einsum('bgrsn,nj->bgsj', p_cmp, cmp_to_slc_overlap(n_cmp, n_slc))
    tb = (t // NSA_SLC_LEN)[:, None]
    j = jnp.arange(n_slc)[None, :]
    forced = (j == 0) | (j == tb) | (j == tb - 1)
    imp = jnp.where(j > tb, NEG, jnp.where(forced, NSA_FORCE_BONUS, imp))
    _, sel = lax.top_k(imp, k_sel)
    o_slc = selected_block_attention(q, k[:, :, 1], v[:, :, 1], sel)

    o_win = banded_attention(q, k[:, :, 2], v[:, :, 2], NSA_WINDOW)

    o = gates[:, :, 0] * o_cmp + gates[:, :, 1] * o_slc + gates[:, :, 2] * o_win
    return o.astype(h.dtype).reshape(B, S, Q_WIDTH) @ w_out

def swa_mixer(h, cos, sin, w_in, sinks, w_out):
    B, S, _ = h.shape
    proj = h @ w_in
    q = apply_rope(proj[..., :Q_WIDTH].reshape(B, S, N_HEADS_3, HEAD_DIM_3), cos, sin)
    q = q.reshape(B, S, SWA_KV_HEADS, SWA_REP, HEAD_DIM_3)
    kv = proj[..., Q_WIDTH:].reshape(B, S, 2, SWA_KV_HEADS, HEAD_DIM_3)
    k = apply_rope(kv[:, :, 0], cos, sin)
    v = kv[:, :, 1]
    o = banded_attention(q, k, v, SWA_WINDOW, sinks.reshape(SWA_KV_HEADS, SWA_REP))
    return o.reshape(B, S, Q_WIDTH) @ w_out

def fox_mixer(h, w_in, b_f, w_out):
    B, S, _ = h.shape
    dh = HEAD_DIM_3
    scale = dh ** -0.5
    proj = h @ w_in
    qkv = proj[..., :3 * FOX_HEADS * dh].reshape(B, S, 3, FOX_HEADS, dh)
    q, k, v = qkv[:, :, 0], qkv[:, :, 1], qkv[:, :, 2]
    log_f = jax.nn.log_sigmoid((proj[..., 3 * FOX_HEADS * dh:] + b_f).astype(jnp.float32))
    c = jnp.cumsum(log_f, axis=1).transpose(0, 2, 1)
    kpos = jnp.arange(S)

    def step(i):
        start = i * BLOCK_Q
        qi = lax.dynamic_slice_in_dim(q, start, BLOCK_Q, axis=1)
        ci = lax.dynamic_slice_in_dim(c, start, BLOCK_Q, axis=2)
        s = jnp.einsum('bqhd,bkhd->bhqk', qi, k).astype(jnp.float32) * scale
        s = s + ci[..., None] - c[:, :, None, :]
        qpos = start + jnp.arange(BLOCK_Q)
        p = jax.nn.softmax(jnp.where(kpos[None, :] <= qpos[:, None], s, NEG), axis=-1)
        return jnp.einsum('bhqk,bkhd->bqhd', p.astype(v.dtype), v)

    o = lax.map(step, jnp.arange(S // BLOCK_Q))
    return jnp.moveaxis(o, 0, 1).reshape(B, S, FOX_HEADS * dh) @ w_out

def third_inputs(seed: int = 0) -> dict:
    key = jax.random.key(seed)
    ks = iter(jax.random.split(key, 32))
    f32 = jnp.float32

    def nrm(shape, scale):
        return scale * jax.random.normal(next(ks), shape, f32)

    def gain(shape):
        return 1.0 + 0.01 * jax.random.normal(next(ks), shape, f32)

    L, dh, Hc = NSA_CMP_LEN, HEAD_DIM_3, NSA_CMP_HIDDEN
    return {
        'x': nrm((BATCH, SEQ, D_MODEL), 1.0),
        'ffn1_norm': gain((DEPTH_3, D_MODEL)),
        'ffn1_w_gu': nrm((DEPTH_3, D_MODEL, 2 * D_FF_3), D_MODEL ** -0.5),
        'ffn1_w_down': nrm((DEPTH_3, D_FF_3, D_MODEL), D_FF_3 ** -0.5),
        'mix_norm': gain((DEPTH_3, D_MODEL)),
        'ffn2_norm': gain((DEPTH_3, D_MODEL)),
        'ffn2_w_gu': nrm((DEPTH_3, D_MODEL, 2 * D_FF_3), D_MODEL ** -0.5),
        'ffn2_w_down': nrm((DEPTH_3, D_FF_3, D_MODEL), D_FF_3 ** -0.5),
        'nsa_w_in': nrm((N_A, D_MODEL, NSA_IN), D_MODEL ** -0.5),
        'nsa_ck_pe': nrm((N_A, L, dh), 0.1),
        'nsa_ck_w1': nrm((N_A, L * dh, Hc), (L * dh) ** -0.5),
        'nsa_ck_w2': nrm((N_A, Hc, dh), Hc ** -0.5),
        'nsa_cv_pe': nrm((N_A, L, dh), 0.1),
        'nsa_cv_w1': nrm((N_A, L * dh, Hc), (L * dh) ** -0.5),
        'nsa_cv_w2': nrm((N_A, Hc, dh), Hc ** -0.5),
        'nsa_w_out': nrm((N_A, Q_WIDTH, D_MODEL), Q_WIDTH ** -0.5),
        'swa_w_in': nrm((N_B, D_MODEL, SWA_IN), D_MODEL ** -0.5),
        'swa_sinks': nrm((N_B, N_HEADS_3), 1.0),
        'swa_w_out': nrm((N_B, Q_WIDTH, D_MODEL), Q_WIDTH ** -0.5),
        'fox_w_in': nrm((N_C, D_MODEL, FOX_IN), D_MODEL ** -0.5),
        'fox_b_f': jax.random.uniform(next(ks), (N_C, FOX_HEADS), f32, 1.0, 4.0),
        'fox_w_out': nrm((N_C, FOX_HEADS * HEAD_DIM_3, D_MODEL), (FOX_HEADS * HEAD_DIM_3) ** -0.5),
        'final_norm': gain((D_MODEL,)),
    }

def third_block(x, ffn1_norm, ffn1_w_gu, ffn1_w_down, mix_norm, ffn2_norm, ffn2_w_gu, ffn2_w_down,
              nsa_w_in, nsa_ck_pe, nsa_ck_w1, nsa_ck_w2, nsa_cv_pe, nsa_cv_w1, nsa_cv_w2, nsa_w_out,
              swa_w_in, swa_sinks, swa_w_out, fox_w_in, fox_b_f, fox_w_out, final_norm):
    S = x.shape[1]
    cos, sin = rope_tables(S)
    for i in range(DEPTH_3):
        kind, j = i % N_MIXERS, i // N_MIXERS
        x = x + 0.5 * swiglu(rmsnorm(x, ffn1_norm[i]), ffn1_w_gu[i], ffn1_w_down[i])
        h = rmsnorm(x, mix_norm[i])
        if kind == 0:
            y = nsa_mixer(h, cos, sin, nsa_w_in[j], nsa_ck_pe[j], nsa_ck_w1[j], nsa_ck_w2[j],
                          nsa_cv_pe[j], nsa_cv_w1[j], nsa_cv_w2[j], nsa_w_out[j])
        elif kind == 1:
            y = swa_mixer(h, cos, sin, swa_w_in[j], swa_sinks[j], swa_w_out[j])
        else:
            y = fox_mixer(h, fox_w_in[j], fox_b_f[j], fox_w_out[j])
        x = x + y
        x = x + 0.5 * swiglu(rmsnorm(x, ffn2_norm[i]), ffn2_w_gu[i], ffn2_w_down[i])
    return rmsnorm(x, final_norm)


def setup_inputs(seed=0):
    out = dict(first_inputs(seed))
    for name, value in second_inputs(seed + 1).items():
        if name != "x":
            out[name + "_2"] = value
    for name, value in third_inputs(seed + 2).items():
        if name != "x":
            out[name + "_3"] = value
    return out


def reference(
    x, c, w_ada, b_ada, g_norm_mix, w_in, b_gate, w_fourier, w_conv, w_conv_out, w_o,
    g_norm_moe, w_router, b_router, w_gate_e, w_up_e, w_down_e, g_final, p_2, mix_norm_2,
    w_in_2, lru_conv_w_2, lru_conv_b_2, lru_wa_2, lru_ba_2, lru_wx_2, lru_bx_2, lru_lambda_2,
    q_norm_2, k_norm_2, rel_bias_2, w_lru_br_2, w_attn_br_2, w_out_2, ffn_norm_2, w_up_2,
    ffn_conv_w_2, ffn_conv_b_2, w_down_2, ple_norm_2, w_ple_gate_2, w_ple_proj_2, ffn1_norm_3,
    ffn1_w_gu_3, ffn1_w_down_3, mix_norm_3, ffn2_norm_3, ffn2_w_gu_3, ffn2_w_down_3, nsa_w_in_3,
    nsa_ck_pe_3, nsa_ck_w1_3, nsa_ck_w2_3, nsa_cv_pe_3, nsa_cv_w1_3, nsa_cv_w2_3, nsa_w_out_3,
    swa_w_in_3, swa_sinks_3, swa_w_out_3, fox_w_in_3, fox_b_f_3, fox_w_out_3, final_norm_3,
):
    x = first_block(
        x, c, w_ada, b_ada, g_norm_mix, w_in, b_gate, w_fourier, w_conv, w_conv_out, w_o,
        g_norm_moe, w_router, b_router, w_gate_e, w_up_e, w_down_e, g_final,
    )
    x = second_block(
        x, p_2, mix_norm_2, w_in_2, lru_conv_w_2, lru_conv_b_2, lru_wa_2, lru_ba_2, lru_wx_2,
        lru_bx_2, lru_lambda_2, q_norm_2, k_norm_2, rel_bias_2, w_lru_br_2, w_attn_br_2,
        w_out_2, ffn_norm_2, w_up_2, ffn_conv_w_2, ffn_conv_b_2, w_down_2, ple_norm_2,
        w_ple_gate_2, w_ple_proj_2,
    )
    return third_block(
        x, ffn1_norm_3, ffn1_w_gu_3, ffn1_w_down_3, mix_norm_3, ffn2_norm_3, ffn2_w_gu_3,
        ffn2_w_down_3, nsa_w_in_3, nsa_ck_pe_3, nsa_ck_w1_3, nsa_ck_w2_3, nsa_cv_pe_3,
        nsa_cv_w1_3, nsa_cv_w2_3, nsa_w_out_3, swa_w_in_3, swa_sinks_3, swa_w_out_3, fox_w_in_3,
        fox_b_f_3, fox_w_out_3, final_norm_3,
    )


_drawn_inputs = setup_inputs


def setup_inputs(seed=0):
    import zlib

    import numpy as np

    out = dict(_drawn_inputs(seed))
    spreads = {}
    factors = {'g_norm_mix': 3.415,
     'b_gate': 7.129,
     'g_norm_moe': 4.852,
     'b_router': 8.0,
     'lru_conv_b_2': 3.728,
     'lru_ba_2': 8.0,
     'lru_bx_2': 8.0,
     'q_norm_2': 7.429,
     'k_norm_2': 7.9,
     'ffn_conv_b_2': 8.0,
     'ple_norm_2': 6.779,
     'ffn1_norm_3': 8.0,
     'mix_norm_3': 8.0,
     'ffn2_norm_3': 8.0,
     'nsa_ck_pe_3': 8.0,
     'swa_sinks_3': 166.33,
     'final_norm_3': 186.408,
     'nsa_cv_pe_3': 8.0}
    for name, (base, spread) in spreads.items():
        noise = np.random.default_rng([zlib.crc32(name.encode()), seed]).standard_normal(out[name].shape)
        drawn = base * np.exp(spread * noise) if base else spread * noise
        out[name] = jnp.asarray(drawn.astype(out[name].dtype))
    for name, factor in factors.items():
        out[name] = (out[name] * factor).astype(out[name].dtype)
    return out
```

```python
from contextlib import ExitStack

import numpy as np

import concourse.bass as bass
from concourse import mybir

T, D = 256, 1024
P = 128
TT, DC = T // P, D // P
EPS = 1e-6
NEG = -1e30
NE, CAP, DE = 16, 32, 2048
F2, F3 = 3072, 2816
NSLOT, SLAB = 3, 4096
NB, BL, BS = 15, 32, 16


def shape_constants():
    i128 = np.arange(P)
    tok = np.arange(T)
    parts = {}
    parts["ident"] = np.eye(P)
    parts["tri"] = (i128[:, None] < i128[None, :])
    ang = 2 * np.pi * ((tok[:, None] * tok[None, :]) % T) / T
    norm = 1 / math_sqrt(T * P)
    cs = np.concatenate([np.cos(ang), -np.sin(ang)], 1) * norm
    parts["dft_seq"] = cs.reshape(TT, P, 2 * T).transpose(1, 0, 2).reshape(P, -1)
    angc = 2 * np.pi * ((i128[:, None] * i128[None, :]) % P) / P
    parts["dft_cos"] = np.cos(angc)
    parts["dft_sin"] = np.sin(angc)
    t = tok.reshape(TT, P).T[:, :, None]
    s = tok[None, None, :]
    parts["causal"] = np.where(s <= t, 0.0, NEG).reshape(P, -1)
    parts["window"] = np.where((s <= t) & (t - s < P), 0.0, NEG).reshape(P, -1)
    n = np.arange(NB)[None, None, :]
    valid = (n * BS + BL - 1 <= t)
    parts["cmp_neg"] = np.where(valid, 0.0, NEG).reshape(P, -1)
    parts["cmp_one"] = valid.reshape(P, -1)
    parts["iota"] = np.broadcast_to(np.arange(CAP), (P, CAP))
    inv = (np.float32(10000.0) ** (-np.arange(0, 64, 2, dtype=np.float32) / np.float32(64)))
    rope = tok.astype(np.float32)[None, :] * inv.astype(np.float32)[:, None]
    parts["rope_cos"] = np.tile(np.cos(rope), (4, 1))
    parts["rope_sin"] = np.tile(np.sin(rope), (4, 1))
    rot = np.zeros((P, P))
    for h in range(0, P, 64):
        for j in range(32):
            rot[h + 32 + j, h + j] = -1.0
            rot[h + j, h + 32 + j] = 1.0
    parts["rope_rot"] = rot
    dist = np.maximum(255 - np.arange(2 * T), 0)
    df = np.maximum(dist, 1).astype(np.float32)
    large = 16 + (np.log(df / np.float32(16)) / np.float32(math_log(128 / 16)) * np.float32(16)).astype(np.int32)
    bucket = np.where(dist < 16, dist, np.minimum(large, 31))
    oh = np.zeros((P, 2 * T))
    oh[bucket, np.arange(2 * T)] = 1.0
    parts["buckets"] = oh
    return pack(parts)


def math_sqrt(v):
    return float(np.sqrt(v))


def math_log(v):
    return float(np.log(v))


def pack(parts):
    at, where, cols = 0, {}, []
    for name, a in parts.items():
        a = np.asarray(a, np.float32).reshape(P, -1)
        where[name] = (at, a.shape[1])
        at += a.shape[1]
        cols.append(a)
    return np.ascontiguousarray(np.concatenate(cols, 1)), where


def column_inputs(v):
    def col(a):
        a = a.reshape(-1, P)
        return a.T
    parts = {"c": col(v("c"))}
    for name in ("b_ada", "g_norm_mix", "b_gate", "w_conv", "g_norm_moe", "mix_norm_2", "lru_conv_w_2",
                 "lru_conv_b_2", "lru_ba_2", "lru_bx_2", "lru_lambda_2", "q_norm_2", "k_norm_2", "ffn_norm_2",
                 "ffn_conv_w_2", "ffn_conv_b_2", "ple_norm_2", "ffn1_norm_3", "mix_norm_3", "ffn2_norm_3",
                 "nsa_ck_pe_3", "nsa_cv_pe_3"):
        parts[name] = col(v(name))
    return pack(parts)


def row_inputs(v):
    b_ada = v("b_ada").reshape(-1)
    parts = {"g_final": v("g_final"), "gate_m": b_ada[2 * D:3 * D],
             "gate_f": b_ada[5 * D:6 * D], "b_router": v("b_router"), "sinks": v("swa_sinks_3")}
    at, where, rows = 0, {}, []
    for name, a in parts.items():
        a = a.reshape(1, -1)
        where[name] = (at, a.shape[1])
        at += a.shape[1]
        rows.append(a)
    return np.ascontiguousarray(np.concatenate(rows, 1)), where


class Plan:

    def __init__(self):
        self.batch0, self.work0, self.slab0, self.kinds, self.times = {}, {}, {}, {}, {}
        self.slab0_body = {}
        self.batches = self.works = self.slabs = 0
        self.slab_end = []

    def add(self, name, kinds, frees=(), times=1):
        self.batch0[name], self.work0[name], self.slab0[name] = self.batches, self.works, self.slabs
        self.kinds[name], self.times[name] = kinds, times
        self.slab0_body[name] = len(frees)
        for k in range(times):
            self.slab_end += [self.batches + k * len(kinds) + f + 1 for f in frees]
        self.batches += times * len(kinds)
        self.works += times * kinds.count("W")
        self.slabs += times * len(frees)

    def done(self, name, i):
        return self.batch0[name] + i + 1

    def work(self, name, i):
        return self.work0[name] + self.kinds[name][:i].count("W")


def make_plan():
    p = Plan()
    p.add("ada", "WW" * 12, [2 * m for m in range(12)])
    p.add("norm0", "WWWW")
    p.add("uf", "WW", [1])
    p.add("dft_a", "WWWW")
    p.add("dft_b", "WW")
    p.add("vbc", "WW" * 6, [2 * s + 1 for s in range(6)])
    p.add("gates", "WW" * 4, [2 * s + 1 for s in range(4)])
    p.add("fourier_out", "WWWW", [3])
    p.add("conv_out", "WWWW", [1, 3])
    p.add("w_o", "AA", [0, 1])
    p.add("norm1", "WWWW")
    p.add("router", "W")
    p.add("probsT", "W")
    p.add("maskT", "W")
    p.add("slots", "W")
    p.add("scatterT", "W" * 8)
    p.add("gather", "W" * 8)
    p.add("experts", "AAAW" + "AAAW" + "W" + "AAAW" + "A", [0, 1, 2, 3, 4, 5, 6, 7, 9, 10, 11, 12], times=NE)
    p.add("experts_end", "A")
    p.add("norm2", "WWWW")
    p.add("lru_x", "WWWW", [1, 3])
    p.add("lru_ri", "W" * 8, [7])
    p.add("lru_gate", "WWWW", [1, 3])
    p.add("q", "WWWW", [1, 3])
    p.add("kv", "WW", [1])
    p.add("qi", "WW", [1])
    p.add("kiwi", "WW")
    p.add("qk_ms", "W" * 5)
    p.add("bias", "W" * 8)
    p.add("score", "W" * 8)
    p.add("gate_a", "WWWW", [1, 3])
    p.add("lru_out", "WWWW", [1, 3])
    p.add("gate_b", "WWWW", [1, 3])
    p.add("logits2", "W" * 8)
    p.add("pv2", "WWW" * 4)
    p.add("attn_out", "WWWW", [1, 3])
    p.add("w_out2", "AA", [0, 1])
    p.add("norm3", "WWWW")
    p.add("ffn2", "WWWWA", [1, 3, 4], times=F2 // 512)
    p.add("ffn2_end", "A")
    p.add("norm4", "WWWW")
    p.add("ple", "WW" * 2 + "WWWW", [1, 3, 7])
    for n in range(4):
        p.add(f"ffnorm{n}", "WWWW")
        p.add(f"ffn3_{n}", "WWWWA", [1, 3, 4], times=5)
        p.add(f"ffn3_{n}_end", "WWA", [1, 2])
        if n == 0:
            p.add("nsa_norm", "WWWW")
            p.add("nsa_q", "WWWW", [1, 3])
            p.add("nsa_kv0", "WW", [1])
            p.add("nsa_kv12", "WW" * 2, [1, 3])
            p.add("nsa_g", "W")
            p.add("nsa_rope", "W" * 7)
            p.add("cmp_hid", "WW", [1])
            p.add("cmp_kv", "WW")
            p.add("cmp_s", "WW")
            p.add("nsa_heads", "W" * 10 * 8)
            p.add("nsa_out", "AA", [0, 1])
        if n == 2:
            p.add("swa_norm", "WWWW")
            p.add("swa_q", "WWWW", [1, 3])
            p.add("swa_kv", "W", [0])
            p.add("swa_rope", "W" * 5)
            p.add("swa_heads", "W" * 5 * 8)
            p.add("swa_out", "AA", [0, 1])
    return p


def network(nc, dram, out, const_at, col_at, row_at):
    fp32 = mybir.dt.float32
    ALU = mybir.AluOpType
    ACT = mybir.ActivationFunctionType
    AX = mybir.AxisListType
    plan = make_plan()
    ctx = ExitStack()

    def sb(name, shape):
        return ctx.enter_context(nc.sbuf_tensor(name, shape, fp32))

    def sem(name):
        return ctx.enter_context(nc.semaphore(name))

    n_const = sum(w for _, w in const_at.values())
    n_col = sum(w for _, w in col_at.values())
    n_row = sum(w for _, w in row_at.values())
    ring = [sb(f"ring{i}", [P, SLAB]) for i in range(NSLOT)]
    consts = sb("consts", [P, n_const])
    cols = sb("cols", [P, n_col])
    rows = sb("rows", [P, n_row])
    x = sb("x", [P, TT, D])
    xn = sb("xn", [P, TT, D])
    hT = sb("hT", [P, DC, T])
    AB, AC = sb("AB", [P, 4096]), sb("AC", [P, 4096])
    A = [sb(f"A{i}", [P, 2048]) for i in range(9) if i not in (1, 2)]
    A[1:1] = [AC[:, 0:2048], AC[:, 2048:4096]]
    w_router = sb("w_router_sb", [P, DC, NE])
    w_kiwi = sb("w_kiwi", [P, DC, 72])
    w_nsa_gate = sb("w_nsa_gate", [P, DC, 48])
    ck_w2 = sb("ck_w2", [P, 64])
    cv_w2 = sb("cv_w2", [P, 64])
    pT_in = sb("pT_in", [P, 2, T])
    rel_in = sb("rel_in", [32, 8])
    ones = sb("ones", [P, P])
    ones_mean = sb("ones_mean", [P, P])
    zeros = sb("zeros", [P, P])
    neg_half = sb("neg_half", [P, TT])
    tmp = [sb(f"tmp{i}", [P, 512]) for i in range(4)]
    small = sb("small", [P, 640])

    def const(name, shape=None, **k):
        at, n = const_at[name]
        v = consts[:, at:at + n]
        return v.rearrange(shape, **k) if shape else v

    def col(name, i=0, n=1):
        return cols[:, col_at[name][0] + i:col_at[name][0] + i + n]

    def row(name):
        at, n = row_at[name]
        return rows[:, at:at + n]

    small_at = [0]

    def narrow(n):
        small_at[0] += n
        assert small_at[0] <= 640
        return small[:, small_at[0] - n:small_at[0]]

    ident = const("ident")
    causal = const("causal", "p (t s) -> p t s", t=TT)
    window = const("window", "p (t s) -> p t s", t=TT)
    fm = lambda a: a[:, :].rearrange("p (c t) -> p c t", t=T)

    junk = hT[:, 0:4, :].rearrange("p c t -> p (c t)")
    rel_rep = xn[0:32, 0, :].rearrange("p (h n) -> p h n", h=8)

    ss, ms, rstd = narrow(2), narrow(2), narrow(2)
    c_act = narrow(8)
    c_pad = A[0][:, 0:256].rearrange("p (k m) -> p k m", m=32)
    mod_part = [tmp[0], tmp[1]]
    modc = narrow(48)
    g_mix, g_moe = narrow(8), narrow(8)
    uf = A[0][:, 0:1024].rearrange("p (t n) -> p t n", t=TT)
    dft_v = A[1][:, :].rearrange("p (g n) -> p g n", g=4)
    yT = A[0][:, 1024:2048].rearrange("p (g t) -> p g t", g=4)
    f_v, f_b, f_cv, f_ga, f_gb, f_bc, f_z = (fm(A[i]) for i in (2, 3, 4, 5, 6, 7, 8))
    logit = narrow(32).rearrange("p (t e) -> p t e", t=TT)
    prob = narrow(32).rearrange("p (t e) -> p t e", t=TT)
    rmax, rsum = narrow(2), narrow(2)
    probT = tmp[0][0:NE, 0:T]
    probW = tmp[1][0:NE, 0:T]
    mask = tmp[2][0:NE, 0:T]
    top8 = narrow(8)
    maskT = narrow(32).rearrange("p (t e) -> p t e", t=TT)
    slot_of = narrow(32).rearrange("p (t e) -> p t e", t=TT)
    sel = A[0][:, 0:1024].rearrange("p (t e s) -> p t e s", t=TT, e=NE)
    sel_prob = AB[:, :].rearrange("p (t e g s) -> p t e g s", t=TT, e=NE, g=4)
    scat = AC[:, :].rearrange("p (e t) -> p e t", e=NE)
    xeT = AB[:, :].rearrange("p (c s) -> p c s", c=DC)
    xe_now = A[3][:, 0:256].rearrange("p (c s) -> p c s", c=DC)
    scat_now = A[3][:, 256:512]
    e_act, e_h, e_hT, e_y = (A[3][:, 512:1024], A[3][:, 1024:1536], A[3][:, 1536:2048], A[4][:, 0:512])
    l_t, l_ua, l_a, l_i, l_tmp, l_g = (fm(A[i]) for i in (0, 1, 2, 3, 4, 8))
    sp8, nsp8, sp_a, sp_b = narrow(8), narrow(8), narrow(8), narrow(8)
    q2 = fm(A[7])
    sq2 = fm(A[6])
    k2 = A[5][:, 0:512].rearrange("p (g t) -> p g t", g=2)
    v2 = A[5][:, 512:1024].rearrange("p (t n) -> p t n", t=TT)
    qi = A[5][:, 1024:2048].rearrange("p (c t) -> p c t", t=T)
    ki = tmp[0][:, :].rearrange("p (d t) -> p d t", d=2)
    wi = narrow(16).rearrange("p (t h) -> p t h", t=TT)
    sqk = tmp[1]
    bias2 = AB[:, :].rearrange("p (t h s) -> p t h s", t=TT, h=8)
    bias_row = AB[:, :].rearrange("p (h j) -> p h j", h=8)
    msq = [tmp[2], tmp[3]]
    relu_s = [A[6][:, 0:512], A[6][:, 512:1024]]
    score = A[6][:, 1024:1536].rearrange("p (t s) -> p t s", t=TT)
    score_w = A[6][:, 1536:2048].rearrange("p (t s) -> p t s", t=TT)
    t8 = narrow(8)
    att = [fm(A[4]), fm(A[8])]
    nm2 = narrow(16).rearrange("p (t h) -> p t h", t=TT)
    rs2 = narrow(16).rearrange("p (t h) -> p t h", t=TT)
    pT2 = [tmp[2], tmp[3]]
    o2 = fm(A[1])
    merged = fm(A[0])
    hid = A[0][:, 0:1024].rearrange("p (f t) -> p f t", t=T)
    f_conv = [tmp[0][:, 0:256], tmp[1][:, 0:256]]
    f_act = [tmp[2][:, 0:256], tmp[3][:, 0:256]]
    p_gate = A[1][:, :].rearrange("p (h t n) -> p h t n", h=2, t=TT)
    q3 = fm(A[0])
    kraw = A[1][:, 0:1536].rearrange("p (c t) -> p c t", t=T)
    vraw = A[1][:, 1536:2048].rearrange("p (c t) -> p c t", t=T)
    v3 = A[2][:, 0:1024].rearrange("p (b t n) -> p b t n", b=2, t=TT)
    kd = [A[i][:, :].rearrange("p (g d t) -> p g d t", g=4, d=2) for i in (3, 4)]
    kp = A[4][:, 0:1024].rearrange("p (g t) -> p g t", g=4)
    vp = A[4][:, 1024:2048].rearrange("p (g t) -> p g t", g=4)
    xb = [A[5][:, 0:960].rearrange("p (m g b) -> p m g b", m=16, g=4),
          A[5][:, 960:1920].rearrange("p (m g b) -> p m g b", m=16, g=4)]
    hid_c = [A[2][:, 1024:1084], A[2][:, 1084:1144]]
    kc = A[2][:, 1144:1264].rearrange("p (d g b) -> p d g b", d=2, g=4)
    vc = A[2][0:NB, 1264:1520]
    gate3 = narrow(96).rearrange("p (t b h) -> p t b h", t=TT, b=3)
    pc = A[6][:, 0:480].rearrange("p (t h b) -> p t h b", t=TT, h=16)
    cm, cr = (narrow(32).rearrange("p (t h) -> p t h", t=TT) for _ in range(2))
    p3 = [A[7][:, 512 * i:512 * i + 512].rearrange("p (d s) -> p d s", d=2) for i in range(4)]
    pT3 = [AB[:, 512 * i:512 * i + 384] for i in range(4)]
    pcT = AB[0:NB, 2048:2560]
    o3 = fm(A[8])
    nm3 = [narrow(2) for _ in range(4)]
    rs3 = [narrow(2) for _ in range(4)]
    rw3 = [narrow(2) for _ in range(4)]
    v4 = A[2][:, 0:256].rearrange("p (t n) -> p t n", t=TT)
    k4 = A[1][:, 0:256]
    kd4 = A[3][:, 0:1024].rearrange("p (g d t) -> p g d t", g=2, d=2)
    sk = [narrow(2) for _ in range(2)]

    skew = nc.dram_tensor("bias_rows", [P * 8 * 512], fp32, kind="Internal").ap()

    bank = [ctx.enter_context(nc.psum_tensor(f"bank{i}", [P, 512], fp32)) for i in range(8)]
    acc = [[bank[0], bank[1]], [bank[2], bank[3]]]

    products_done = sem("products_done")
    bank_copied = [sem(f"bank_copied{i}") for i in range(4)]
    slab_loaded = [sem(f"slab_loaded{i}") for i in range(NSLOT)]
    inputs_loaded = sem("inputs_loaded")
    fills_done = sem("fills_done")
    own = {e: sem(f"{e}_own") for e in ("dve", "act", "pool")}

    def filled(eng, name, i, it=0):
        eng.wait_ge(products_done, plan.done(name, i) + it * len(plan.kinds[name]))

    def work_bank(name, i):
        return bank[4 + plan.work(name, i) % 4]

    def copied(eng, name, i, it=0):
        w = plan.work(name, i)
        eng.wait_ge(bank_copied[w % 4], w // 4 + 1 + it * (plan.kinds[name].count("W") // 4))

    def frees(ins, name, i):
        return ins.then_inc(bank_copied[plan.work(name, i) % 4], 1)

    class Chain:

        def __init__(self, eng, which):
            self.eng, self.sem, self.n, self.off = eng, own[which], 0, 0

        def __call__(self, ins):
            ins.then_inc(self.sem, 1)
            self.n += 1
            self.eng.wait_ge(self.sem, self.n + self.off)

    def wide(a, dim, n):
        shape = list(a.shape)
        assert shape[dim] == 1
        shape[dim] = n
        return a.broadcast_to(shape)

    names = ("c_act_ready", "c_pad_ready", "mod_ready", "x_new", "squares_done", "mean_ready", "rstd_ready",
             "xn_ready", "conv_ready", "z_ready", "logit_ready", "exp_ready", "prob_ready", "mask_ready", "zeroed", "msq_ready",
             "sel_ready", "sel_prob_ready", "maskT_ready", "expert_staged", "rel_ready", "rows_out", "bias_in",
             "lam_exp_in", "lam_exp_out", "sp_ready", "ua_ready", "tanh_done", "decay_done", "mult_in",
             "mult_out", "scan_done", "lru_ready", "rsq_ready", "qk_ready", "relu_used",
             "att_in", "att_exp", "att_ready", "merged_ready", "conv_in", "gelu_done", "rope_ready",
             "final_row_in", "cmp_x_ready", "cmp_in", "cmp_exp", "cmp_ready", "max3_ready", "p3_ready", "sink_exp",
             "out_ready", "out_stored")
    S = {n: sem(n) for n in names}

    NORMS = ["norm0", "norm1", "g_final", "norm2", "norm3", "norm4", "ffnorm0", "nsa_norm", "ffnorm1",
             "ffnorm2", "swa_norm", "ffnorm3", "final"]
    N_INPUTS, N_FILLS = 16 * 11, 5
    dft_seq = const("dft_seq", "p (t n) -> p t n", t=TT)
    block = ctx.enter_context(nc.Block())

    @block.sync
    def _(sp):
        def k_rows(w, c0, n):
            return w[:, c0:c0 + n].rearrange("(k p) n -> p k n", p=P)

        def two_halves(slot, src, n):
            dst = ring[slot][:, 0:8 * n].rearrange("p (k n) -> p k n", k=8)
            return [(dst[:, 4 * a:4 * a + 4, :], src[:, 4 * a:4 * a + 4, :]) for a in range(2)]

        def row_block(slot, w, r0, n):
            dst = ring[slot][:, 0:n * D].rearrange("p (k n) -> p k n", k=n)
            src = w[r0:r0 + n * P, :].rearrange("(k p) n -> p k n", p=P)
            h = n // 2
            return [(dst[:, 0:h, :], src[:, 0:h, :]), (dst[:, h:n, :], src[:, h:n, :])]

        def row_block_at(slot, w, r0, n):
            dst = ring[slot][:, 0:n * D].rearrange("p (k n) -> p k n", k=n)
            src = w[bass.ds(r0, n * P), :].rearrange("(k p) n -> p k n", p=P)
            h = n // 2
            return [(dst[:, 0:h, :], src[:, 0:h, :]), (dst[:, h:n, :], src[:, h:n, :])]

        def gate_up(slot, w, f0, width):
            dst = ring[slot][:, :].rearrange("p (k n) -> p k n", k=8)
            gate = w[:, bass.ds(f0, 256)].rearrange("(k p) n -> p k n", p=P)
            up = w[:, bass.ds(f0 + width, 256)].rearrange("(k p) n -> p k n", p=P)
            return [(dst[:, :, 0:256], gate), (dst[:, :, 256:512], up)]

        def load(name, s, halves, it=0, after=None):
            n = plan.slab0[name] + s
            if n >= NSLOT:
                sp.wait_ge(products_done, (plan.slab_end[n - NSLOT] if after is None else after))
            for dst, src in halves:
                sp.dma_start(dst, src).then_inc(slab_loaded[n % NSLOT], 16)

        def slot(name, s):
            return (plan.slab0[name] + s) % NSLOT

        def dense(name, w, n_slabs, c0=0):
            for s in range(n_slabs):
                load(name, s, two_halves(slot(name, s), k_rows(w, c0 + 512 * s, 512), 512))

        def loop(name, slab):
            body = plan.slab0_body[name]
            for s in range(body):
                load(name, s, slab(s, 0))
            with sp.Fori(1, plan.times[name]) as it:
                for s in range(body):
                    n = plan.slab0[name] + body + s
                    load(name, s, slab(s, it), after=plan.slab_end[n - NSLOT] + (it - 1) * len(plan.kinds[name]))

        dense("ada", dram("w_ada"), 12)
        w_in = dram("w_in")
        dense("uf", w_in, 1)
        dense("vbc", w_in, 6, 512)
        dense("gates", w_in, 4, 512 + 3 * D)
        load("fourier_out", 0, row_block(slot("fourier_out", 0), dram("w_fourier"), 0, 4))
        dense("conv_out", dram("w_conv_out"), 2)
        dense("w_o", dram("w_o"), 2)

        w_gate_e, w_up_e, w_down_e = dram("w_gate_e"), dram("w_up_e"), dram("w_down_e")

        def expert_slab(s, e):
            sl = slot("experts", s)
            if s < 8:
                w = w_gate_e if s < 4 else w_up_e
                dst = ring[sl][:, :].rearrange("p (k n) -> p k n", k=2)
                src = w[bass.ds(e * D + (s % 4) * 256, 256), :].rearrange("(k p) n -> p k n", p=P)
                return [(dst[:, k:k + 1, :], src[:, k:k + 1, :]) for k in range(2)]
            return row_block_at(sl, w_down_e, e * DE + (s % 4) * 512, 4)

        loop("experts", expert_slab)

        w_in2 = dram("w_in_2")
        dense("lru_x", w_in2, 2, 0)
        sl = slot("lru_ri", 0)
        gate_w = [dram(n).rearrange("(b c) d -> c b d", c=P) for n in ("lru_wa_2", "lru_wx_2")]
        load("lru_ri", 0, [(ring[sl][:, i * D:(i + 1) * D].rearrange("p (b d) -> p b d", b=8), gate_w[i])
                           for i in range(2)])
        dense("lru_gate", w_in2, 2, 1024)
        dense("q", w_in2, 2, 2048)
        dense("kv", w_in2, 1, 3072)
        dense("qi", w_in2, 1, 3584)
        dense("gate_a", w_in2, 2, 4168)
        dense("lru_out", dram("w_lru_br_2"), 2)
        dense("gate_b", w_in2, 2, 5192)
        dense("attn_out", dram("w_attn_br_2"), 2)
        dense("w_out2", dram("w_out_2"), 2)

        def ffn_slab(name, w_up, w_down, width):
            def slab(s, it):
                if s < 2:
                    return gate_up(slot(name, s), w_up, it * 512 + s * 256, width)
                return row_block_at(slot(name, s), w_down, it * 512, 4)
            return slab

        loop("ffn2", ffn_slab("ffn2", dram("w_up_2"), dram("w_down_2"), F2))
        w_ple_gate, w_ple_proj = dram("w_ple_gate_2"), dram("w_ple_proj_2")
        dense("ple", w_ple_gate, 2)
        load("ple", 2, row_block(slot("ple", 2), w_ple_proj, 0, 2))

        def ffn3(n, w_gu, w_down):
            loop(f"ffn3_{n}", ffn_slab(f"ffn3_{n}", w_gu, w_down, F3))
            end = f"ffn3_{n}_end"
            load(end, 0, gate_up(slot(end, 0), w_gu, F3 - 256, F3))
            load(end, 1, row_block(slot(end, 1), w_down, F3 - 256, 2))

        gu1, dn1, gu2, dn2 = (dram(n) for n in ("ffn1_w_gu_3", "ffn1_w_down_3", "ffn2_w_gu_3", "ffn2_w_down_3"))
        ffn3(0, gu1[0:D, :], dn1[0:F3, :])
        w_nsa = dram("nsa_w_in_3")
        dense("nsa_q", w_nsa, 2)
        dense("nsa_kv0", w_nsa, 1, 1024)
        dense("nsa_kv12", w_nsa, 2, 1536)
        sl = slot("cmp_hid", 0)
        load("cmp_hid", 0, [(ring[sl][:, i * 2048:(i + 1) * 2048].rearrange("p (m h) -> p m h", m=16),
                             dram(n).rearrange("(m p) h -> p m h", p=P))
                            for i, n in enumerate(("nsa_ck_w1_3", "nsa_cv_w1_3"))])
        dense("nsa_out", dram("nsa_w_out_3"), 2)
        ffn3(1, gu2[0:D, :], dn2[0:F3, :])
        ffn3(2, gu1[D:2 * D, :], dn1[F3:2 * F3, :])
        w_swa = dram("swa_w_in_3")
        dense("swa_q", w_swa, 2)
        load("swa_kv", 0, two_halves(slot("swa_kv", 0), k_rows(w_swa, 1024, 256), 256))
        dense("swa_out", dram("swa_w_out_3"), 2)
        ffn3(3, gu2[D:2 * D, :], dn2[F3:2 * F3, :])
        sp.wait_ge(S["out_ready"], TT)
        sp.dma_start(out.rearrange("(t p) d -> p t d", p=P), xn[:, :, :]).then_inc(S["out_stored"], 16)
        sp.wait_ge(S["out_stored"], 16)

    @block.tensor
    def _(pe):
        mm = nc.tensor.matmul

        def open_bank(name, i, it=0):
            w = plan.work(name, i)
            if w >= 4:
                pe.wait_ge(bank_copied[w % 4], w // 4 + it * (plan.kinds[name].count("W") // 4))
            return bank[4 + w % 4]

        def slab(name, s, it=0):
            n = plan.slab0[name] + s
            per_pass = plan.slab0_body[name] // NSLOT * 32 if plan.times[name] > 1 else 0
            pe.wait_ge(slab_loaded[n % NSLOT], 32 * (n // NSLOT + 1) + it * per_pass)
            return ring[n % NSLOT]

        def batch(ins):
            ins.then_inc(products_done, 1)

        def all_copied(name, idx):
            for i in idx:
                copied(pe, name, i)

        def normT(k, name):
            pe.wait_ge(S["xn_ready"], TT * k)
            for g in range(4):
                b = open_bank(name, g)
                for c in range(2):
                    for t in range(TT):
                        last = nc.tensor.transpose(b[:, c * T + t * P:c * T + (t + 1) * P],
                                                   xn[:, t, (2 * g + c) * P:(2 * g + c + 1) * P], ident)
                batch(last)

        def feature_major(name, b0, s, src, n_k, n_f=4, stride=512, c0=0):
            w = slab(name, s)
            for g in range(n_f // 2):
                b = open_bank(name, b0 + g)
                for f in range(2):
                    for k in range(n_k):
                        at = k * stride + c0 + (2 * g + f) * P
                        last = mm(b[:, f * T:(f + 1) * T], w[:, at:at + P], src[:, k, :],
                                  start=(k == 0), stop=(k == n_k - 1))
                batch(last)

        def to_acc(name, s, src):
            w = slab(name, s)
            for t in range(TT):
                for k in range(DC):
                    last = mm(acc[t][s][:, :], src[:, k, t * P:(t + 1) * P], w[:, 512 * k:512 * k + 512],
                              start=(k == 0), stop=(k == DC - 1))
            batch(last)

        def clear_acc():
            for t in range(TT):
                for h in range(2):
                    mm(acc[t][h][:, :], zeros[:, :], consts[:, 0:512], start=True, stop=False, skip_group_check=True)

        pe.wait_ge(inputs_loaded, N_INPUTS)
        pe.wait_ge(fills_done, N_FILLS)
        pe.wait_ge(S["c_pad_ready"], 1)
        for m in range(12):
            w = slab("ada", m)
            b = open_bank("ada", 2 * m)
            for k in range(DC):
                j = 32 * (k % 4)
                last = mm(b[j:j + 32, :], c_pad[:, k, :], w[:, 512 * k:512 * k + 512], start=(k < 4),
                          stop=(k >= 4), tile_position=(0, j), skip_group_check=True)
            batch(last)
            copied(pe, "ada", 2 * m)
            b = open_bank("ada", 2 * m + 1)
            if m // 2 in (2, 5):
                last = mm(b[:, :], ones[:, :], mod_part[m % 2][:, :], start=True, stop=True)
            else:
                for c in range(4):
                    last = mm(b[:, c:c + 1], mod_part[m % 2][:, c * P:(c + 1) * P], ones[:, 0:1],
                              start=True, stop=True)
            batch(last)
        normT(1, "norm0")
        all_copied("norm0", range(4))
        w = slab("uf", 0)
        for t in range(TT):
            b = open_bank("uf", t)
            for k in range(DC):
                last = mm(b[:, :], hT[:, k, t * P:(t + 1) * P], w[:, 512 * k:512 * k + 512],
                          start=(k == 0), stop=(k == DC - 1))
            batch(last)
        all_copied("uf", range(2))
        for g in range(4):
            b = open_bank("dft_a", g)
            for t in range(TT):
                last = mm(b[:, :], uf[:, t, g * P:(g + 1) * P], dft_seq[:, t, :], start=(t == 0), stop=(t == 1))
            batch(last)
        all_copied("dft_a", range(4))
        for i in range(2):
            b = open_bank("dft_b", i)
            for j in range(2):
                mm(b[:, j * T:(j + 1) * T], const("dft_cos"), dft_v[:, 2 * i + j, 0:T], start=True, stop=False)
                last = mm(b[:, j * T:(j + 1) * T], const("dft_sin"), dft_v[:, 2 * i + j, T:2 * T],
                          start=False, stop=True)
            batch(last)
        for s in range(6):
            feature_major("vbc", 2 * s, s, hT, DC)
        for s in range(4):
            feature_major("gates", 2 * s, s, hT, DC)
        all_copied("dft_b", range(2))
        feature_major("fourier_out", 0, 0, yT, 4, n_f=8, stride=D)
        pe.wait_ge(S["conv_ready"], 1)
        for s in range(2):
            feature_major("conv_out", 2 * s, s, f_bc, DC)
        pe.wait_ge(S["z_ready"], 4)
        for s in range(2):
            to_acc("w_o", s, f_z)
        normT(2, "norm1")
        all_copied("norm1", range(4))
        b = open_bank("router", 0)
        for t in range(TT):
            for k in range(DC):
                last = mm(b[:, t * NE:(t + 1) * NE], hT[:, k, t * P:(t + 1) * P], w_router[:, k, :],
                          start=(k == 0), stop=(k == DC - 1))
        batch(last)
        pe.wait_ge(S["prob_ready"], 1)
        b = open_bank("probsT", 0)
        for t in range(TT):
            last = nc.tensor.transpose(b[0:NE, t * P:(t + 1) * P], prob[:, t, :], ident)
        batch(last)
        pe.wait_ge(S["mask_ready"], 1)
        b = open_bank("maskT", 0)
        for t in range(TT):
            last = nc.tensor.transpose(b[:, t * NE:(t + 1) * NE], mask[:, t * P:(t + 1) * P], ident[0:NE, 0:NE])
        batch(last)
        copied(pe, "maskT", 0)
        b = open_bank("slots", 0)
        mm(b[:, 0:NE], const("tri"), maskT[:, 0, :], start=True, stop=True)
        mm(b[:, NE:2 * NE], ones[:, :], maskT[:, 0, :], start=True, stop=False)
        batch(mm(b[:, NE:2 * NE], const("tri"), maskT[:, 1, :], start=False, stop=True))
        pe.wait_ge(S["sel_prob_ready"], TT)
        for i in range(8):
            b = open_bank("scatterT", i)
            for j in range(2):
                for t in range(TT):
                    last = nc.tensor.transpose(b[:, j * T + t * P:j * T + (t + 1) * P],
                                               sel_prob[:, t, 2 * i + j, :, :].rearrange("p g s -> p (g s)"), ident)
            batch(last)
        for c in range(DC):
            b = open_bank("gather", c)
            for t in range(TT):
                last = mm(b[:, :], xn[:, t, c * P:(c + 1) * P], sel[:, t, :, :].rearrange("p e s -> p (e s)"),
                          start=(t == 0), stop=(t == 1))
            batch(last)
        clear_acc()
        with pe.Fori(0, NE) as e:
            for part in range(2):
                b = open_bank("experts", 4 * part + 3, e)
                if part == 0:
                    pe.wait_ge(S["expert_staged"], 2 * e + 1)
                for m in range(4):
                    w = slab("experts", 4 * part + m, e)
                    for kk in range(2):
                        k = 2 * m + kk
                        for j in range(4):
                            last = mm(b[32 * j:32 * j + 32, :], xe_now[:, k, :],
                                      w[:, kk * DE + 512 * j:kk * DE + 512 * j + 512], start=(k == 0),
                                      stop=(k == DC - 1), tile_position=(0, 32 * j), skip_group_check=True)
                    batch(last)
            copied(pe, "experts", 7, e)
            b = open_bank("experts", 8, e)
            for q in range(4):
                last = nc.tensor.transpose(b[:, q * P:(q + 1) * P], e_h[:, q * P:(q + 1) * P], ident)
            batch(last)
            copied(pe, "experts", 8, e)
            b = open_bank("experts", 12, e)
            for m in range(4):
                w = slab("experts", 8 + m, e)
                for q in range(4):
                    for half in range(2):
                        j = 32 * (2 * half + q % 2)
                        last = mm(b[j:j + 32, :], e_hT[:, q * P + 32 * m:q * P + 32 * m + 32],
                                  w[:, q * D + 512 * half:q * D + 512 * half + 512], start=(m == 0 and q < 2),
                                  stop=(m == 3 and q >= 2), tile_position=(0, j), skip_group_check=True)
                batch(last)
            copied(pe, "experts", 12, e)
            pe.wait_ge(S["expert_staged"], 2 * e + 2)
            for t in range(TT):
                for half in range(2):
                    last = mm(acc[t][half][:, :], scat_now[64 * half:64 * half + 64, t * P:(t + 1) * P],
                              e_y[64 * half:64 * half + 64, :], start=False, stop=False,
                              tile_position=(64 * half, 0), skip_group_check=True)
            batch(last)

        def close_acc(name):
            for t in range(TT):
                for h in range(2):
                    last = mm(acc[t][h][:, :], zeros[:, :], consts[:, 0:512], start=False, stop=True,
                              skip_group_check=True)
            batch(last)

        close_acc("experts_end")
        normT(3, "norm2")
        all_copied("norm2", range(4))
        for s in range(2):
            feature_major("lru_x", 2 * s, s, hT, DC)
        pe.wait_ge(S["ua_ready"], 1)
        w = slab("lru_ri", 0)
        for i in range(8):
            b = open_bank("lru_ri", i)
            for j in range(2):
                n = 2 * (i % 4) + j
                at = (i // 4) * D + n * P
                last = mm(b[:, j * T:(j + 1) * T], w[:, at:at + P], l_ua[:, n, :], start=True, stop=True)
            batch(last)
        for s in range(2):
            feature_major("lru_gate", 2 * s, s, hT, DC)
        for s in range(2):
            feature_major("q", 2 * s, s, hT, DC)
        feature_major("kv", 0, 0, hT, DC, n_f=2)
        w = ring[plan.slab0["kv"] % NSLOT]
        b = open_bank("kv", 1)
        for t in range(TT):
            for k in range(DC):
                last = mm(b[:, t * T:(t + 1) * T], hT[:, k, t * P:(t + 1) * P], w[:, 512 * k + 256:512 * k + 512],
                          start=(k == 0), stop=(k == DC - 1))
        batch(last)
        feature_major("qi", 0, 0, hT, DC)
        b = open_bank("kiwi", 0)
        for d in range(2):
            for k in range(DC):
                last = mm(b[64 * d:64 * d + 64, 0:T], w_kiwi[:, k, 0:64], hT[:, k, :], start=(k == 0),
                          stop=(k == DC - 1), tile_position=(0, 64 * d), skip_group_check=True)
        batch(last)
        b = open_bank("kiwi", 1)
        for t in range(TT):
            for k in range(DC):
                last = mm(b[:, t * 8:(t + 1) * 8], hT[:, k, t * P:(t + 1) * P], w_kiwi[:, k, 64:72],
                          start=(k == 0), stop=(k == DC - 1))
        batch(last)
        all_copied("q", range(4))
        copied(pe, "kv", 0)
        for i in range(5):
            b = open_bank("qk_ms", i)
            src = sq2[:, 2 * i:2 * i + 2, :].rearrange("p c t -> p (c t)") if i < 4 else sqk[:, :]
            batch(mm(b[:, :], ones_mean[:, :], src, start=True, stop=True))
        pe.wait_ge(S["rel_ready"], 1)
        for h in range(8):
            b = open_bank("bias", h)
            batch(mm(b[:, :], rel_rep[:, h, :], const("buckets")[0:32, :], start=True, stop=True))
        all_copied("qi", range(2))
        all_copied("kiwi", range(1))
        for t in range(TT):
            for m in range(4):
                b = open_bank("score", 4 * t + m)
                for d in range(2):
                    last = mm(b[:, d * T:(d + 1) * T], qi[:, m, t * P:(t + 1) * P], ki[:, d, :],
                              start=True, stop=True)
                batch(last)
        for s in range(2):
            feature_major("gate_a", 2 * s, s, hT, DC)
        pe.wait_ge(S["lru_ready"], 1)
        for s in range(2):
            feature_major("lru_out", 2 * s, s, l_ua, DC)
        for s in range(2):
            feature_major("gate_b", 2 * s, s, hT, DC)
        pe.wait_ge(S["qk_ready"], 5)
        for t in range(TT):
            for m in range(4):
                b = open_bank("logits2", 4 * t + m)
                for d in range(2):
                    h = 2 * m + d
                    last = mm(b[:, d * T:(d + 1) * T], q2[:, h, t * P:(t + 1) * P], k2[:, h // 4, :],
                              start=True, stop=True)
                batch(last)
        pe.wait_ge(S["att_ready"], TT)

        def causal_blocks(b, p_of_t):
            nc.tensor.transpose(b[:, 0:P], p_of_t(0)[:, 0:P], ident)
            nc.tensor.transpose(b[:, P:2 * P], p_of_t(1)[:, 0:P], ident)
            return nc.tensor.transpose(b[:, 2 * P:3 * P], p_of_t(1)[:, P:2 * P], ident)

        for m in range(4):
            for d in range(2):
                b = open_bank("pv2", 3 * m + d)
                batch(causal_blocks(b, lambda t: att[t][:, 2 * m + d, :]))
            b = open_bank("pv2", 3 * m + 2)
            g = m // 2
            for d in range(2):
                copied(pe, "pv2", 3 * m + d)
                mm(b[:, d * T:(d + 1) * T], v2[:, 0, g * P:(g + 1) * P], pT2[d][:, 0:T], start=True, stop=False)
                last = mm(b[:, d * T + P:(d + 1) * T], v2[:, 1, g * P:(g + 1) * P], pT2[d][:, T:T + P],
                          start=False, stop=True)
            batch(last)
        all_copied("pv2", (2, 5, 8, 11))
        for s in range(2):
            feature_major("attn_out", 2 * s, s, o2, DC)
        pe.wait_ge(S["merged_ready"], 4)
        for s in range(2):
            to_acc("w_out2", s, merged)

        def gate_up_tile(name, i, w, j, it=0):
            b = open_bank(name, i, it)
            for part in range(2):
                for k in range(DC):
                    at = 512 * k + 256 * part + P * j
                    last = mm(b[:, part * T:(part + 1) * T], w[:, at:at + P], hT[:, k, :],
                              start=(k == 0), stop=(k == DC - 1))
            batch(last)

        def down(name, n_f, w, it, stop):
            for f in range(n_f):
                copied(pe, name, f, it)
                for t in range(TT):
                    for h in range(2):
                        last = mm(acc[t][h][:, :], hid[:, f, t * P:(t + 1) * P],
                                  w[:, f * D + 512 * h:f * D + 512 * h + 512], start=False,
                                  stop=(stop and f == n_f - 1), skip_group_check=True)
            batch(last)

        def ffn(name):
            clear_acc()
            with pe.Fori(0, plan.times[name]) as it:
                for s in range(2):
                    w = slab(name, s, it)
                    for j in range(2):
                        gate_up_tile(name, 2 * s + j, w, j, it)
                down(name, 4, slab(name, 2, it), it, False)

        normT(4, "norm3")
        all_copied("norm3", range(4))
        ffn("ffn2")
        close_acc("ffn2_end")
        normT(5, "norm4")
        all_copied("norm4", range(4))
        for h in range(2):
            w = slab("ple", h)
            for t in range(TT):
                b = open_bank("ple", 2 * h + t)
                for k in range(DC):
                    last = mm(b[:, :], hT[:, k, t * P:(t + 1) * P], w[:, 512 * k:512 * k + 512],
                              start=(k == 0), stop=(k == DC - 1))
                batch(last)
        w = slab("ple", 2)
        for h in range(2):
            for t in range(TT):
                b = open_bank("ple", 4 + 2 * h + t)
                for k in range(2):
                    last = mm(b[:, :], pT_in[:, k, t * P:(t + 1) * P], w[:, k * D + 512 * h:k * D + 512 * h + 512],
                              start=(k == 0), stop=(k == 1))
                batch(last)
        def ffn3(n, k):
            normT(k, f"ffnorm{n}")
            all_copied(f"ffnorm{n}", range(4))
            ffn(f"ffn3_{n}")
            end = f"ffn3_{n}_end"
            w = slab(end, 0)
            for j in range(2):
                gate_up_tile(end, j, w, j)
            down(end, 2, slab(end, 1), 0, True)

        def rope(name, i, src):
            b = open_bank(name, i)
            batch(mm(b[:, 0:src.shape[1]], const("rope_rot"), src, start=True, stop=True))

        def pairs(a, i, n=2):
            return a[:, 2 * i:2 * i + n, :].rearrange("p c t -> p (c t)")

        ffn3(0, 6)
        normT(7, "nsa_norm")
        all_copied("nsa_norm", range(4))
        for s in range(2):
            feature_major("nsa_q", 2 * s, s, hT, DC)
        feature_major("nsa_kv0", 0, 0, hT, DC)
        for s in range(2):
            feature_major("nsa_kv12", 2 * s, s, hT, DC, n_f=2)
            w = ring[(plan.slab0["nsa_kv12"] + s) % NSLOT]
            b = open_bank("nsa_kv12", 2 * s + 1)
            for t in range(TT):
                for k in range(DC):
                    last = mm(b[:, t * T:(t + 1) * T], hT[:, k, t * P:(t + 1) * P],
                              w[:, 512 * k + 256:512 * k + 512], start=(k == 0), stop=(k == DC - 1))
            batch(last)
        b = open_bank("nsa_g", 0)
        for t in range(TT):
            for k in range(DC):
                last = mm(b[:, t * 48:(t + 1) * 48], hT[:, k, t * P:(t + 1) * P], w_nsa_gate[:, k, :],
                          start=(k == 0), stop=(k == DC - 1))
        batch(last)
        all_copied("nsa_q", range(4))
        all_copied("nsa_kv0", range(2))
        all_copied("nsa_kv12", range(4))
        for i in range(7):
            rope("nsa_rope", i, pairs(q3, i) if i < 4 else pairs(kraw, i - 4))
        pe.wait_ge(S["cmp_x_ready"], 1)
        w = slab("cmp_hid", 0)
        for i in range(2):
            b = open_bank("cmp_hid", i)
            for m in range(16):
                at = i * 2048 + m * P
                last = mm(b[:, 0:60], w[:, at:at + P], xb[i][:, m, :, :].rearrange("p g b -> p (g b)"),
                          start=(m == 0), stop=(m == 15))
            batch(last)
        all_copied("cmp_hid", range(2))
        b = open_bank("cmp_kv", 0)
        for d in range(2):
            last = mm(b[64 * d:64 * d + 64, 0:60], ck_w2[:, :], hid_c[0], start=True, stop=True,
                      tile_position=(0, 64 * d), skip_group_check=True)
        batch(last)
        b = open_bank("cmp_kv", 1)
        for g in range(4):
            last = mm(b[0:NB, g * 64:(g + 1) * 64], hid_c[1][:, g * NB:(g + 1) * NB], cv_w2[:, :],
                      start=True, stop=True)
        batch(last)
        all_copied("cmp_kv", range(2))
        pe.wait_ge(S["rope_ready"], 7)
        for t in range(TT):
            b = open_bank("cmp_s", t)
            for h in range(16):
                d, m = h % 2, h // 2
                last = mm(b[:, h * NB:(h + 1) * NB], q3[:, m, t * P:(t + 1) * P], kc[:, d, m // 2, :],
                          start=True, stop=True)
            batch(last)

        def masked_scores(name, i, m, t, keys, neg):
            b = open_bank(name, i)
            for d in range(2):
                mm(b[:, d * T:(d + 1) * T], q3[:, m, t * P:(t + 1) * P], keys[:, d, :], start=True, stop=False)
                last = mm(b[:, d * T:(d + 1) * T], ident, neg[:, t, :], start=False, stop=True)
            batch(last)

        pe.wait_ge(S["cmp_ready"], 1)
        for m in range(8):
            g = m // 2
            n = 10 * m
            for br in range(2):
                for t in range(TT):
                    masked_scores("nsa_heads", n + 2 * br + t, m, t, kd[br][:, g, :, :], causal)
            for br in range(2):
                pe.wait_ge(S["p3_ready"], 4 * m + 2 * br + 2)
                for d in range(2):
                    b = open_bank("nsa_heads", n + 4 + 2 * br + d)
                    batch(causal_blocks(b, lambda t: p3[2 * br + t][:, d, :]))
            b = open_bank("nsa_heads", n + 8)
            for d in range(2):
                for t in range(TT):
                    last = nc.tensor.transpose(b[0:NB, d * T + t * P:d * T + (t + 1) * P], pc[:, t, 2 * m + d, :],
                                               ident)
            batch(last)
            b = open_bank("nsa_heads", n + 9)
            for i in range(5):
                copied(pe, "nsa_heads", n + 4 + i)
            for d in range(2):
                o = b[64 * d:64 * d + 64, 0:T]
                o_late = b[64 * d:64 * d + 64, P:T]
                k = dict(tile_position=(0, 64 * d), skip_group_check=True)
                mm(o, vc[:, g * 64:(g + 1) * 64], pcT[:, d * T:(d + 1) * T], start=True, stop=False, **k)
                for br in range(2):
                    pt = pT3[2 * br + d]
                    mm(o, v3[:, br, 0, g * 64:(g + 1) * 64], pt[:, 0:T], start=False, stop=False, **k)
                    last = mm(o_late, v3[:, br, 1, g * 64:(g + 1) * 64], pt[:, T:T + P], start=False,
                              stop=(br == 1), **k)
            batch(last)
        for m in range(8):
            copied(pe, "nsa_heads", 10 * m + 9)
        for s in range(2):
            to_acc("nsa_out", s, o3)
        ffn3(1, 8)
        ffn3(2, 9)
        normT(10, "swa_norm")
        all_copied("swa_norm", range(4))
        for s in range(2):
            feature_major("swa_q", 2 * s, s, hT, DC)
        w = slab("swa_kv", 0)
        b = open_bank("swa_kv", 0)
        for k in range(DC):
            mm(b[:, 0:T], w[:, 256 * k:256 * k + P], hT[:, k, :], start=(k == 0), stop=(k == DC - 1))
        for t in range(TT):
            for k in range(DC):
                last = mm(b[:, T + t * P:T + (t + 1) * P], hT[:, k, t * P:(t + 1) * P],
                          w[:, 256 * k + P:256 * k + 2 * P], start=(k == 0), stop=(k == DC - 1))
        batch(last)
        all_copied("swa_q", range(4))
        copied(pe, "swa_kv", 0)
        for i in range(5):
            rope("swa_rope", i, pairs(q3, i) if i < 4 else k4)
        pe.wait_ge(S["rope_ready"], 12)
        for m in range(8):
            n, g = 5 * m, m // 4
            for t in range(TT):
                masked_scores("swa_heads", n + t, m, t, kd4[:, g, :, :], window)
            pe.wait_ge(S["p3_ready"], 32 + 2 * m + 2)
            for d in range(2):
                b = open_bank("swa_heads", n + 2 + d)
                batch(causal_blocks(b, lambda t: p3[2 * (m % 2) + t][:, d, :]))
            b = open_bank("swa_heads", n + 4)
            for d in range(2):
                copied(pe, "swa_heads", n + 2 + d)
                k = dict(tile_position=(0, 64 * d), skip_group_check=True)
                pt = pT3[d]
                mm(b[64 * d:64 * d + 64, 0:T], v4[:, 0, g * 64:(g + 1) * 64], pt[:, 0:T], start=True, stop=False, **k)
                last = mm(b[64 * d:64 * d + 64, P:T], v4[:, 1, g * 64:(g + 1) * 64], pt[:, T:T + P],
                          start=False, stop=True, **k)
            batch(last)
        for m in range(8):
            copied(pe, "swa_heads", 5 * m + 4)
        for s in range(2):
            to_acc("swa_out", s, o3)
        ffn3(3, 11)

    @block.scalar
    def _(act):
        run = nc.scalar.activation
        link = Chain(act, "act")

        def copy_out(name, i, dst, n=512, scale=1.0, rows_=P, it=0):
            filled(act, name, i, it)
            frees(run(dst, work_bank(name, i)[0:rows_, 0:n], ACT.Copy, scale=scale), name, i)

        def squares(k):
            if k:
                act.wait_ge(S["x_new"], k)
            for t in range(TT):
                if k or t:
                    act.wait_ge(S["squares_done"], TT * k + t)
                run(junk, x[:, t, :], ACT.Square, accum_out=ss[:, t:t + 1]).then_inc(S["squares_done"], 1)

        def norm_out(name, gain, shift=None):
            for g in range(4):
                filled(act, name, g)
                for c in range(2):
                    k = 2 * g + c
                    args = {} if shift is None else {"bias": shift[:, k:k + 1]}
                    ins = run(hT[:, k, :], work_bank(name, g)[:, c * T:(c + 1) * T], ACT.Identity,
                              scale=gain[:, k:k + 1], **args)
                frees(ins, name, g)

        def two(name, i, fn):
            filled(act, name, i)
            for f in range(2):
                ins = fn(f, work_bank(name, i)[:, f * T:(f + 1) * T])
            frees(ins, name, i)

        act.wait_ge(inputs_loaded, N_INPUTS)
        act.wait_ge(fills_done, N_FILLS)
        squares(0)
        run(c_act, col("c", 0, 8), ACT.Silu).then_inc(S["c_act_ready"], 1)
        for m in range(12):
            copy_out("ada", 2 * m, mod_part[m % 2][:, :])
        act.wait_ge(S["mod_ready"], 2)
        norm_out("norm0", g_mix, modc[:, 0:8])
        for t in range(TT):
            copy_out("uf", t, uf[:, t, :])
        for g in range(4):
            copy_out("dft_a", g, dft_v[:, g, :])
        for i in range(2):
            copy_out("dft_b", i, yT[:, 2 * i:2 * i + 2, :].rearrange("p g t -> p (g t)"))
        for i in range(8):
            dst = (f_v, f_b)[i // 4][:, 2 * (i % 4):2 * (i % 4) + 2, :]
            copy_out("vbc", i, dst.rearrange("p g t -> p (g t)"))
        for i in range(8):
            dst = (f_ga, f_gb)[i // 4]
            two("gates", i, lambda f, b: run(dst[:, 2 * (i % 4) + f, :], b, ACT.Sigmoid,
                                             bias=col("b_gate", 2 * i + f)))
        squares(1)
        norm_out("norm1", g_moe, modc[:, 24:32])
        act.wait_ge(S["logit_ready"], 1)
        run(logit[:, :, :], logit[:, :, :], ACT.Exp).then_inc(S["exp_ready"], 1)
        for i in range(8):
            copy_out("scatterT", i, scat[:, 2 * i:2 * i + 2, :].rearrange("p e t -> p (e t)"))
        for c in range(DC):
            filled(act, "gather", c)
            frees(run(xeT[:, c, :], work_bank("gather", c)[:, :], ACT.Identity, scale=g_moe[:, c:c + 1],
                      bias=modc[:, 24 + c:25 + c]), "gather", c)
        with act.Fori(0, NE) as e:
            filled(act, "experts", 3, e)
            frees(run(e_act, work_bank("experts", 3)[:, :], ACT.Silu), "experts", 3)
            copy_out("experts", 8, e_hT, it=e)
            copy_out("experts", 12, e_y, it=e)
        squares(2)
        squares(3)
        norm_out("norm2", col("mix_norm_2", 0, 8))
        act.wait_ge(S["lam_exp_in"], 1)
        run(sp_a, sp_a, ACT.Exp).then_inc(S["lam_exp_out"], 1)
        for i in range(4):
            copy_out("lru_x", i, l_t[:, 2 * i:2 * i + 2, :].rearrange("p g t -> p (g t)"))
        for i in range(8):
            dst, bias = ((l_a, "lru_ba_2"), (l_i, "lru_bx_2"))[i // 4]
            two("lru_ri", i, lambda f, b: run(dst[:, 2 * (i % 4) + f, :], b, ACT.Sigmoid,
                                              bias=col(bias, 2 * (i % 4) + f)))
        for i in range(4):
            copied(act, "lru_ri", i)
        act.wait_ge(S["sp_ready"], 1)
        for c in range(DC):
            ins = run(l_t[:, c, :], l_a[:, c, :], ACT.Tanh, scale=sp8[:, c:c + 1])
        ins.then_inc(S["tanh_done"], 1)
        for c in range(DC):
            ins = run(l_a[:, c, :], l_a[:, c, :], ACT.Exp, scale=nsp8[:, c:c + 1])
        ins.then_inc(S["decay_done"], 1)
        for i in range(4):
            copy = l_g[:, 2 * i:2 * i + 2, :].rearrange("p g t -> p (g t)")
            filled(act, "lru_gate", i)
            frees(run(copy, work_bank("lru_gate", i)[:, :], ACT.Gelu_apprx_tanh), "lru_gate", i)
        act.wait_ge(S["mult_in"], 1)
        run(l_t[:, :, :], l_t[:, :, :], ACT.Sqrt, scale=2.0).then_inc(S["mult_out"], 1)
        for i in range(4):
            filled(act, "q", i)
            run(q2[:, 2 * i:2 * i + 2, :].rearrange("p g t -> p (g t)"), work_bank("q", i)[:, :], ACT.Copy)
            frees(run(sq2[:, 2 * i:2 * i + 2, :].rearrange("p g t -> p (g t)"), work_bank("q", i)[:, :],
                      ACT.Square), "q", i)
        filled(act, "kv", 0)
        run(k2[:, :, :].rearrange("p g t -> p (g t)"), work_bank("kv", 0)[:, :], ACT.Copy)
        frees(run(sqk[:, :], work_bank("kv", 0)[:, :], ACT.Square), "kv", 0)
        copy_out("kv", 1, v2[:, :, :].rearrange("p t n -> p (t n)"))
        for i in range(2):
            copy_out("qi", i, qi[:, 2 * i:2 * i + 2, :].rearrange("p g t -> p (g t)"))
        filled(act, "kiwi", 0)
        act.wait_ge(S["zeroed"], 1)
        for d in range(2):
            half = slice(64 * d, 64 * d + 64)
            ins = run(ki[half, d, :], work_bank("kiwi", 0)[half, 0:T], ACT.Copy)
        frees(ins, "kiwi", 0)
        copy_out("kiwi", 1, wi[:, :, :].rearrange("p t h -> p (t h)"), n=16, scale=8 ** -0.5)
        for i in range(5):
            act.wait_ge(S["msq_ready"], i + 1)
            run(msq[i % 2][:, :], msq[i % 2][:, :], ACT.Sqrt).then_inc(S["rsq_ready"], 1)
        for h in range(8):
            copy_out("bias", h, bias_row[:, h, :])
        for i in range(8):
            filled(act, "score", i)
            if i >= 2:
                act.wait_ge(S["relu_used"], i - 1)
            else:
                filled(act, "qk_ms", 3)
            frees(run(relu_s[i % 2], work_bank("score", i)[:, :], ACT.Relu, scale=64 ** -0.5), "score", i)
        act.wait_ge(S["scan_done"], 1)
        for i in range(4):
            filled(act, "gate_a", i)
            frees(run(l_a[:, 2 * i:2 * i + 2, :].rearrange("p g t -> p (g t)"), work_bank("gate_a", i)[:, :],
                      ACT.Sigmoid), "gate_a", i)
        for i in range(4):
            filled(act, "gate_b", i)
            frees(run(l_i[:, 2 * i:2 * i + 2, :].rearrange("p g t -> p (g t)"), work_bank("gate_b", i)[:, :],
                      ACT.Sigmoid), "gate_b", i)
        for t in range(TT):
            act.wait_ge(S["att_in"], t + 1)
            for h in range(8):
                ins = run(att[t][:, h, :], att[t][:, h, :], ACT.Exp, bias=nm2[:, t, h:h + 1],
                          accum_out=rs2[:, t, h:h + 1])
            ins.then_inc(S["att_exp"], 1)
        for m in range(4):
            for d in range(2):
                copy_out("pv2", 3 * m + d, pT2[d][:, 0:384], n=384)
            copy_out("pv2", 3 * m + 2, o2[:, 2 * m:2 * m + 2, :].rearrange("p g t -> p (g t)"))
        squares(4)
        norm_out("norm3", col("ffn_norm_2", 0, 8))
        with act.Fori(0, plan.times["ffn2"]) as it:
            for b in range(4):
                act.wait_ge(S["conv_in"], b + 1 + 4 * it)
                run(f_act[b % 2], f_conv[b % 2], ACT.Gelu_apprx_tanh).then_inc(S["gelu_done"], 1)
        squares(5)
        norm_out("norm4", col("ple_norm_2", 0, 8))
        for i in range(4):
            filled(act, "ple", i)
            frees(run(p_gate[:, i // 2, i % 2, :], work_bank("ple", i)[:, :], ACT.Sigmoid), "ple", i)

        def ffn3(n, k):
            squares(k)
            norm_out(f"ffnorm{n}", col("ffn1_norm_3" if n % 2 == 0 else "ffn2_norm_3", 8 * (n // 2), 8))
            name = f"ffn3_{n}"

            def gates(name, n_b, it, before, before_it):
                for b in range(n_b):
                    filled(act, name, b, it)
                    if b < 2:
                        copied(act, before, b + 2, before_it)
                    else:
                        copied(act, name, b - 2, it)
                    run(f_act[b % 2], work_bank(name, b)[:, 0:T], ACT.Silu).then_inc(S["gelu_done"], 1)

            with act.Fori(0, plan.times[name]) as it:
                gates(name, 4, it, name, it - 1)
            gates(name + "_end", 2, 0, name, plan.times[name] - 1)

        ffn3(0, 6)
        squares(7)
        norm_out("nsa_norm", col("mix_norm_3", 0, 8))
        for i in range(4):
            copy_out("nsa_q", i, q3[:, 2 * i:2 * i + 2, :].rearrange("p g t -> p (g t)"))
        copy_out("nsa_kv0", 0, kraw[:, 0:2, :].rearrange("p g t -> p (g t)"))
        copy_out("nsa_kv0", 1, vraw[:, :, :].rearrange("p g t -> p (g t)"))
        for b in range(2):
            copy_out("nsa_kv12", 2 * b, kraw[:, 2 + 2 * b:4 + 2 * b, :].rearrange("p g t -> p (g t)"))
            copy_out("nsa_kv12", 2 * b + 1, v3[:, b, :, :].rearrange("p t n -> p (t n)"))
        filled(act, "nsa_g", 0)
        frees(run(gate3[:, :, :, :].rearrange("p t b h -> p (t b h)"), work_bank("nsa_g", 0)[:, 0:96], ACT.Sigmoid),
              "nsa_g", 0)
        for i in range(2):
            filled(act, "cmp_hid", i)
            frees(run(hid_c[i], work_bank("cmp_hid", i)[:, 0:60], ACT.Gelu_apprx_tanh), "cmp_hid", i)
        filled(act, "cmp_kv", 0)
        act.wait_ge(S["zeroed"], 2)
        for d in range(2):
            half = slice(64 * d, 64 * d + 64)
            ins = run(kc[half, d, :, :].rearrange("p g b -> p (g b)"), work_bank("cmp_kv", 0)[half, 0:60], ACT.Copy)
        frees(ins, "cmp_kv", 0)
        copy_out("cmp_kv", 1, vc, n=T, rows_=NB)
        act.wait_ge(S["cmp_in"], 1)
        run(pc[:, :, :, :], pc[:, :, :, :], ACT.Exp).then_inc(S["cmp_exp"], 1)

        def exps(name, i, slot, n):
            act.wait_ge(S["max3_ready"], n)
            for d in range(2):
                ins = run(p3[slot][:, d, :], work_bank(name, i)[:, d * T:(d + 1) * T], ACT.Exp,
                          scale=64 ** -0.5, bias=nm3[slot][:, d:d + 1], accum_out=rs3[slot][:, d:d + 1])
            frees(ins, name, i)

        for m in range(8):
            n = 10 * m
            for s in range(4):
                exps("nsa_heads", n + s, s, 4 * m + s + 1)
            for s in range(4):
                copy_out("nsa_heads", n + 4 + s, pT3[s][:, :], n=384)
            copy_out("nsa_heads", n + 8, pcT, rows_=NB)
            copy_out("nsa_heads", n + 9, o3[:, m, :], n=T)
        ffn3(1, 8)
        ffn3(2, 9)
        squares(10)
        norm_out("swa_norm", col("mix_norm_3", 8, 8))
        for i in range(4):
            copy_out("swa_q", i, q3[:, 2 * i:2 * i + 2, :].rearrange("p g t -> p (g t)"))
        filled(act, "swa_kv", 0)
        run(k4, work_bank("swa_kv", 0)[:, 0:T], ACT.Copy)
        frees(run(v4[:, :, :].rearrange("p t n -> p (t n)"), work_bank("swa_kv", 0)[:, T:2 * T], ACT.Copy),
              "swa_kv", 0)
        for m in range(8):
            for t in range(TT):
                slot = 2 * (m % 2) + t
                n = 32 + 2 * m + t + 1
                act.wait_ge(S["max3_ready"], n)
                run(sk[t], sk[t], ACT.Exp).then_inc(S["sink_exp"], 1)
                exps("swa_heads", 5 * m + t, slot, n)
            for d in range(2):
                copy_out("swa_heads", 5 * m + 2 + d, pT3[d][:, :], n=384)
            copy_out("swa_heads", 5 * m + 4, o3[:, m, :], n=T)
        ffn3(3, 11)
        squares(12)

    @block.gpsimd
    def _(pool):
        loads = [(consts[:, :], dram("consts")), (cols[:, :], dram("cols")),
                 (x[:, :, :], dram("x").rearrange("(t p) d -> p t d", p=P)),
                 (rows[:, :], wide(dram("rows"), 0, P)),
                 (w_router[:, :, :], dram("w_router").rearrange("(k p) n -> p k n", p=P)),
                 (w_kiwi[:, :, :], dram("w_in_2")[:, 4096:4168].rearrange("(k p) n -> p k n", p=P)),
                 (w_nsa_gate[:, :, :], dram("nsa_w_in_3")[:, 2560:2608].rearrange("(k p) n -> p k n", p=P)),
                 (ck_w2[:, :], dram("nsa_ck_w2_3")), (cv_w2[:, :], dram("nsa_cv_w2_3")),
                 (pT_in[:, :, :], dram("pT").rearrange("(k p) t -> p k t", p=P)),
                 (rel_in[:, :], dram("rel_bias_2"))]
        assert 16 * len(loads) == N_INPUTS
        for dst, src in loads:
            pool.dma_start(dst, src).then_inc(inputs_loaded, 16)
        fills = [(ones[:, :], 1.0), (ones_mean[:, :], 1.0 / P), (zeros[:, :], 0.0), (neg_half[:, :], -0.5),
                 (c_pad[:, :, :], 0.0)]
        assert len(fills) == N_FILLS
        for dst, v in fills:
            nc.gpsimd.memset(dst, v).then_inc(fills_done, 1)
        pool.wait_ge(fills_done, N_FILLS)

        def rsqrt(k):
            pool.wait_ge(S["mean_ready"], k + 1)
            nc.gpsimd.tensor_tensor(out=rstd, in0=ms, in1=neg_half[:, 0:TT], op=ALU.pow).then_inc(S["rstd_ready"], 1)

        rsqrt(0)
        rsqrt(1)
        for c in range(DC):
            copied(pool, "gather", c)
        for i in range(8):
            copied(pool, "scatterT", i)
        with pool.Fori(0, NE) as e:
            body = len(plan.kinds["experts"])
            pool.wait_ge(products_done, plan.done("experts", 7) - body + e * body)
            nc.gpsimd.tensor_copy(xe_now[:, :, :], xeT[:, :, bass.ds(e * CAP, CAP)]).then_inc(S["expert_staged"], 1)
            pool.wait_ge(products_done, plan.batch0["experts"] + e * body)
            nc.gpsimd.tensor_copy(scat_now, AC[:, bass.ds(e * T, T)]).then_inc(S["expert_staged"], 1)
        rsqrt(2)
        rsqrt(3)
        for h in range(8):
            copied(pool, "bias", h)
        pool.dma_start(skew.rearrange("(p n) -> p n", p=P), bias_row[:, :, :].rearrange("p h j -> p (h j)"))\
            .then_inc(S["rows_out"], 16)
        pool.wait_ge(S["rows_out"], 16)
        for t in range(TT):
            src = bass.AP(tensor=skew.tensor, offset=T - 1 - P * t, ap=[[8 * 512 - 1, P], [512, 8], [1, T]])
            pool.dma_start(bias2[:, t, :, :], src).then_inc(S["bias_in"], 16)
        pool.wait_ge(S["x_new"], 1)
        pool.dma_start(row("gate_m"), wide(dram("final_norm"), 0, P)).then_inc(S["final_row_in"], 16)
        for k in range(4, len(NORMS)):
            rsqrt(k)

    @block.vector
    def _(dve):
        v = nc.vector
        link = Chain(dve, "dve")

        def mean(k):
            dve.wait_ge(S["squares_done"], TT * (k + 1))
            v.tensor_scalar(ms, ss, 1.0 / D, EPS, ALU.mult, ALU.add).then_inc(S["mean_ready"], 1)
            dve.wait_ge(S["rstd_ready"], k + 1)

        def normalise(k, n_T):
            mean(k)
            for t in range(TT):
                v.tensor_scalar(xn[:, t, :], x[:, t, :], rstd[:, t:t + 1], None, ALU.mult)\
                    .then_inc(S["xn_ready"], 1)

        def x_updated(ins):
            ins.then_inc(S["x_new"], 1)

        dve.wait_ge(inputs_loaded, N_INPUTS)
        dve.wait_ge(fills_done, N_FILLS)
        dve.wait_ge(S["c_act_ready"], 1)
        v.tensor_copy(c_pad[:, :, 0:1], c_act[:, :].rearrange("p (k a) -> p k a", a=1)).then_inc(S["c_pad_ready"], 1)
        normalise(0, 1)
        for m in range(12):
            i = 2 * m + 1
            filled(dve, "ada", i)
            b = work_bank("ada", i)
            if m // 2 in (2, 5):
                dst = row("gate_m" if m < 6 else "gate_f")[:, (m % 2) * 512:(m % 2) * 512 + 512]
                frees(v.tensor_tensor(dst, b[:, :], dst, ALU.add), "ada", i)
            else:
                frees(v.tensor_tensor(modc[:, 4 * m:4 * m + 4], b[:, 0:4], col("b_ada", 4 * m, 4), ALU.add), "ada", i)
        for m in range(12):
            copied(dve, "ada", 2 * m + 1)
        for dst, scale_at, g in ((g_mix, 8, "g_norm_mix"), (g_moe, 32, "g_norm_moe")):
            v.scalar_tensor_tensor(dst, modc[:, scale_at:scale_at + 8], 1.0, col(g, 0, 8), ALU.add, ALU.mult)\
                .then_inc(S["mod_ready"], 1)
        for i in range(4):
            filled(dve, "vbc", 8 + i)
            copied(dve, "vbc", i)
            frees(v.tensor_tensor(f_cv[:, 2 * i:2 * i + 2, :].rearrange("p c t -> p (c t)"),
                                  work_bank("vbc", 8 + i)[:, :],
                                  f_v[:, 2 * i:2 * i + 2, :].rearrange("p c t -> p (c t)"), ALU.mult), "vbc", 8 + i)
        for i in range(4):
            copied(dve, "vbc", 8 + i)
            copied(dve, "vbc", 4 + i)
        link(v.tensor_tensor(f_bc[:, :, :], f_cv[:, :, :],
                             wide(col("w_conv", DC, DC).rearrange("p (c a) -> p c a", a=1), 2, T), ALU.mult))
        for c in range(DC):
            ins = v.scalar_tensor_tensor(f_bc[:, c, 1:T], f_cv[:, c, 0:T - 1], col("w_conv", c), f_bc[:, c, 1:T],
                                         ALU.mult, ALU.add)
        link(ins)
        for c in range(DC):
            ins = v.scalar_tensor_tensor(f_bc[:, c, 0:T - 1], f_cv[:, c, 1:T], col("w_conv", 2 * DC + c),
                                         f_bc[:, c, 0:T - 1], ALU.mult, ALU.add)
        link(ins)
        v.tensor_tensor(f_bc[:, :, :], f_bc[:, :, :], f_b[:, :, :], ALU.mult).then_inc(S["conv_ready"], 1)
        for i in range(8):
            copied(dve, "gates", i)
        for i in range(4):
            filled(dve, "fourier_out", i)
            two = slice(2 * i, 2 * i + 2)
            frees(v.tensor_tensor(f_z[:, two, :].rearrange("p c t -> p (c t)"), work_bank("fourier_out", i)[:, :],
                                  f_ga[:, two, :].rearrange("p c t -> p (c t)"), ALU.mult), "fourier_out", i)
        for i in range(4):
            filled(dve, "conv_out", i)
            if i >= 2:
                dve.wait_ge(S["z_ready"], i - 1)
            two = slice(2 * i, 2 * i + 2)
            frees(v.tensor_tensor(tmp[i % 2][:, :], work_bank("conv_out", i)[:, :],
                                  f_gb[:, two, :].rearrange("p c t -> p (c t)"), ALU.mult), "conv_out", i)
            copied(dve, "conv_out", i)
            copied(dve, "fourier_out", i)
            z = f_z[:, two, :].rearrange("p c t -> p (c t)")
            v.tensor_tensor(z, z, tmp[i % 2][:, :], ALU.add).then_inc(S["z_ready"], 1)

        def add_acc(name, gate=None, scale=1.0, batches=(0, 1)):
            for h in range(2):
                filled(dve, name, batches[h])
                for t in range(TT):
                    xs = x[:, t, 512 * h:512 * h + 512]
                    if gate is not None:
                        link(v.tensor_tensor(tmp[0][:, :], acc[t][h][:, :], gate[:, 512 * h:512 * h + 512], ALU.mult))
                        ins = v.tensor_tensor(xs, xs, tmp[0][:, :], ALU.add)
                    else:
                        ins = v.scalar_tensor_tensor(xs, acc[t][h][:, :], scale, xs, ALU.mult, ALU.add)
                    if (h, t) == (1, 1):
                        x_updated(ins)
                    else:
                        link(ins)

        add_acc("w_o", gate=row("gate_m"))
        dve.wait_ge(S["x_new"], 1)
        normalise(1, 2)
        filled(dve, "router", 0)
        b = work_bank("router", 0)
        for t in range(TT):
            ins = v.tensor_tensor(logit[:, t, :], b[:, t * NE:(t + 1) * NE], row("b_router"), ALU.add)
        frees(ins, "router", 0)
        copied(dve, "router", 0)
        link(v.reduce_max(rmax, logit[:, :, :], AX.X))
        v.tensor_tensor(logit[:, :, :], logit[:, :, :], wide(rmax[:, :].rearrange("p (t a) -> p t a", a=1), 2, NE),
                        ALU.subtract).then_inc(S["logit_ready"], 1)
        dve.wait_ge(S["exp_ready"], 1)
        link(v.reduce_sum(rsum, logit[:, :, :], AX.X))
        link(v.reciprocal(rsum, rsum))
        v.tensor_tensor(prob[:, :, :], logit[:, :, :], wide(rsum[:, :].rearrange("p (t a) -> p t a", a=1), 2, NE),
                        ALU.mult).then_inc(S["prob_ready"], 1)
        filled(dve, "probsT", 0)
        frees(v.tensor_copy(probT, work_bank("probsT", 0)[0:NE, 0:T]), "probsT", 0)
        copied(dve, "probsT", 0)
        src = probT
        for r in range(CAP // 8):
            link(v.max(top8[0:NE, :], src))
            link(v.match_replace(probW, top8[0:NE, :], src, -1.0))
            src = probW
        v.tensor_scalar(mask, probW, 0.0, None, ALU.is_lt).then_inc(S["mask_ready"], 1)
        filled(dve, "maskT", 0)
        frees(v.tensor_copy(maskT[:, :, :].rearrange("p t e -> p (t e)"), work_bank("maskT", 0)[:, 0:2 * NE]),
              "maskT", 0)
        copied(dve, "maskT", 0)
        filled(dve, "slots", 0)
        frees(v.scalar_tensor_tensor(slot_of[:, :, :].rearrange("p t e -> p (t e)"),
                                     work_bank("slots", 0)[:, 0:2 * NE], 1.0,
                                     maskT[:, :, :].rearrange("p t e -> p (t e)"), ALU.add, ALU.mult), "slots", 0)
        copied(dve, "slots", 0)
        link(v.tensor_scalar(slot_of[:, :, :], slot_of[:, :, :], -1.0, None, ALU.add))
        for t in range(TT):
            link(v.tensor_tensor(sel[:, t, :, :], wide(const("iota", "p (a s) -> p a s", a=1), 1, NE),
                                 wide(slot_of[:, t, :].rearrange("p (e a) -> p e a", a=1), 2, CAP), ALU.is_equal))
        dve.wait_ge(S["prob_ready"], 1)
        for t in range(TT):
            for g in range(4):
                ins = v.tensor_tensor(sel_prob[:, t, :, g, :], sel[:, t, :, :],
                                      wide(prob[:, t, :].rearrange("p (e a) -> p e a", a=1), 2, CAP), ALU.mult)
            ins.then_inc(S["sel_prob_ready"], 1)
        with dve.Fori(0, NE) as e:
            filled(dve, "experts", 7, e)
            copied(dve, "experts", 3, e)
            frees(v.tensor_tensor(e_h, work_bank("experts", 7)[:, :], e_act, ALU.mult), "experts", 7)
        add_acc("experts_end", gate=row("gate_f"), batches=(0, 0))
        dve.wait_ge(S["x_new"], 2)
        mean(2)
        link(v.scalar_tensor_tensor(x[:, 0, :], x[:, 0, :], rstd[:, 0:1], row("g_final"), ALU.mult, ALU.mult))
        x_updated(v.scalar_tensor_tensor(x[:, 1, :], x[:, 1, :], rstd[:, 1:2], row("g_final"), ALU.mult, ALU.mult))
        dve.wait_ge(S["x_new"], 3)
        lam = col("lru_lambda_2", 0, 8)
        link(v.tensor_scalar(sp_b, lam, -1.0, 0.0, ALU.mult, ALU.max))
        v.scalar_tensor_tensor(sp_a, sp_b, -2.0, lam, ALU.mult, ALU.subtract)\
            .then_inc(S["lam_exp_in"], 1)
        normalise(3, 3)
        dve.wait_ge(S["lam_exp_out"], 1)
        link(v.tensor_scalar(nsp8, sp_a, 2.0, None, ALU.add))
        link(v.reciprocal(nsp8, nsp8))
        link(v.tensor_tensor(sp_a, sp_a, nsp8, ALU.mult))
        link(v.tensor_tensor(nsp8, sp_a, sp_a, ALU.mult))
        link(v.tensor_scalar(sp8, nsp8, 1.0 / 17, 1.0 / 15, ALU.mult, ALU.add))
        for n in range(13, 0, -2):
            link(v.tensor_tensor(sp8, sp8, nsp8, ALU.mult))
            link(v.tensor_scalar(sp8, sp8, 1.0 / n, None, ALU.add))
        link(v.tensor_tensor(sp8, sp8, sp_a, ALU.mult))
        link(v.scalar_tensor_tensor(sp8, sp8, 2.0, sp_b, ALU.mult, ALU.add))
        link(v.tensor_scalar(nsp8, sp8, -8.0, None, ALU.mult))
        v.tensor_scalar(sp8, sp8, 8.0, None, ALU.mult).then_inc(S["sp_ready"], 1)
        v.memset(ki[:, :, :], 0.0).then_inc(S["zeroed"], 1)
        filled(dve, "norm2", 3)
        for h in range(8):
            ins = v.tensor_copy(rel_rep[:, h, :], wide(rel_in[:, h:h + 1], 1, P))
        ins.then_inc(S["rel_ready"], 1)
        for i in range(4):
            copied(dve, "lru_x", i)
        for c in range(DC):
            ins = v.tensor_scalar(l_ua[:, c, :], l_t[:, c, :], col("lru_conv_w_2", 3 * DC + c),
                                  col("lru_conv_b_2", c), ALU.mult, ALU.add)
        for s in (1, 2, 3):
            link(ins)
            for c in range(DC):
                ins = v.scalar_tensor_tensor(l_ua[:, c, s:T], l_t[:, c, 0:T - s], col("lru_conv_w_2", (3 - s) * DC + c),
                                             l_ua[:, c, s:T], ALU.mult, ALU.add)
        ins.then_inc(S["ua_ready"], 1)
        dve.wait_ge(S["ua_ready"], 1)
        for i in range(4, 8):
            copied(dve, "lru_ri", i)
        link(v.tensor_tensor(l_i[:, :, :], l_i[:, :, :], l_ua[:, :, :], ALU.mult))
        dve.wait_ge(S["tanh_done"], 1)
        link(v.tensor_scalar(l_tmp[:, :, :], l_t[:, :, :], 1.0, None, ALU.add))
        link(v.reciprocal(l_tmp[:, :, :], l_tmp[:, :, :]))
        v.tensor_tensor(l_t[:, :, :], l_t[:, :, :], l_tmp[:, :, :], ALU.mult).then_inc(S["mult_in"], 1)
        dve.wait_ge(S["mult_out"], 1)
        link(v.tensor_tensor(l_i[:, :, :], l_i[:, :, :], l_t[:, :, :], ALU.mult))
        dve.wait_ge(S["decay_done"], 1)
        for c in range(DC):
            ins = v.tensor_tensor_scan(out=l_ua[:, c, :], data0=l_a[:, c, :], data1=l_i[:, c, :], initial=0.0,
                                       op0=ALU.mult, op1=ALU.add)
        ins.then_inc(S["scan_done"], 1)
        dve.wait_ge(S["scan_done"], 1)
        for i in range(4):
            copied(dve, "lru_gate", i)
        v.tensor_tensor(l_ua[:, :, :], l_ua[:, :, :], l_g[:, :, :], ALU.mult).then_inc(S["lru_ready"], 1)
        for i in range(5):
            a, r = (q2[:, 2 * i:2 * i + 2, :] if i < 4 else k2[:, :, :]).rearrange("p c t -> p (c t)"), msq[i % 2]
            filled(dve, "qk_ms", i)
            frees(v.tensor_scalar(r[:, :], work_bank("qk_ms", i)[:, :], EPS, None, ALU.add), "qk_ms", i)
            copied(dve, "qk_ms", i)
            v.reciprocal(r[:, :], r[:, :]).then_inc(S["msq_ready"], 1)
            dve.wait_ge(S["rsq_ready"], i + 1)
            v.scalar_tensor_tensor(a, a, col("q_norm_2" if i < 4 else "k_norm_2"), r[:, :], ALU.mult, ALU.mult)\
                .then_inc(S["qk_ready"], 1)
        copied(dve, "kiwi", 1)
        for t in range(TT):
            for m in range(4):
                copied(dve, "score", 4 * t + m)
                r = relu_s[m % 2]
                for d in range(2):
                    w = wi[:, t, 2 * m + d:2 * m + d + 1]
                    if m == 0 and d == 0:
                        link(v.tensor_scalar(score[:, t, :], r[:, 0:T], w, None, ALU.mult))
                    else:
                        ins = v.scalar_tensor_tensor(score[:, t, :], r[:, d * T:(d + 1) * T], w, score[:, t, :],
                                                     ALU.mult, ALU.add)
                        if d == 0:
                            link(ins)
                ins.then_inc(S["relu_used"], 1)
                dve.wait_ge(S["relu_used"], 4 * t + m + 1)
        link(v.tensor_tensor(score[:, :, :], score[:, :, :], causal, ALU.add))
        for t in range(TT):
            src = score[:, t, :]
            for r in range(8):
                link(v.max(t8, src))
                link(v.match_replace(score_w[:, t, :], t8, src, -3e38))
                src = score_w[:, t, :]
        link(v.tensor_scalar(score_w[:, :, :], score_w[:, :, :], -2e38, NEG, ALU.is_gt, ALU.mult))
        link(v.tensor_tensor(score_w[:, :, :], score_w[:, :, :], causal, ALU.add))
        for i in range(4):
            copied(dve, "gate_a", i)
            filled(dve, "lru_out", i)
            two = slice(2 * i, 2 * i + 2)
            frees(v.tensor_tensor(merged[:, two, :].rearrange("p c t -> p (c t)"), work_bank("lru_out", i)[:, :],
                                  l_a[:, two, :].rearrange("p c t -> p (c t)"), ALU.mult), "lru_out", i)
        dve.wait_ge(S["bias_in"], 16 * TT)
        for t in range(TT):
            for m in range(4):
                filled(dve, "logits2", 4 * t + m)
                frees(v.scalar_tensor_tensor(att[t][:, 2 * m:2 * m + 2, :].rearrange("p h s -> p (h s)"),
                                             work_bank("logits2", 4 * t + m)[:, :], P ** -0.5,
                                             bias2[:, t, 2 * m:2 * m + 2, :].rearrange("p h s -> p (h s)"),
                                             ALU.mult, ALU.add), "logits2", 4 * t + m)
            for m in range(4):
                copied(dve, "logits2", 4 * t + m)
            link(v.tensor_tensor(att[t][:, :, :], att[t][:, :, :],
                                 wide(score_w[:, t, :].rearrange("p (a s) -> p a s", a=1), 1, 8), ALU.add))
            v.tensor_reduce(nm2[:, t, :], att[t][:, :, :], AX.X, ALU.max, negate=True).then_inc(S["att_in"], 1)
        for t in range(TT):
            dve.wait_ge(S["att_exp"], t + 1)
            link(v.reciprocal(rs2[:, t, :], rs2[:, t, :]))
            v.tensor_tensor(att[t][:, :, :], att[t][:, :, :],
                            wide(rs2[:, t, :].rearrange("p (h a) -> p h a", a=1), 2, T), ALU.mult)\
                .then_inc(S["att_ready"], 1)
        for i in range(4):
            copied(dve, "gate_b", i)
            filled(dve, "attn_out", i)
            two = slice(2 * i, 2 * i + 2)
            frees(v.tensor_tensor(tmp[i % 2][:, :], work_bank("attn_out", i)[:, :],
                                  l_i[:, two, :].rearrange("p c t -> p (c t)"), ALU.mult), "attn_out", i)
            copied(dve, "attn_out", i)
            copied(dve, "lru_out", i)
            a = merged[:, two, :].rearrange("p c t -> p (c t)")
            v.tensor_tensor(a, a, tmp[i % 2][:, :], ALU.add).then_inc(S["merged_ready"], 1)
        add_acc("w_out2")
        dve.wait_ge(S["x_new"], 4)
        normalise(4, 4)
        n_f = F2 // P
        c0 = col_at["ffn_conv_w_2"][0]
        cb = col_at["ffn_conv_b_2"][0]
        link2 = sem("conv_step")
        with dve.Fori(0, plan.times["ffn2"]) as it:
            for b in range(4):
                filled(dve, "ffn2", b, it)
                g, fc = work_bank("ffn2", b), f_conv[b % 2]
                wc = lambda j: cols[:, bass.ds(c0 + j * n_f + b + 4 * it, 1)]
                v.tensor_scalar(fc, g[:, 0:T], wc(2), cols[:, bass.ds(cb + b + 4 * it, 1)], ALU.mult, ALU.add)\
                    .then_inc(link2, 1)
                dve.wait_ge(link2, 8 * it + 2 * b + 1)
                v.scalar_tensor_tensor(fc[:, 1:T], g[:, 0:T - 1], wc(1), fc[:, 1:T], ALU.mult, ALU.add)\
                    .then_inc(link2, 1)
                dve.wait_ge(link2, 8 * it + 2 * b + 2)
                v.scalar_tensor_tensor(fc[:, 2:T], g[:, 0:T - 2], wc(0), fc[:, 2:T], ALU.mult, ALU.add)\
                    .then_inc(S["conv_in"], 1)
                dve.wait_ge(S["gelu_done"], 4 * it + b + 1)
                frees(v.tensor_tensor(hid[:, b, :], g[:, T:2 * T], f_act[b % 2], ALU.mult), "ffn2", b)
        add_acc("ffn2_end", batches=(0, 0))
        dve.wait_ge(S["x_new"], 5)
        normalise(5, 5)
        for i in range(4):
            h, t = i // 2, i % 2
            copied(dve, "ple", i)
            filled(dve, "ple", 4 + i)
            frees(v.tensor_tensor(tmp[i][:, :], work_bank("ple", 4 + i)[:, :], p_gate[:, h, t, :], ALU.mult),
                  "ple", 4 + i)
            copied(dve, "ple", 4 + i)
            xs = x[:, t, 512 * h:512 * h + 512]
            ins = v.tensor_tensor(xs, xs, tmp[i][:, :], ALU.add)
            if i == 3:
                x_updated(ins)
            else:
                link(ins)
        dve.wait_ge(S["x_new"], 6)

        gelus = [4 * plan.times["ffn2"]]

        def ffn3(n, k):
            normalise(k, 0)
            name = f"ffn3_{n}"

            def tiles(name, n_b, base, it, per):
                for b in range(n_b):
                    dve.wait_ge(S["gelu_done"], base + b + 1 + per * it)
                    frees(v.tensor_tensor(hid[:, b, :], work_bank(name, b)[:, T:2 * T], f_act[b % 2], ALU.mult),
                          name, b)

            with dve.Fori(0, plan.times[name]) as it:
                tiles(name, 4, gelus[0], it, 4)
            gelus[0] += 4 * plan.times[name]
            filled(dve, name, 4, plan.times[name] - 1)
            tiles(name + "_end", 2, gelus[0], 0, 0)
            gelus[0] += 2
            add_acc(name + "_end", scale=0.5, batches=(2, 2))

        def rope(name, i, a, n):
            k = (0 if name == "nsa_rope" else 7) + i
            filled(dve, name, i)
            sin = const("rope_sin", "p (a t) -> p a t", a=1)
            cos = const("rope_cos", "p (a t) -> p a t", a=1)
            if n > 1:
                sin, cos = wide(sin, 1, n), wide(cos, 1, n)
            t_ = tmp[i % 2][:, 0:n * T].rearrange("p (c t) -> p c t", c=n)
            frees(v.tensor_tensor(t_, work_bank(name, i)[:, 0:n * T].rearrange("p (c t) -> p c t", c=n), sin,
                                  ALU.mult), name, i)
            link(v.tensor_tensor(a, a, cos, ALU.mult))
            copied(dve, name, i)
            v.tensor_tensor(a, a, t_, ALU.add).then_inc(S["rope_ready"], 1)

        def row_max(name, i, slot):
            filled(dve, name, i)
            link(v.tensor_reduce(nm3[slot], work_bank(name, i)[:, :].rearrange("p (d s) -> p d s", d=2), AX.X,
                                 ALU.max, negate=True))
            v.tensor_scalar(nm3[slot], nm3[slot], 64 ** -0.5, None, ALU.mult).then_inc(S["max3_ready"], 1)

        def weigh(name, i, slot, gate):
            copied(dve, name, i)
            link(v.reciprocal(rw3[slot], rs3[slot]))
            link(v.tensor_tensor(rw3[slot], rw3[slot], gate, ALU.mult))
            v.tensor_tensor(p3[slot][:, :, :], p3[slot][:, :, :],
                            wide(rw3[slot].rearrange("p (d a) -> p d a", a=1), 2, T), ALU.mult)\
                .then_inc(S["p3_ready"], 1)

        ffn3(0, 6)
        dve.wait_ge(S["x_new"], 7)
        normalise(7, 0)
        for i in range(4):
            copied(dve, "nsa_q", i)
            rope("nsa_rope", i, q3[:, 2 * i:2 * i + 2, :], 2)
        for i in range(3):
            rope("nsa_rope", 4 + i, kraw[:, 2 * i:2 * i + 2, :], 2)
        dve.wait_ge(S["rope_ready"], 7)
        v.memset(kc[:, :, :, :], 0.0).then_inc(S["zeroed"], 1)
        for src, dst in ((kraw[:, 0:2, :], kp), (vraw, vp)):
            for half in range(2):
                v.tensor_copy(dst[0:64, half:4:2, :], src[64 * half:64 * half + 64, :, :])
                ins = v.tensor_copy(dst[64:128, half:4:2, 0:T - 1], src[64 * half:64 * half + 64, :, 1:T])
        link(ins)
        for i, (src, pe_) in enumerate(((kp, "nsa_ck_pe_3"), (vp, "nsa_cv_pe_3"))):
            for a in range(2):
                win = src[:, :, BS * a:BS * a + BS * NB].rearrange("p g (b m two) -> p m g b two", b=NB, two=2)
                bias = wide(wide(col(pe_, 8 * a, 8).rearrange("p (m a b) -> p m a b", a=1, b=1), 2, 4), 3, NB)
                for m in range(8):
                    ins = v.tensor_tensor(xb[i][:, 8 * a + m, :, :], win[:, m, :, :, 0], bias[:, m, :, :], ALU.add)
        ins.then_inc(S["cmp_x_ready"], 1)
        dve.wait_ge(S["cmp_x_ready"], 1)
        for br in range(2):
            link(v.memset(A[3 + br][:, :], 0.0))
            for half in range(2):
                for d in range(2):
                    ins = v.tensor_copy(kd[br][64 * d:64 * d + 64, half:4:2, d, :],
                                        kraw[64 * half:64 * half + 64, 2 + 2 * br:4 + 2 * br, :])
        link(ins)
        copied(dve, "nsa_g", 0)
        for t in range(TT):
            filled(dve, "cmp_s", t)
            frees(v.tensor_scalar(pc[:, t, :, :].rearrange("p h b -> p (h b)"), work_bank("cmp_s", t)[:, 0:240],
                                  64 ** -0.5, None, ALU.mult), "cmp_s", t)
        for t in range(TT):
            copied(dve, "cmp_s", t)
        for t in range(TT):
            ins = v.tensor_tensor(pc[:, t, :, :], pc[:, t, :, :],
                                  wide(const("cmp_neg", "p (t a b) -> p t a b", t=TT, a=1)[:, t, :, :], 1, 16),
                                  ALU.add)
        link(ins)
        link(v.reduce_max(cm[:, :, :], pc[:, :, :, :], AX.X))
        v.tensor_tensor(pc[:, :, :, :].rearrange("p t h b -> p (t h) b"), pc[:, :, :, :].rearrange("p t h b -> p (t h) b"),
                        wide(cm[:, :, :].rearrange("p t (h a) -> p (t h) a", a=1), 2, NB),
                        ALU.subtract).then_inc(S["cmp_in"], 1)
        dve.wait_ge(S["cmp_exp"], 1)
        link(v.reduce_sum(cr[:, :, :], pc[:, :, :, :], AX.X))
        link(v.reciprocal(cr[:, :, :], cr[:, :, :]))
        link(v.tensor_tensor(cr[:, :, :], cr[:, :, :], gate3[:, :, 0, :], ALU.mult))
        link(v.tensor_tensor(pc[:, :, :, :].rearrange("p t h b -> p (t h) b"), pc[:, :, :, :].rearrange("p t h b -> p (t h) b"),
                             wide(cr[:, :, :].rearrange("p t (h a) -> p (t h) a", a=1), 2, NB), ALU.mult))
        for t in range(TT):
            ins = v.tensor_tensor(pc[:, t, :, :], pc[:, t, :, :],
                                  wide(const("cmp_one", "p (t a b) -> p t a b", t=TT, a=1)[:, t, :, :], 1, 16),
                                  ALU.mult)
        ins.then_inc(S["cmp_ready"], 1)
        for m in range(8):
            for s in range(4):
                row_max("nsa_heads", 10 * m + s, s)
            for s in range(4):
                br, t = s // 2, s % 2
                weigh("nsa_heads", 10 * m + s, s, gate3[:, t, 1 + br, 2 * m:2 * m + 2])
        add_acc("nsa_out")
        dve.wait_ge(S["x_new"], 8)
        ffn3(1, 8)
        dve.wait_ge(S["x_new"], 9)
        ffn3(2, 9)
        dve.wait_ge(S["x_new"], 10)
        normalise(10, 0)
        for i in range(4):
            copied(dve, "swa_q", i)
            rope("swa_rope", i, q3[:, 2 * i:2 * i + 2, :], 2)
        copied(dve, "swa_kv", 0)
        filled(dve, "swa_rope", 4)
        frees(v.tensor_tensor(tmp[0][:, 0:T], work_bank("swa_rope", 4)[:, 0:T], const("rope_sin"), ALU.mult),
              "swa_rope", 4)
        link(v.tensor_tensor(k4, k4, const("rope_cos"), ALU.mult))
        copied(dve, "swa_rope", 4)
        link(v.tensor_tensor(k4, k4, tmp[0][:, 0:T], ALU.add))
        link(v.memset(kd4[:, :, :, :], 0.0))
        for half in range(2):
            for d in range(2):
                ins = v.tensor_copy(kd4[64 * d:64 * d + 64, half, d, :], k4[64 * half:64 * half + 64, :])
        ins.then_inc(S["rope_ready"], 1)
        for m in range(8):
            sinks = row("sinks")[:, 2 * m:2 * m + 2]
            for t in range(TT):
                slot, i = 2 * (m % 2) + t, 5 * m + t
                filled(dve, "swa_heads", i)
                link(v.tensor_reduce(nm3[slot], work_bank("swa_heads", i)[:, :].rearrange("p (d s) -> p d s", d=2),
                                     AX.X, ALU.max))
                link(v.scalar_tensor_tensor(nm3[slot], nm3[slot], 64 ** -0.5, sinks, ALU.mult, ALU.max))
                link(v.tensor_tensor(sk[t], sinks, nm3[slot], ALU.subtract))
                v.tensor_scalar(nm3[slot], nm3[slot], -1.0, None, ALU.mult).then_inc(S["max3_ready"], 1)
            for t in range(TT):
                slot, i = 2 * (m % 2) + t, 5 * m + t
                copied(dve, "swa_heads", i)
                dve.wait_ge(S["sink_exp"], 2 * m + t + 1)
                link(v.tensor_tensor(rw3[slot], rs3[slot], sk[t], ALU.add))
                link(v.reciprocal(rw3[slot], rw3[slot]))
                v.tensor_tensor(p3[slot][:, :, :], p3[slot][:, :, :],
                                wide(rw3[slot].rearrange("p (d a) -> p d a", a=1), 2, T), ALU.mult)\
                    .then_inc(S["p3_ready"], 1)
        add_acc("swa_out")
        dve.wait_ge(S["x_new"], 11)
        ffn3(3, 11)
        dve.wait_ge(S["x_new"], 12)
        mean(12)
        dve.wait_ge(S["final_row_in"], 16)
        for t in range(TT):
            v.scalar_tensor_tensor(xn[:, t, :], x[:, t, :], rstd[:, t:t + 1], row("gate_m"), ALU.mult, ALU.mult)\
                .then_inc(S["out_ready"], 1)

    ctx.close()


OUT_SHAPE = (1, T, D)
WEIGHTS = {
    "w_ada": D, "w_in": D, "w_fourier": 512, "w_conv_out": D, "w_o": D, "w_router": D,
    "w_gate_e": NE * D, "w_up_e": NE * D, "w_down_e": NE * DE, "w_in_2": D, "lru_wa_2": D, "lru_wx_2": D,
    "w_lru_br_2": D, "w_attn_br_2": D, "w_out_2": D, "w_up_2": D, "w_down_2": F2, "w_ple_gate_2": D,
    "w_ple_proj_2": 256, "rel_bias_2": 32, "ffn1_w_gu_3": 2 * D, "ffn1_w_down_3": 2 * F3,
    "ffn2_w_gu_3": 2 * D, "ffn2_w_down_3": 2 * F3, "nsa_w_in_3": D, "nsa_ck_w1_3": 2048, "nsa_ck_w2_3": P,
    "nsa_cv_w1_3": 2048, "nsa_cv_w2_3": P, "nsa_w_out_3": D, "swa_w_in_3": D, "swa_w_out_3": D, "x": T,
}


def kernel(**inputs):
    import numpy as _np
    import concourse.bacc as _bacc
    from concourse import mybir as _mybir
    from concourse.bass_utils import run_bass_kernel_spmd as _run

    def given(name):
        return _np.asarray(inputs[name])

    nc = _bacc.Bacc("TRN2", target_bir_lowering=False, num_devices=1)
    arrays = {name: _np.ascontiguousarray(given(name)).reshape(rows, -1) for name, rows in WEIGHTS.items()}
    arrays["consts"], const_at = shape_constants()
    arrays["cols"], col_at = column_inputs(given)
    arrays["rows"], row_at = row_inputs(given)
    arrays["final_norm"] = _np.ascontiguousarray(given("final_norm_3").reshape(1, D))
    arrays["pT"] = _np.ascontiguousarray(given("p_2").reshape(T, 256).T)
    handles = {n: nc.dram_tensor(f"in_{n}", a.shape, _mybir.dt.from_np(a.dtype), kind="ExternalInput").ap()
               for n, a in arrays.items()}
    out = nc.dram_tensor("out_0", (T, D), _mybir.dt.float32, kind="ExternalOutput").ap()
    network(nc, lambda name: handles[name], out, const_at, col_at, row_at)
    r = _run(nc, [{f"in_{n}": a for n, a in arrays.items()}], core_ids=[0])
    return r.results[0]["out_0"].reshape(OUT_SHAPE)
```

```python
from contextlib import ExitStack

import numpy as np

import concourse.bass as bass
from concourse import mybir

T, D = 256, 1024
P = 128
TT, DC = T // P, D // P
EPS = 1e-6
NEG = -1e30
NE, CAP, DE = 16, 32, 2048
F2, F3 = 3072, 2816
NSLOT, SLAB = 3, 4096
NB, BL, BS = 15, 32, 16


def shape_constants():
    i128 = np.arange(P)
    tok = np.arange(T)
    parts = {}
    parts["ident"] = np.eye(P)
    parts["tri"] = (i128[:, None] < i128[None, :])
    ang = 2 * np.pi * ((tok[:, None] * tok[None, :]) % T) / T
    norm = 1 / math_sqrt(T * P)
    cs = np.concatenate([np.cos(ang), -np.sin(ang)], 1) * norm
    parts["dft_seq"] = cs.reshape(TT, P, 2 * T).transpose(1, 0, 2).reshape(P, -1)
    angc = 2 * np.pi * ((i128[:, None] * i128[None, :]) % P) / P
    parts["dft_cos"] = np.cos(angc)
    parts["dft_sin"] = np.sin(angc)
    t = tok.reshape(TT, P).T[:, :, None]
    s = tok[None, None, :]
    masks = np.stack([np.where(s <= t, 0.0, NEG), np.where((s <= t) & (t - s < P), 0.0, NEG)], 1)
    n = np.arange(NB)[None, None, :]
    valid = (n * BS + BL - 1 <= t)
    parts["cmp_neg"] = np.where(valid, 0.0, NEG).reshape(P, -1)
    parts["cmp_one"] = valid.reshape(P, -1)
    parts["iota"] = np.broadcast_to(np.arange(CAP), (P, CAP))
    inv = (np.float32(10000.0) ** (-np.arange(0, 64, 2, dtype=np.float32) / np.float32(64)))
    rope = tok.astype(np.float32)[None, :] * inv.astype(np.float32)[:, None]
    parts["rope_cos"] = np.tile(np.cos(rope), (4, 1))
    parts["rope_sin"] = np.tile(np.sin(rope), (4, 1))
    rot = np.zeros((P, P))
    for h in range(0, P, 64):
        for j in range(32):
            rot[h + 32 + j, h + j] = -1.0
            rot[h + j, h + 32 + j] = 1.0
    parts["rope_rot"] = rot
    dist = np.maximum(255 - np.arange(2 * T), 0)
    df = np.maximum(dist, 1).astype(np.float32)
    large = 16 + (np.log(df / np.float32(16)) / np.float32(math_log(128 / 16)) * np.float32(16)).astype(np.int32)
    bucket = np.where(dist < 16, dist, np.minimum(large, 31))
    oh = np.zeros((P, 2 * T))
    oh[bucket, np.arange(2 * T)] = 1.0
    parts["buckets"] = oh
    return pack(parts), masks.astype(np.float32).reshape(P, -1)


def math_sqrt(v):
    return float(np.sqrt(v))


def math_log(v):
    return float(np.log(v))


def pack(parts):
    at, where, cols = 0, {}, []
    for name, a in parts.items():
        a = np.asarray(a, np.float32).reshape(P, -1)
        where[name] = (at, a.shape[1])
        at += a.shape[1]
        cols.append(a)
    return np.ascontiguousarray(np.concatenate(cols, 1)), where


def column_inputs(v):
    def col(a):
        a = a.reshape(-1, P)
        return a.T
    parts = {"c": col(v("c"))}
    for name in ("b_ada", "g_norm_mix", "b_gate", "w_conv", "g_norm_moe", "mix_norm_2", "lru_conv_w_2",
                 "lru_conv_b_2", "lru_ba_2", "lru_bx_2", "lru_lambda_2", "q_norm_2", "k_norm_2", "ffn_norm_2",
                 "ffn_conv_w_2", "ffn_conv_b_2", "ple_norm_2", "ffn1_norm_3", "mix_norm_3", "ffn2_norm_3",
                 "nsa_ck_pe_3", "nsa_cv_pe_3"):
        parts[name] = col(v(name))
    return pack(parts)


def row_inputs(v):
    b_ada = v("b_ada").reshape(-1)
    parts = {"g_final": v("g_final"), "gate_m": b_ada[2 * D:3 * D],
             "gate_f": b_ada[5 * D:6 * D], "b_router": v("b_router"), "sinks": v("swa_sinks_3")}
    at, where, rows = 0, {}, []
    for name, a in parts.items():
        a = a.reshape(1, -1)
        where[name] = (at, a.shape[1])
        at += a.shape[1]
        rows.append(a)
    return np.ascontiguousarray(np.concatenate(rows, 1)), where


class Plan:

    def __init__(self):
        self.split0, self.split_body, self.splits = {}, {}, 0
        self.batch0, self.work0, self.slab0, self.kinds, self.times = {}, {}, {}, {}, {}
        self.slab0_body = {}
        self.batches = self.works = self.slabs = 0
        self.slab_end = []

    def add(self, name, kinds, frees=(), times=1, split=0):
        self.split0[name], self.split_body[name] = self.splits, split
        self.splits += split * times
        self.batch0[name], self.work0[name], self.slab0[name] = self.batches, self.works, self.slabs
        self.kinds[name], self.times[name] = kinds, times
        self.slab0_body[name] = len(frees)
        for k in range(times):
            self.slab_end += [self.batches + k * len(kinds) + f + 1 for f in frees]
        self.batches += times * len(kinds)
        self.works += times * kinds.count("W")
        self.slabs += times * len(frees)

    def done(self, name, i):
        return self.batch0[name] + i + 1

    def work(self, name, i):
        return self.work0[name] + self.kinds[name][:i].count("W")


def pair_scores(m, n_s, n_w):
    return 0 if m == 0 else n_s + (n_s + n_w) * (m - 1)


def pair_rest(m, n_s, n_w):
    return n_s + (n_s + n_w) * m + (n_s if m < 7 else 0)


def make_plan():
    p = Plan()
    p.add("ada", "WW" * 12, [2 * m for m in range(12)])
    p.add("norm0", "WWWW")
    p.add("uf", "WW", [1])
    p.add("dft_a", "WWWW")
    p.add("dft_b", "WW")
    p.add("vbc", "WW" * 6, [2 * s + 1 for s in range(6)])
    p.add("gates", "WW" * 4, [2 * s + 1 for s in range(4)])
    p.add("fourier_out", "WWWW", [3])
    p.add("conv_out", "WWWW", [1, 3])
    p.add("w_o", "AA", [0, 1])
    p.add("norm1", "WWWW")
    p.add("router", "W")
    p.add("probsT", "W")
    p.add("maskT", "W")
    p.add("slots", "W")
    p.add("scatterT", "W" * 8)
    p.add("gather", "W" * 8)
    p.add("experts", "AAAW" + "AAAW" + "W" + "AAAW" + "A", [0, 1, 2, 3, 4, 5, 6, 7, 9, 10, 11, 12], times=NE)
    p.add("experts_end", "A")
    p.add("norm2", "WWWW")
    p.add("lru_x", "WWWW", [1, 3])
    p.add("lru_gate", "WWWW", [1, 3])
    p.add("q", "WWWW", [1, 3])
    p.add("lru_ri", "W" * 8, [7])
    p.add("kv", "WW", [1])
    p.add("qi", "WW", [1])
    p.add("kiwi", "WW")
    p.add("qk_ms", "W" * 5)
    p.add("bias", "W" * 8)
    p.add("gate_a", "WWWW", [1, 3])
    p.add("score", "W" * 8)
    p.add("gate_b", "WWWW", [1, 3])
    p.add("lru_out", "WWWW", [1, 3])
    p.add("logits2", "W" * 8)
    p.add("pv2", "WWW" * 4)
    p.add("attn_out", "WWWW", [1, 3])
    p.add("w_out2", "AA", [0, 1])
    p.add("norm3", "WWWW")
    p.add("ffn2", "WWWWA", [1, 3, 4], times=F2 // 512, split=3)
    p.add("ffn2_end", "A")
    p.add("norm4", "WWWW")
    p.add("ple", "WW" * 2 + "WWWW", [1, 3, 7], split=2)
    for n in range(4):
        p.add(f"ffnorm{n}", "WWWW")
        p.add(f"ffn3_{n}", "WWWWA", [1, 3, 4], times=5, split=3)
        p.add(f"ffn3_{n}_end", "WWA", [1, 2], split=2)
        if n == 0:
            p.add("nsa_norm", "WWWW")
            p.add("nsa_q", "WWWW", [1, 3])
            p.add("nsa_kv0", "WW", [1])
            p.add("nsa_kv12", "WW" * 2, [1, 3])
            p.add("nsa_g", "W")
            p.add("nsa_rope", "W" * 7)
            p.add("cmp_hid", "WW", [1])
            p.add("cmp_kv", "WW")
            p.add("cmp_s", "WW")
            p.add("nsa_heads", "AAAA" + ("AAAA" + "WWWWWW") * 7 + "WWWWWW")
            p.add("nsa_out", "AA", [0, 1])
        if n == 2:
            p.add("swa_norm", "WWWW")
            p.add("swa_q", "WWWW", [1, 3])
            p.add("swa_kv", "W", [0])
            p.add("swa_rope", "W" * 5)
            p.add("swa_heads", "AA" + ("AA" + "WWW") * 7 + "WWW")
            p.add("swa_out", "AA", [0, 1])
    return p


def network(nc, dram, out, const_at, col_at, row_at):
    fp32, fp32r, bf16 = mybir.dt.float32, mybir.dt.float32r, mybir.dt.bfloat16
    ALU = mybir.AluOpType
    ACT = mybir.ActivationFunctionType
    AX = mybir.AxisListType
    plan = make_plan()
    ctx = ExitStack()

    def sb(name, shape):
        return ctx.enter_context(nc.sbuf_tensor(name, shape, fp32))

    twins = {}

    def twinned(name, shape):
        with nc.sbuf_tensor(name, shape, fp32) as plain:
            pass
        twins[name] = ctx.enter_context(nc.sbuf_tensor(f"{name}_r", shape, fp32r))
        return plain

    def sem(name):
        return ctx.enter_context(nc.semaphore(name))

    n_const = sum(w for _, w in const_at.values())
    n_col = sum(w for _, w in col_at.values())
    n_row = sum(w for _, w in row_at.values())
    ring = [twinned(f"ring{i}", [P, SLAB]) for i in range(NSLOT)]
    consts = sb("consts", [P, n_const])
    cols = sb("cols", [P, n_col])
    rows = sb("rows", [P, n_row])
    x = sb("x", [P, TT, D])
    xn = sb("xn", [P, TT, D])
    hT = twinned("hT", [P, DC, T])
    AB, AC = twinned("AB", [P, 4096]), twinned("AC", [P, 4096])
    A = [twinned(f"A{i}", [P, 2048]) for i in range(9) if i not in (1, 2)]
    A[1:1] = [AC[:, 0:2048], AC[:, 2048:4096]]
    w_router = sb("w_router_sb", [P, DC, NE])
    w_kiwi = sb("w_kiwi", [P, DC, 72])
    w_nsa_gate = sb("w_nsa_gate", [P, DC, 48])
    ck_w2 = sb("ck_w2", [P, 64])
    cv_w2 = sb("cv_w2", [P, 64])
    pT_in = sb("pT_in", [P, 2, T])
    rel_in = sb("rel_in", [32, 8])
    ones = sb("ones", [P, P])
    ones_mean = sb("ones_mean", [P, P])
    zeros = ctx.enter_context(nc.sbuf_tensor("zeros", [P, 512], bf16))
    diag = sb("diag", [P, TT, P])
    ident16 = ctx.enter_context(nc.sbuf_tensor("ident16", [P, P], bf16))
    masks16 = ctx.enter_context(nc.sbuf_tensor("masks16", [P, 2 * TT, T], bf16))
    causal16, window16 = masks16[:, 0:TT, :], masks16[:, TT:2 * TT, :]
    neg_half = sb("neg_half", [P, TT])
    tmp = [sb(f"tmp{i}", [P, 512]) for i in range(4)]
    small = sb("small", [P, 640])

    def const(name, shape=None, **k):
        at, n = const_at[name]
        v = consts[:, at:at + n]
        return v.rearrange(shape, **k) if shape else v

    def col(name, i=0, n=1):
        return cols[:, col_at[name][0] + i:col_at[name][0] + i + n]

    def row(name):
        at, n = row_at[name]
        return rows[:, at:at + n]

    small_at = [0]

    def narrow(n):
        small_at[0] += n
        assert small_at[0] <= 640
        return small[:, small_at[0] - n:small_at[0]]

    ident = const("ident")
    fm = lambda a: a[:, :].rearrange("p (c t) -> p c t", t=T)

    junk = hT[:, :, :].rearrange("p (a c) t -> p a (c t)", a=TT)
    rel_rep = xn[0:32, 0, :].rearrange("p (h n) -> p h n", h=8)

    masks_in = A[8][:, 0:2 * TT * T]
    ss, ms, rstd = narrow(2), narrow(2), narrow(2)
    c_act = narrow(8)
    c_pad = A[0][:, 0:256].rearrange("p (k m) -> p k m", m=32)
    mod_part = [tmp[0], tmp[1]]
    modc = narrow(48)
    g_mix, g_moe = narrow(8), narrow(8)
    uf = A[0][:, 0:1024].rearrange("p (t n) -> p t n", t=TT)
    dft_v = A[1][:, :].rearrange("p (g n) -> p g n", g=4)
    yT = A[0][:, 1024:2048].rearrange("p (g t) -> p g t", g=4)
    f_v, f_b, f_cv, f_ga, f_gb, f_bc, f_z = (fm(A[i]) for i in (2, 3, 4, 5, 6, 7, 8))
    logit = narrow(32).rearrange("p (t e) -> p t e", t=TT)
    prob = narrow(32).rearrange("p (t e) -> p t e", t=TT)
    rmax, rsum = narrow(2), narrow(2)
    probT = tmp[0][0:NE, 0:T]
    probW = tmp[1][0:NE, 0:T]
    mask = tmp[2][0:NE, 0:T]
    top8 = narrow(8)
    maskT = narrow(32).rearrange("p (t e) -> p t e", t=TT)
    slot_of = narrow(32).rearrange("p (t e) -> p t e", t=TT)
    sel = A[0][:, 0:1024].rearrange("p (t e s) -> p t e s", t=TT, e=NE)
    sel_prob = AB[:, :].rearrange("p (t e g s) -> p t e g s", t=TT, e=NE, g=4)
    scat = AC[:, :].rearrange("p (e t) -> p e t", e=NE)
    xeT = AB[:, :].rearrange("p (c s) -> p c s", c=DC)
    xe_now = A[3][:, 0:256].rearrange("p (c s) -> p c s", c=DC)
    scat_now = A[3][:, 256:512]
    e_act, e_h, e_hT, e_y = (A[3][:, 512:1024], A[3][:, 1024:1536], A[3][:, 1536:2048], A[4][:, 0:512])
    l_t, l_ua, l_a, l_i, l_tmp, l_g = (fm(A[i]) for i in (0, 1, 2, 3, 4, 8))
    sp8, nsp8, sp_a, sp_b = narrow(8), narrow(8), narrow(8), narrow(8)
    q2 = fm(A[7])
    sq2 = fm(A[6])
    k2 = A[5][:, 0:512].rearrange("p (g t) -> p g t", g=2)
    v2 = A[5][:, 512:1024].rearrange("p (t n) -> p t n", t=TT)
    qi = A[5][:, 1024:2048].rearrange("p (c t) -> p c t", t=T)
    ki = tmp[0][:, :].rearrange("p (d t) -> p d t", d=2)
    wi = narrow(16).rearrange("p (t h) -> p t h", t=TT)
    sqk = tmp[1]
    bias2 = AB[:, :].rearrange("p (t h s) -> p t h s", t=TT, h=8)
    bias_row = AB[:, :].rearrange("p (h j) -> p h j", h=8)
    msq = [tmp[2], tmp[3]]
    relu_s = [A[6][:, 0:512], A[6][:, 512:1024]]
    score = A[6][:, 1024:1536].rearrange("p (t s) -> p t s", t=TT)
    score_w = A[6][:, 1536:2048].rearrange("p (t s) -> p t s", t=TT)
    t8 = narrow(8)
    att = [fm(A[4]), fm(A[8])]
    nm2 = narrow(16).rearrange("p (t h) -> p t h", t=TT)
    rs2 = narrow(16).rearrange("p (t h) -> p t h", t=TT)
    pT2 = [tmp[2], tmp[3]]
    o2 = fm(A[1])
    merged = fm(A[0])
    h_high = twins["A7"][:, :].rearrange("p (c t) -> p c t", t=T)
    h_low = twins["hT"]
    hid_high = twins["A8"][:, 0:1024].rearrange("p (f t) -> p f t", t=T)
    hid_low = twins["A0"][:, 0:1024].rearrange("p (f t) -> p f t", t=T)

    def split_areas(name, s):
        if name.endswith("_end") and s == 1:
            return [(0, twins["A5"])]
        return ([(0, twins["AB"])], [(0, twins["AC"])], [(0, twins["A3"]), (2048, twins["A4"])])[s]

    def hidden_tiles(n):
        return (F2 + n * F3) // P

    hid = A[0][:, 0:1024].rearrange("p (f t) -> p f t", t=T)
    f_conv = [tmp[0][:, 0:256], tmp[1][:, 0:256]]
    f_act = [tmp[2][:, 0:256], tmp[3][:, 0:256]]
    p_gate = A[6][:, :].rearrange("p (h t n) -> p h t n", h=2, t=TT)
    q3 = fm(A[0])
    kraw = A[1][:, 0:1536].rearrange("p (c t) -> p c t", t=T)
    vraw = A[1][:, 1536:2048].rearrange("p (c t) -> p c t", t=T)
    v3 = A[2][:, 0:1024].rearrange("p (b t n) -> p b t n", b=2, t=TT)
    kd = [A[i][:, :].rearrange("p (g d t) -> p g d t", g=4, d=2) for i in (3, 4)]
    kp = A[4][:, 0:1024].rearrange("p (g t) -> p g t", g=4)
    vp = A[4][:, 1024:2048].rearrange("p (g t) -> p g t", g=4)
    xb = [A[5][:, 0:960].rearrange("p (m g b) -> p m g b", m=16, g=4),
          A[5][:, 960:1920].rearrange("p (m g b) -> p m g b", m=16, g=4)]
    hid_c = [A[2][:, 1024:1084], A[2][:, 1084:1144]]
    kc = A[2][:, 1144:1264].rearrange("p (d g b) -> p d g b", d=2, g=4)
    vc = A[2][0:NB, 1264:1520]
    gate3 = narrow(96).rearrange("p (t b h) -> p t b h", t=TT, b=3)
    pc = A[6][:, 0:480].rearrange("p (t h b) -> p t h b", t=TT, h=16)
    cm, cr = (narrow(32).rearrange("p (t h) -> p t h", t=TT) for _ in range(2))
    p3 = [A[a][:, 512 * i:512 * i + 512].rearrange("p (d s) -> p d s", d=2) for a in (7, 1) for i in range(4)]
    pT3 = [AB[:, 512 * i:512 * i + 384] for i in range(4)]
    pcT = AB[0:NB, 2048:2560]
    o3 = fm(A[8])
    nm3 = [narrow(2) for _ in range(8)]
    rs3 = [narrow(2) for _ in range(8)]
    rw3 = [narrow(2) for _ in range(8)]
    v4 = A[2][:, 0:256].rearrange("p (t n) -> p t n", t=TT)
    k4 = A[1][:, 0:256]
    kd4 = A[3][:, 0:1024].rearrange("p (g d t) -> p g d t", g=2, d=2)
    sk = [narrow(2) for _ in range(4)]

    skew = nc.dram_tensor("bias_rows", [P * 8 * 512], fp32, kind="Internal").ap()

    bank = [ctx.enter_context(nc.psum_tensor(f"bank{i}", [P, 512], fp32)) for i in range(8)]
    acc = [[bank[0], bank[1]], [bank[2], bank[3]]]

    products_done = sem("products_done")
    bank_copied = [sem(f"bank_copied{i}") for i in range(4)]
    slab_loaded = [sem(f"slab_loaded{i}") for i in range(NSLOT)]
    inputs_loaded = sem("inputs_loaded")
    fills_done = sem("fills_done")
    own = {e: sem(f"{e}_own") for e in ("dve", "act", "pool")}

    def filled(eng, name, i, it=0):
        eng.wait_ge(products_done, plan.done(name, i) + it * len(plan.kinds[name]))

    def loaded(eng, name, s, it=0):
        n = plan.slab0[name] + s
        per_pass = plan.slab0_body[name] // NSLOT * 32 if plan.times[name] > 1 else 0
        eng.wait_ge(slab_loaded[n % NSLOT], 32 * (n // NSLOT + 1) + it * per_pass)
        return ring[n % NSLOT]

    def split_number(name, s, it=0):
        return plan.split0[name] + s + 1 + it * plan.split_body[name]

    def work_bank(name, i):
        return bank[4 + plan.work(name, i) % 4]

    def copied(eng, name, i, it=0):
        w = plan.work(name, i)
        eng.wait_ge(bank_copied[w % 4], w // 4 + 1 + it * (plan.kinds[name].count("W") // 4))

    def frees(ins, name, i):
        return ins.then_inc(bank_copied[plan.work(name, i) % 4], 1)

    class Chain:

        def __init__(self, eng, which):
            self.eng, self.sem, self.n, self.off = eng, own[which], 0, 0

        def __call__(self, ins):
            ins.then_inc(self.sem, 1)
            self.n += 1
            self.eng.wait_ge(self.sem, self.n + self.off)

    def wide(a, dim, n):
        shape = list(a.shape)
        assert shape[dim] == 1
        shape[dim] = n
        return a.broadcast_to(shape)

    names = ("c_act_ready", "c_pad_ready", "mod_ready", "x_new", "squares_done", "mean_ready", "rstd_ready",
             "xn_ready", "conv_ready", "z_ready", "logit_ready", "exp_ready", "prob_ready", "mask_ready", "zeroed", "msq_ready",
             "sel_ready", "sel_prob_ready", "maskT_ready", "expert_staged", "rel_ready", "rows_out", "bias_in",
             "lam_exp_in", "lam_exp_out", "sp_ready", "ua_ready", "tanh_done", "decay_done", "mult_in",
             "mult_out", "scan_done", "lru_ready", "rsq_ready", "qk_ready", "relu_used",
             "att_in", "att_exp", "att_ready", "merged_ready", "conv_in", "gelu_done", "rope_ready",
             "final_row_in", "high_ready", "low_ready", "high_norm", "hid_split", "cmp_x_ready", "cmp_in", "cmp_exp", "cmp_ready", "max3_ready", "exp3_done", "masks16_ready", "p3_ready", "sink_exp",
             "out_ready", "out_stored")
    S = {n: sem(n) for n in names}

    NORMS = ["norm0", "norm1", "g_final", "norm2", "norm3", "norm4", "ffnorm0", "nsa_norm", "ffnorm1",
             "ffnorm2", "swa_norm", "ffnorm3", "final"]
    N_INPUTS, N_FILLS = 16 * 12, 5
    dft_seq = const("dft_seq", "p (t n) -> p t n", t=TT)
    block = ctx.enter_context(nc.Block())

    @block.sync
    def _(sp):
        def k_rows(w, c0, n):
            return w[:, c0:c0 + n].rearrange("(k p) n -> p k n", p=P)

        def two_halves(slot, src, n):
            dst = ring[slot][:, 0:8 * n].rearrange("p (k n) -> p k n", k=8)
            return [(dst[:, 4 * a:4 * a + 4, :], src[:, 4 * a:4 * a + 4, :]) for a in range(2)]

        def row_block(slot, w, r0, n):
            dst = ring[slot][:, 0:n * D].rearrange("p (k n) -> p k n", k=n)
            src = w[r0:r0 + n * P, :].rearrange("(k p) n -> p k n", p=P)
            h = n // 2
            return [(dst[:, 0:h, :], src[:, 0:h, :]), (dst[:, h:n, :], src[:, h:n, :])]

        def row_block_at(slot, w, r0, n):
            dst = ring[slot][:, 0:n * D].rearrange("p (k n) -> p k n", k=n)
            src = w[bass.ds(r0, n * P), :].rearrange("(k p) n -> p k n", p=P)
            h = n // 2
            return [(dst[:, 0:h, :], src[:, 0:h, :]), (dst[:, h:n, :], src[:, h:n, :])]

        def gate_up(slot, w, f0, width):
            dst = ring[slot][:, :].rearrange("p (k n) -> p k n", k=8)
            gate = w[:, bass.ds(f0, 256)].rearrange("(k p) n -> p k n", p=P)
            up = w[:, bass.ds(f0 + width, 256)].rearrange("(k p) n -> p k n", p=P)
            return [(dst[:, :, 0:256], gate), (dst[:, :, 256:512], up)]

        def load(name, s, halves, it=0, after=None):
            n = plan.slab0[name] + s
            if n >= NSLOT:
                sp.wait_ge(products_done, (plan.slab_end[n - NSLOT] if after is None else after))
            for dst, src in halves:
                sp.dma_start(dst, src).then_inc(slab_loaded[n % NSLOT], 16)

        def slot(name, s):
            return (plan.slab0[name] + s) % NSLOT

        def dense(name, w, n_slabs, c0=0):
            for s in range(n_slabs):
                load(name, s, two_halves(slot(name, s), k_rows(w, c0 + 512 * s, 512), 512))

        def loop(name, slab):
            body = plan.slab0_body[name]
            for s in range(body):
                load(name, s, slab(s, 0))
            with sp.Fori(1, plan.times[name]) as it:
                for s in range(body):
                    n = plan.slab0[name] + body + s
                    load(name, s, slab(s, it), after=plan.slab_end[n - NSLOT] + (it - 1) * len(plan.kinds[name]))

        dense("ada", dram("w_ada"), 12)
        w_in = dram("w_in")
        dense("uf", w_in, 1)
        dense("vbc", w_in, 6, 512)
        dense("gates", w_in, 4, 512 + 3 * D)
        load("fourier_out", 0, row_block(slot("fourier_out", 0), dram("w_fourier"), 0, 4))
        dense("conv_out", dram("w_conv_out"), 2)
        dense("w_o", dram("w_o"), 2)

        w_gate_e, w_up_e, w_down_e = dram("w_gate_e"), dram("w_up_e"), dram("w_down_e")

        def expert_slab(s, e):
            sl = slot("experts", s)
            if s < 8:
                w = w_gate_e if s < 4 else w_up_e
                dst = ring[sl][:, :].rearrange("p (k n) -> p k n", k=2)
                src = w[bass.ds(e * D + (s % 4) * 256, 256), :].rearrange("(k p) n -> p k n", p=P)
                return [(dst[:, k:k + 1, :], src[:, k:k + 1, :]) for k in range(2)]
            return row_block_at(sl, w_down_e, e * DE + (s % 4) * 512, 4)

        loop("experts", expert_slab)

        w_in2 = dram("w_in_2")
        dense("lru_x", w_in2, 2, 0)
        dense("lru_gate", w_in2, 2, 1024)
        dense("q", w_in2, 2, 2048)
        sl = slot("lru_ri", 0)
        gate_w = [dram(n).rearrange("(b c) d -> c b d", c=P) for n in ("lru_wa_2", "lru_wx_2")]
        load("lru_ri", 0, [(ring[sl][:, i * D:(i + 1) * D].rearrange("p (b d) -> p b d", b=8), gate_w[i])
                           for i in range(2)])
        dense("kv", w_in2, 1, 3072)
        dense("qi", w_in2, 1, 3584)
        dense("gate_a", w_in2, 2, 4168)
        dense("gate_b", w_in2, 2, 5192)
        dense("lru_out", dram("w_lru_br_2"), 2)
        dense("attn_out", dram("w_attn_br_2"), 2)
        dense("w_out2", dram("w_out_2"), 2)

        def ffn_slab(name, w_up, w_down, width):
            def slab(s, it):
                if s < 2:
                    return gate_up(slot(name, s), w_up, it * 512 + s * 256, width)
                return row_block_at(slot(name, s), w_down, it * 512, 4)
            return slab

        loop("ffn2", ffn_slab("ffn2", dram("w_up_2"), dram("w_down_2"), F2))
        w_ple_gate, w_ple_proj = dram("w_ple_gate_2"), dram("w_ple_proj_2")
        dense("ple", w_ple_gate, 2)
        load("ple", 2, row_block(slot("ple", 2), w_ple_proj, 0, 2))

        def ffn3(n, w_gu, w_down):
            loop(f"ffn3_{n}", ffn_slab(f"ffn3_{n}", w_gu, w_down, F3))
            end = f"ffn3_{n}_end"
            load(end, 0, gate_up(slot(end, 0), w_gu, F3 - 256, F3))
            load(end, 1, row_block(slot(end, 1), w_down, F3 - 256, 2))

        gu1, dn1, gu2, dn2 = (dram(n) for n in ("ffn1_w_gu_3", "ffn1_w_down_3", "ffn2_w_gu_3", "ffn2_w_down_3"))
        ffn3(0, gu1[0:D, :], dn1[0:F3, :])
        w_nsa = dram("nsa_w_in_3")
        dense("nsa_q", w_nsa, 2)
        dense("nsa_kv0", w_nsa, 1, 1024)
        dense("nsa_kv12", w_nsa, 2, 1536)
        sl = slot("cmp_hid", 0)
        load("cmp_hid", 0, [(ring[sl][:, i * 2048:(i + 1) * 2048].rearrange("p (m h) -> p m h", m=16),
                             dram(n).rearrange("(m p) h -> p m h", p=P))
                            for i, n in enumerate(("nsa_ck_w1_3", "nsa_cv_w1_3"))])
        dense("nsa_out", dram("nsa_w_out_3"), 2)
        ffn3(1, gu2[0:D, :], dn2[0:F3, :])
        ffn3(2, gu1[D:2 * D, :], dn1[F3:2 * F3, :])
        w_swa = dram("swa_w_in_3")
        dense("swa_q", w_swa, 2)
        load("swa_kv", 0, two_halves(slot("swa_kv", 0), k_rows(w_swa, 1024, 256), 256))
        dense("swa_out", dram("swa_w_out_3"), 2)
        ffn3(3, gu2[D:2 * D, :], dn2[F3:2 * F3, :])
        sp.wait_ge(S["out_ready"], TT)
        sp.dma_start(out.rearrange("(t p) d -> p t d", p=P), xn[:, :, :]).then_inc(S["out_stored"], 16)
        sp.wait_ge(S["out_stored"], 16)

    @block.tensor
    def _(pe):
        mm = nc.tensor.matmul

        def open_bank(name, i, it=0):
            w = plan.work(name, i)
            if w >= 4:
                pe.wait_ge(bank_copied[w % 4], w // 4 + it * (plan.kinds[name].count("W") // 4))
            return bank[4 + w % 4]

        def slab(name, s, it=0):
            return loaded(pe, name, s, it)

        def split_slab(name, s, it=0):
            pe.wait_ge(S["low_ready"], split_number(name, s, it))
            low = twins[f"ring{(plan.slab0[name] + s) % NSLOT}"]
            areas = split_areas(name, s)

            def at(c, n):
                start, area = [a for a in areas if a[0] <= c][-1]
                return area[:, c - start:c - start + n], low[:, c:c + n]
            return at

        def mm3(out_, lhs, rhs, start, stop):
            mm(out_, lhs[0], rhs[0], start=start, stop=False, skip_group_check=True)
            mm(out_, lhs[0], rhs[1], start=False, stop=False, skip_group_check=True)
            return mm(out_, lhs[1], rhs[0], start=False, stop=stop, skip_group_check=True)

        def h_parts(k, at=0, n=T):
            return h_high[:, k, at:at + n], h_low[:, k, at:at + n]

        def batch(ins):
            ins.then_inc(products_done, 1)

        def all_copied(name, idx):
            for i in idx:
                copied(pe, name, i)

        def normT(k, name):
            pe.wait_ge(S["xn_ready"], TT * k)
            for g in range(4):
                b = open_bank(name, g)
                for c in range(2):
                    for t in range(TT):
                        dst = b[:, c * T + t * P:c * T + (t + 1) * P]
                        chunk = slice((2 * g + c) * P, (2 * g + c + 1) * P)
                        if name == "norm1":
                            last = nc.tensor.transpose(dst, xn[:, t, chunk], ident)
                        else:
                            last = mm(dst, x[:, t, chunk], diag[:, t, :], start=True, stop=True)
                batch(last)

        def feature_major(name, b0, s, src, n_k, n_f=4, stride=512, c0=0):
            w = slab(name, s)
            for g in range(n_f // 2):
                b = open_bank(name, b0 + g)
                for f in range(2):
                    for k in range(n_k):
                        at = k * stride + c0 + (2 * g + f) * P
                        last = mm(b[:, f * T:(f + 1) * T], w[:, at:at + P], src[:, k, :],
                                  start=(k == 0), stop=(k == n_k - 1))
                batch(last)

        def to_acc(name, s, src):
            w = slab(name, s)
            for t in range(TT):
                for k in range(DC):
                    last = mm(acc[t][s][:, :], src[:, k, t * P:(t + 1) * P], w[:, 512 * k:512 * k + 512],
                              start=(k == 0), stop=(k == DC - 1))
            batch(last)

        def clear_acc():
            for t in range(TT):
                for h in range(2):
                    mm(acc[t][h][:, :], zeros[:, 0:P], zeros[:, :], start=True, stop=False, skip_group_check=True)

        pe.wait_ge(inputs_loaded, N_INPUTS)
        pe.wait_ge(fills_done, N_FILLS)
        pe.wait_ge(S["c_pad_ready"], 1)
        for m in range(12):
            w = slab("ada", m)
            b = open_bank("ada", 2 * m)
            for k in range(DC):
                j = 32 * (k % 4)
                last = mm(b[j:j + 32, :], c_pad[:, k, :], w[:, 512 * k:512 * k + 512], start=(k < 4),
                          stop=(k >= 4), tile_position=(0, j), skip_group_check=True)
            batch(last)
            copied(pe, "ada", 2 * m)
            b = open_bank("ada", 2 * m + 1)
            if m // 2 in (2, 5):
                last = mm(b[:, :], ones[:, :], mod_part[m % 2][:, :], start=True, stop=True)
            else:
                for c in range(4):
                    last = mm(b[:, c:c + 1], mod_part[m % 2][:, c * P:(c + 1) * P], ones[:, 0:1],
                              start=True, stop=True)
            batch(last)
        normT(1, "norm0")
        all_copied("norm0", range(4))
        w = slab("uf", 0)
        for t in range(TT):
            b = open_bank("uf", t)
            for k in range(DC):
                last = mm(b[:, :], hT[:, k, t * P:(t + 1) * P], w[:, 512 * k:512 * k + 512],
                          start=(k == 0), stop=(k == DC - 1))
            batch(last)
        all_copied("uf", range(2))
        for g in range(4):
            b = open_bank("dft_a", g)
            for t in range(TT):
                last = mm(b[:, :], uf[:, t, g * P:(g + 1) * P], dft_seq[:, t, :], start=(t == 0), stop=(t == 1))
            batch(last)
        all_copied("dft_a", range(4))
        for i in range(2):
            b = open_bank("dft_b", i)
            for j in range(2):
                mm(b[:, j * T:(j + 1) * T], const("dft_cos"), dft_v[:, 2 * i + j, 0:T], start=True, stop=False)
                last = mm(b[:, j * T:(j + 1) * T], const("dft_sin"), dft_v[:, 2 * i + j, T:2 * T],
                          start=False, stop=True)
            batch(last)
        for s in range(6):
            feature_major("vbc", 2 * s, s, hT, DC)
        for s in range(4):
            feature_major("gates", 2 * s, s, hT, DC)
        all_copied("dft_b", range(2))
        feature_major("fourier_out", 0, 0, yT, 4, n_f=8, stride=D)
        pe.wait_ge(S["conv_ready"], 1)
        for s in range(2):
            feature_major("conv_out", 2 * s, s, f_bc, DC)
        pe.wait_ge(S["z_ready"], 4)
        for s in range(2):
            to_acc("w_o", s, f_z)
        normT(2, "norm1")
        all_copied("norm1", range(4))
        b = open_bank("router", 0)
        for t in range(TT):
            for k in range(DC):
                last = mm(b[:, t * NE:(t + 1) * NE], hT[:, k, t * P:(t + 1) * P], w_router[:, k, :],
                          start=(k == 0), stop=(k == DC - 1))
        batch(last)
        pe.wait_ge(S["prob_ready"], 1)
        b = open_bank("probsT", 0)
        for t in range(TT):
            last = nc.tensor.transpose(b[0:NE, t * P:(t + 1) * P], prob[:, t, :], ident)
        batch(last)
        pe.wait_ge(S["mask_ready"], 1)
        b = open_bank("maskT", 0)
        for t in range(TT):
            last = nc.tensor.transpose(b[:, t * NE:(t + 1) * NE], mask[:, t * P:(t + 1) * P], ident[0:NE, 0:NE])
        batch(last)
        copied(pe, "maskT", 0)
        b = open_bank("slots", 0)
        mm(b[:, 0:NE], const("tri"), maskT[:, 0, :], start=True, stop=True)
        mm(b[:, NE:2 * NE], ones[:, :], maskT[:, 0, :], start=True, stop=False)
        batch(mm(b[:, NE:2 * NE], const("tri"), maskT[:, 1, :], start=False, stop=True))
        pe.wait_ge(S["sel_prob_ready"], TT)
        for i in range(8):
            b = open_bank("scatterT", i)
            for j in range(2):
                for t in range(TT):
                    last = nc.tensor.transpose(b[:, j * T + t * P:j * T + (t + 1) * P],
                                               sel_prob[:, t, 2 * i + j, :, :].rearrange("p g s -> p (g s)"), ident)
            batch(last)
        for c in range(DC):
            b = open_bank("gather", c)
            for t in range(TT):
                last = mm(b[:, :], xn[:, t, c * P:(c + 1) * P], sel[:, t, :, :].rearrange("p e s -> p (e s)"),
                          start=(t == 0), stop=(t == 1))
            batch(last)
        clear_acc()
        with pe.Fori(0, NE) as e:
            for part in range(2):
                b = open_bank("experts", 4 * part + 3, e)
                if part == 0:
                    pe.wait_ge(S["expert_staged"], 2 * e + 1)
                for m in range(4):
                    w = slab("experts", 4 * part + m, e)
                    for kk in range(2):
                        k = 2 * m + kk
                        for j in range(4):
                            last = mm(b[32 * j:32 * j + 32, :], xe_now[:, k, :],
                                      w[:, kk * DE + 512 * j:kk * DE + 512 * j + 512], start=(k == 0),
                                      stop=(k == DC - 1), tile_position=(0, 32 * j), skip_group_check=True)
                    batch(last)
            copied(pe, "experts", 7, e)
            b = open_bank("experts", 8, e)
            for q in range(4):
                last = nc.tensor.transpose(b[:, q * P:(q + 1) * P], e_h[:, q * P:(q + 1) * P], ident)
            batch(last)
            copied(pe, "experts", 8, e)
            b = open_bank("experts", 12, e)
            for m in range(4):
                w = slab("experts", 8 + m, e)
                for q in range(4):
                    for half in range(2):
                        j = 32 * (2 * half + q % 2)
                        last = mm(b[j:j + 32, :], e_hT[:, q * P + 32 * m:q * P + 32 * m + 32],
                                  w[:, q * D + 512 * half:q * D + 512 * half + 512], start=(m == 0 and q < 2),
                                  stop=(m == 3 and q >= 2), tile_position=(0, j), skip_group_check=True)
                batch(last)
            copied(pe, "experts", 12, e)
            pe.wait_ge(S["expert_staged"], 2 * e + 2)
            for t in range(TT):
                for half in range(2):
                    last = mm(acc[t][half][:, :], scat_now[64 * half:64 * half + 64, t * P:(t + 1) * P],
                              e_y[64 * half:64 * half + 64, :], start=False, stop=False,
                              tile_position=(64 * half, 0), skip_group_check=True)
            batch(last)

        def close_acc(name):
            for t in range(TT):
                for h in range(2):
                    last = mm(acc[t][h][:, :], zeros[:, 0:P], zeros[:, :], start=False, stop=True,
                              skip_group_check=True)
            batch(last)

        close_acc("experts_end")
        normT(3, "norm2")
        all_copied("norm2", range(4))
        for s in range(2):
            feature_major("lru_x", 2 * s, s, hT, DC)
        for s in range(2):
            feature_major("lru_gate", 2 * s, s, hT, DC)
        for s in range(2):
            feature_major("q", 2 * s, s, hT, DC)
        pe.wait_ge(S["ua_ready"], 1)
        w = slab("lru_ri", 0)
        for i in range(8):
            b = open_bank("lru_ri", i)
            for j in range(2):
                n = 2 * (i % 4) + j
                at = (i // 4) * D + n * P
                last = mm(b[:, j * T:(j + 1) * T], w[:, at:at + P], l_ua[:, n, :], start=True, stop=True)
            batch(last)
        feature_major("kv", 0, 0, hT, DC, n_f=2)
        w = ring[plan.slab0["kv"] % NSLOT]
        b = open_bank("kv", 1)
        for t in range(TT):
            for k in range(DC):
                last = mm(b[:, t * T:(t + 1) * T], hT[:, k, t * P:(t + 1) * P], w[:, 512 * k + 256:512 * k + 512],
                          start=(k == 0), stop=(k == DC - 1))
        batch(last)
        feature_major("qi", 0, 0, hT, DC)
        b = open_bank("kiwi", 0)
        for d in range(2):
            for k in range(DC):
                last = mm(b[64 * d:64 * d + 64, 0:T], w_kiwi[:, k, 0:64], hT[:, k, :], start=(k == 0),
                          stop=(k == DC - 1), tile_position=(0, 64 * d), skip_group_check=True)
        batch(last)
        b = open_bank("kiwi", 1)
        for t in range(TT):
            for k in range(DC):
                last = mm(b[:, t * 8:(t + 1) * 8], hT[:, k, t * P:(t + 1) * P], w_kiwi[:, k, 64:72],
                          start=(k == 0), stop=(k == DC - 1))
        batch(last)
        all_copied("q", range(4))
        copied(pe, "kv", 0)
        for i in range(5):
            b = open_bank("qk_ms", i)
            src = sq2[:, 2 * i:2 * i + 2, :].rearrange("p c t -> p (c t)") if i < 4 else sqk[:, :]
            batch(mm(b[:, :], ones_mean[:, :], src, start=True, stop=True))
        pe.wait_ge(S["rel_ready"], 1)
        for h in range(8):
            b = open_bank("bias", h)
            batch(mm(b[:, :], rel_rep[:, h, :], const("buckets")[0:32, :], start=True, stop=True))
        for s in range(2):
            feature_major("gate_a", 2 * s, s, hT, DC)
        all_copied("qi", range(2))
        all_copied("kiwi", range(1))
        for t in range(TT):
            for m in range(4):
                b = open_bank("score", 4 * t + m)
                for d in range(2):
                    last = mm(b[:, d * T:(d + 1) * T], qi[:, m, t * P:(t + 1) * P], ki[:, d, :],
                              start=True, stop=True)
                batch(last)
        for s in range(2):
            feature_major("gate_b", 2 * s, s, hT, DC)
        pe.wait_ge(S["lru_ready"], 1)
        for s in range(2):
            feature_major("lru_out", 2 * s, s, l_ua, DC)
        pe.wait_ge(S["qk_ready"], 5)
        for t in range(TT):
            for m in range(4):
                b = open_bank("logits2", 4 * t + m)
                for d in range(2):
                    h = 2 * m + d
                    last = mm(b[:, d * T:(d + 1) * T], q2[:, h, t * P:(t + 1) * P], k2[:, h // 4, :],
                              start=True, stop=True)
                batch(last)
        pe.wait_ge(S["att_ready"], TT)

        def causal_blocks(b, p_of_t):
            nc.tensor.transpose(b[:, 0:P], p_of_t(0)[:, 0:P], ident)
            nc.tensor.transpose(b[:, P:2 * P], p_of_t(1)[:, 0:P], ident)
            return nc.tensor.transpose(b[:, 2 * P:3 * P], p_of_t(1)[:, P:2 * P], ident)

        for m in range(4):
            for d in range(2):
                b = open_bank("pv2", 3 * m + d)
                batch(causal_blocks(b, lambda t: att[t][:, 2 * m + d, :]))
            b = open_bank("pv2", 3 * m + 2)
            g = m // 2
            for d in range(2):
                copied(pe, "pv2", 3 * m + d)
                mm(b[:, d * T:(d + 1) * T], v2[:, 0, g * P:(g + 1) * P], pT2[d][:, 0:T], start=True, stop=False)
                last = mm(b[:, d * T + P:(d + 1) * T], v2[:, 1, g * P:(g + 1) * P], pT2[d][:, T:T + P],
                          start=False, stop=True)
            batch(last)
        all_copied("pv2", (2, 5, 8, 11))
        for s in range(2):
            feature_major("attn_out", 2 * s, s, o2, DC)
        pe.wait_ge(S["merged_ready"], 4)
        for s in range(2):
            to_acc("w_out2", s, merged)

        def gate_up_tile(name, i, w, j, it=0):
            b = open_bank(name, i, it)
            for part in range(2):
                for k in range(DC):
                    at = 512 * k + 256 * part + P * j
                    last = mm3(b[:, part * T:(part + 1) * T], w(at, P), h_parts(k), k == 0, k == DC - 1)
            batch(last)

        def down(name, n_f, w, it, stop, hids):
            for f in range(n_f):
                pe.wait_ge(S["hid_split"], hids + f + 1)
                for t in range(TT):
                    tile = slice(t * P, (t + 1) * P)
                    for h in range(2):
                        last = mm3(acc[t][h][:, :], (hid_high[:, f, tile], hid_low[:, f, tile]),
                                   w(f * D + 512 * h, 512), False, stop and f == n_f - 1)
            batch(last)

        def ffn(name, hids):
            clear_acc()
            with pe.Fori(0, plan.times[name]) as it:
                for s in range(2):
                    w = split_slab(name, s, it)
                    for j in range(2):
                        gate_up_tile(name, 2 * s + j, w, j, it)
                down(name, 4, split_slab(name, 2, it), it, False, hids + 4 * it)

        normT(4, "norm3")
        all_copied("norm3", range(4))
        ffn("ffn2", 0)
        close_acc("ffn2_end")
        normT(5, "norm4")
        all_copied("norm4", range(4))
        for h in range(2):
            w = split_slab("ple", h)
            for t in range(TT):
                b = open_bank("ple", 2 * h + t)
                for k in range(DC):
                    last = mm3(b[:, :], h_parts(k, t * P, P), w(512 * k, 512), k == 0, k == DC - 1)
                batch(last)
        w = slab("ple", 2)
        for h in range(2):
            for t in range(TT):
                b = open_bank("ple", 4 + 2 * h + t)
                for k in range(2):
                    last = mm(b[:, :], pT_in[:, k, t * P:(t + 1) * P], w[:, k * D + 512 * h:k * D + 512 * h + 512],
                              start=(k == 0), stop=(k == 1))
                batch(last)
        def ffn3(n, k):
            normT(k, f"ffnorm{n}")
            all_copied(f"ffnorm{n}", range(4))
            hids = hidden_tiles(n)
            ffn(f"ffn3_{n}", hids)
            end = f"ffn3_{n}_end"
            w = split_slab(end, 0)
            for j in range(2):
                gate_up_tile(end, j, w, j)
            down(end, 2, split_slab(end, 1), 0, True, hids + 4 * plan.times[f"ffn3_{n}"])

        def rope(name, i, src):
            b = open_bank(name, i)
            batch(mm(b[:, 0:src.shape[1]], const("rope_rot"), src, start=True, stop=True))

        def pairs(a, i, n=2):
            return a[:, 2 * i:2 * i + n, :].rearrange("p c t -> p (c t)")

        ffn3(0, 6)
        normT(7, "nsa_norm")
        all_copied("nsa_norm", range(4))
        for s in range(2):
            feature_major("nsa_q", 2 * s, s, hT, DC)
        feature_major("nsa_kv0", 0, 0, hT, DC)
        for s in range(2):
            feature_major("nsa_kv12", 2 * s, s, hT, DC, n_f=2)
            w = ring[(plan.slab0["nsa_kv12"] + s) % NSLOT]
            b = open_bank("nsa_kv12", 2 * s + 1)
            for t in range(TT):
                for k in range(DC):
                    last = mm(b[:, t * T:(t + 1) * T], hT[:, k, t * P:(t + 1) * P],
                              w[:, 512 * k + 256:512 * k + 512], start=(k == 0), stop=(k == DC - 1))
            batch(last)
        b = open_bank("nsa_g", 0)
        for t in range(TT):
            for k in range(DC):
                last = mm(b[:, t * 48:(t + 1) * 48], hT[:, k, t * P:(t + 1) * P], w_nsa_gate[:, k, :],
                          start=(k == 0), stop=(k == DC - 1))
        batch(last)
        all_copied("nsa_q", range(4))
        all_copied("nsa_kv0", range(2))
        all_copied("nsa_kv12", range(4))
        for i in range(7):
            rope("nsa_rope", i, pairs(q3, i) if i < 4 else pairs(kraw, i - 4))
        pe.wait_ge(S["cmp_x_ready"], 1)
        w = slab("cmp_hid", 0)
        for i in range(2):
            b = open_bank("cmp_hid", i)
            for m in range(16):
                at = i * 2048 + m * P
                last = mm(b[:, 0:60], w[:, at:at + P], xb[i][:, m, :, :].rearrange("p g b -> p (g b)"),
                          start=(m == 0), stop=(m == 15))
            batch(last)
        all_copied("cmp_hid", range(2))
        b = open_bank("cmp_kv", 0)
        for d in range(2):
            last = mm(b[64 * d:64 * d + 64, 0:60], ck_w2[:, :], hid_c[0], start=True, stop=True,
                      tile_position=(0, 64 * d), skip_group_check=True)
        batch(last)
        b = open_bank("cmp_kv", 1)
        for g in range(4):
            last = mm(b[0:NB, g * 64:(g + 1) * 64], hid_c[1][:, g * NB:(g + 1) * NB], cv_w2[:, :],
                      start=True, stop=True)
        batch(last)
        all_copied("cmp_kv", range(2))
        pe.wait_ge(S["rope_ready"], 7)
        for t in range(TT):
            b = open_bank("cmp_s", t)
            for h in range(16):
                d, m = h % 2, h // 2
                last = mm(b[:, h * NB:(h + 1) * NB], q3[:, m, t * P:(t + 1) * P], kc[:, d, m // 2, :],
                          start=True, stop=True)
            batch(last)

        def masked_scores(b, m, t, keys, neg):
            for d in range(2):
                mm(b[:, d * T:(d + 1) * T], q3[:, m, t * P:(t + 1) * P], keys[:, d, :], start=True, stop=False)
                last = mm(b[:, d * T:(d + 1) * T], ident16[:, :], neg[:, t, :], start=False, stop=True)
            batch(last)

        def nsa_scores(m):
            for br in range(2):
                for t in range(TT):
                    s = 2 * br + t
                    if m:
                        pe.wait_ge(S["exp3_done"], 4 * (m - 1) + s + 1)
                    masked_scores(bank[s], m, t, kd[br][:, m // 2, :, :], causal16)

        pe.wait_ge(S["cmp_ready"], 1)
        pe.wait_ge(S["masks16_ready"], 2)
        nsa_scores(0)
        for m in range(8):
            g = m // 2
            n = pair_rest(m, 4, 6)
            if m < 7:
                nsa_scores(m + 1)
            for br in range(2):
                pe.wait_ge(S["p3_ready"], 4 * m + 2 * br + 2)
                for d in range(2):
                    b = open_bank("nsa_heads", n + 2 * br + d)
                    batch(causal_blocks(b, lambda t: p3[4 * (m % 2) + 2 * br + t][:, d, :]))
            b = open_bank("nsa_heads", n + 4)
            for d in range(2):
                for t in range(TT):
                    last = nc.tensor.transpose(b[0:NB, d * T + t * P:d * T + (t + 1) * P], pc[:, t, 2 * m + d, :],
                                               ident)
            batch(last)
            b = open_bank("nsa_heads", n + 5)
            for i in range(5):
                copied(pe, "nsa_heads", n + i)
            for d in range(2):
                o = b[64 * d:64 * d + 64, 0:T]
                o_late = b[64 * d:64 * d + 64, P:T]
                k = dict(tile_position=(0, 64 * d), skip_group_check=True)
                mm(o, vc[:, g * 64:(g + 1) * 64], pcT[:, d * T:(d + 1) * T], start=True, stop=False, **k)
                for br in range(2):
                    pt = pT3[2 * br + d]
                    mm(o, v3[:, br, 0, g * 64:(g + 1) * 64], pt[:, 0:T], start=False, stop=False, **k)
                    last = mm(o_late, v3[:, br, 1, g * 64:(g + 1) * 64], pt[:, T:T + P], start=False,
                              stop=(br == 1), **k)
            batch(last)
        for m in range(8):
            copied(pe, "nsa_heads", pair_rest(m, 4, 6) + 5)
        for s in range(2):
            to_acc("nsa_out", s, o3)
        ffn3(1, 8)
        ffn3(2, 9)
        normT(10, "swa_norm")
        all_copied("swa_norm", range(4))
        for s in range(2):
            feature_major("swa_q", 2 * s, s, hT, DC)
        w = slab("swa_kv", 0)
        b = open_bank("swa_kv", 0)
        for k in range(DC):
            mm(b[:, 0:T], w[:, 256 * k:256 * k + P], hT[:, k, :], start=(k == 0), stop=(k == DC - 1))
        for t in range(TT):
            for k in range(DC):
                last = mm(b[:, T + t * P:T + (t + 1) * P], hT[:, k, t * P:(t + 1) * P],
                          w[:, 256 * k + P:256 * k + 2 * P], start=(k == 0), stop=(k == DC - 1))
        batch(last)
        all_copied("swa_q", range(4))
        copied(pe, "swa_kv", 0)
        for i in range(5):
            rope("swa_rope", i, pairs(q3, i) if i < 4 else k4)
        pe.wait_ge(S["rope_ready"], 12)
        def swa_scores(m):
            for t in range(TT):
                if m >= 2:
                    pe.wait_ge(S["exp3_done"], 32 + 2 * (m - 2) + t + 1)
                masked_scores(bank[2 * (m % 2) + t], m, t, kd4[:, m // 4, :, :], window16)

        swa_scores(0)
        for m in range(8):
            n, g = pair_rest(m, 2, 3), m // 4
            if m < 7:
                swa_scores(m + 1)
            pe.wait_ge(S["p3_ready"], 32 + 2 * m + 2)
            for d in range(2):
                b = open_bank("swa_heads", n + d)
                batch(causal_blocks(b, lambda t: p3[2 * (m % 2) + t][:, d, :]))
            b = open_bank("swa_heads", n + 2)
            for d in range(2):
                copied(pe, "swa_heads", n + d)
                k = dict(tile_position=(0, 64 * d), skip_group_check=True)
                pt = pT3[d]
                mm(b[64 * d:64 * d + 64, 0:T], v4[:, 0, g * 64:(g + 1) * 64], pt[:, 0:T], start=True, stop=False, **k)
                last = mm(b[64 * d:64 * d + 64, P:T], v4[:, 1, g * 64:(g + 1) * 64], pt[:, T:T + P],
                          start=False, stop=True, **k)
            batch(last)
        for m in range(8):
            copied(pe, "swa_heads", pair_rest(m, 2, 3) + 2)
        for s in range(2):
            to_acc("swa_out", s, o3)
        ffn3(3, 11)

    @block.scalar
    def _(act):
        run = nc.scalar.activation
        link = Chain(act, "act")

        def copy_out(name, i, dst, n=512, scale=1.0, rows_=P, it=0):
            filled(act, name, i, it)
            frees(run(dst, work_bank(name, i)[0:rows_, 0:n], ACT.Copy, scale=scale), name, i)

        def squares(k):
            for t in range(TT):
                if k:
                    act.wait_ge(S["x_new"], TT * (k - 1) + t + 1)
                run(junk[:, t, :], x[:, t, :], ACT.Square, accum_out=ss[:, t:t + 1]).then_inc(S["squares_done"], 1)

        def high(name, s, it=0):
            w = loaded(act, name, s, it)
            for at, area in split_areas(name, s):
                ins = run(area[:, :], w[:, at:at + area.shape[1]], ACT.Copy)
            ins.then_inc(S["high_ready"], 1)

        def norm_out_split(name, gain):
            for g in range(4):
                filled(act, name, g)
                for c in range(2):
                    k = 2 * g + c
                    ins = run(h_high[:, k, :], work_bank(name, g)[:, c * T:(c + 1) * T], ACT.Identity,
                              scale=gain[:, k:k + 1])
                ins.then_inc(S["high_norm"], 1)

        def norm_out(name, gain, shift=None):
            for g in range(4):
                filled(act, name, g)
                for c in range(2):
                    k = 2 * g + c
                    args = {} if shift is None else {"bias": shift[:, k:k + 1]}
                    ins = run(hT[:, k, :], work_bank(name, g)[:, c * T:(c + 1) * T], ACT.Identity,
                              scale=gain[:, k:k + 1], **args)
                frees(ins, name, g)

        def two(name, i, fn):
            filled(act, name, i)
            for f in range(2):
                ins = fn(f, work_bank(name, i)[:, f * T:(f + 1) * T])
            frees(ins, name, i)

        act.wait_ge(inputs_loaded, N_INPUTS)
        act.wait_ge(fills_done, N_FILLS)
        squares(0)
        run(c_act, col("c", 0, 8), ACT.Silu).then_inc(S["c_act_ready"], 1)
        for m in range(12):
            copy_out("ada", 2 * m, mod_part[m % 2][:, :])
        act.wait_ge(S["mod_ready"], 2)
        norm_out("norm0", g_mix, modc[:, 0:8])
        for t in range(TT):
            copy_out("uf", t, uf[:, t, :])
        for g in range(4):
            copy_out("dft_a", g, dft_v[:, g, :])
        for i in range(2):
            copy_out("dft_b", i, yT[:, 2 * i:2 * i + 2, :].rearrange("p g t -> p (g t)"))
        for i in range(8):
            dst = (f_v, f_b)[i // 4][:, 2 * (i % 4):2 * (i % 4) + 2, :]
            copy_out("vbc", i, dst.rearrange("p g t -> p (g t)"))
        for i in range(8):
            dst = (f_ga, f_gb)[i // 4]
            two("gates", i, lambda f, b: run(dst[:, 2 * (i % 4) + f, :], b, ACT.Sigmoid,
                                             bias=col("b_gate", 2 * i + f)))
        squares(1)
        norm_out("norm1", g_moe, modc[:, 24:32])
        act.wait_ge(S["logit_ready"], 1)
        run(logit[:, :, :], logit[:, :, :], ACT.Exp).then_inc(S["exp_ready"], 1)
        for i in range(8):
            copy_out("scatterT", i, scat[:, 2 * i:2 * i + 2, :].rearrange("p e t -> p (e t)"))
        for c in range(DC):
            filled(act, "gather", c)
            frees(run(xeT[:, c, :], work_bank("gather", c)[:, :], ACT.Identity, scale=g_moe[:, c:c + 1],
                      bias=modc[:, 24 + c:25 + c]), "gather", c)
        with act.Fori(0, NE) as e:
            filled(act, "experts", 3, e)
            frees(run(e_act, work_bank("experts", 3)[:, :], ACT.Silu), "experts", 3)
            copy_out("experts", 8, e_hT, it=e)
            copy_out("experts", 12, e_y, it=e)
        squares(2)
        squares(3)
        norm_out("norm2", col("mix_norm_2", 0, 8))
        act.wait_ge(S["lam_exp_in"], 1)
        run(sp_a, sp_a, ACT.Exp).then_inc(S["lam_exp_out"], 1)
        for i in range(4):
            copy_out("lru_x", i, l_t[:, 2 * i:2 * i + 2, :].rearrange("p g t -> p (g t)"))
        for i in range(4):
            copy = l_g[:, 2 * i:2 * i + 2, :].rearrange("p g t -> p (g t)")
            filled(act, "lru_gate", i)
            frees(run(copy, work_bank("lru_gate", i)[:, :], ACT.Gelu_apprx_tanh), "lru_gate", i)
        for i in range(4):
            filled(act, "q", i)
            run(q2[:, 2 * i:2 * i + 2, :].rearrange("p g t -> p (g t)"), work_bank("q", i)[:, :], ACT.Copy)
            frees(run(sq2[:, 2 * i:2 * i + 2, :].rearrange("p g t -> p (g t)"), work_bank("q", i)[:, :],
                      ACT.Square), "q", i)
        for i in range(8):
            dst, bias = ((l_a, "lru_ba_2"), (l_i, "lru_bx_2"))[i // 4]
            two("lru_ri", i, lambda f, b: run(dst[:, 2 * (i % 4) + f, :], b, ACT.Sigmoid,
                                              bias=col(bias, 2 * (i % 4) + f)))
        for i in range(4):
            copied(act, "lru_ri", i)
        act.wait_ge(S["sp_ready"], 1)
        for c in range(DC):
            ins = run(l_t[:, c, :], l_a[:, c, :], ACT.Tanh, scale=sp8[:, c:c + 1])
        ins.then_inc(S["tanh_done"], 1)
        for c in range(DC):
            ins = run(l_a[:, c, :], l_a[:, c, :], ACT.Exp, scale=nsp8[:, c:c + 1])
        ins.then_inc(S["decay_done"], 1)
        act.wait_ge(S["mult_in"], 1)
        run(l_t[:, :, :], l_t[:, :, :], ACT.Sqrt, scale=2.0).then_inc(S["mult_out"], 1)
        filled(act, "kv", 0)
        run(k2[:, :, :].rearrange("p g t -> p (g t)"), work_bank("kv", 0)[:, :], ACT.Copy)
        frees(run(sqk[:, :], work_bank("kv", 0)[:, :], ACT.Square), "kv", 0)
        copy_out("kv", 1, v2[:, :, :].rearrange("p t n -> p (t n)"))
        for i in range(2):
            copy_out("qi", i, qi[:, 2 * i:2 * i + 2, :].rearrange("p g t -> p (g t)"))
        filled(act, "kiwi", 0)
        act.wait_ge(S["zeroed"], 1)
        for d in range(2):
            half = slice(64 * d, 64 * d + 64)
            ins = run(ki[half, d, :], work_bank("kiwi", 0)[half, 0:T], ACT.Copy)
        frees(ins, "kiwi", 0)
        copy_out("kiwi", 1, wi[:, :, :].rearrange("p t h -> p (t h)"), n=16, scale=8 ** -0.5)
        for i in range(5):
            act.wait_ge(S["msq_ready"], i + 1)
            run(msq[i % 2][:, :], msq[i % 2][:, :], ACT.Sqrt).then_inc(S["rsq_ready"], 1)
        for h in range(8):
            copy_out("bias", h, bias_row[:, h, :])
        for i in range(4):
            filled(act, "gate_a", i)
            frees(run(l_tmp[:, 2 * i:2 * i + 2, :].rearrange("p g t -> p (g t)"), work_bank("gate_a", i)[:, :],
                      ACT.Sigmoid), "gate_a", i)
        for i in range(8):
            filled(act, "score", i)
            if i >= 2:
                act.wait_ge(S["relu_used"], i - 1)
            else:
                filled(act, "qk_ms", 3)
            frees(run(relu_s[i % 2], work_bank("score", i)[:, :], ACT.Relu, scale=64 ** -0.5), "score", i)
        act.wait_ge(S["scan_done"], 1)
        for i in range(4):
            filled(act, "gate_b", i)
            frees(run(l_i[:, 2 * i:2 * i + 2, :].rearrange("p g t -> p (g t)"), work_bank("gate_b", i)[:, :],
                      ACT.Sigmoid), "gate_b", i)
        for t in range(TT):
            act.wait_ge(S["att_in"], t + 1)
            for h in range(8):
                ins = run(att[t][:, h, :], att[t][:, h, :], ACT.Exp, bias=nm2[:, t, h:h + 1],
                          accum_out=rs2[:, t, h:h + 1])
            ins.then_inc(S["att_exp"], 1)
        for m in range(4):
            for d in range(2):
                copy_out("pv2", 3 * m + d, pT2[d][:, 0:384], n=384)
            copy_out("pv2", 3 * m + 2, o2[:, 2 * m:2 * m + 2, :].rearrange("p g t -> p (g t)"))
        filled(act, "attn_out", 3)
        high("ffn2", 0)
        squares(4)
        norm_out_split("norm3", col("ffn_norm_2", 0, 8))
        with act.Fori(0, plan.times["ffn2"]) as it:
            for b in range(4):
                if b % 2 == 0:
                    high("ffn2", 1 + b // 2, it)
                act.wait_ge(S["conv_in"], b + 1 + 4 * it)
                run(f_act[b % 2], f_conv[b % 2], ACT.Gelu_apprx_tanh).then_inc(S["gelu_done"], 1)
            high("ffn2", 0, it + 1)
        high("ple", 1)
        squares(5)
        norm_out_split("norm4", col("ple_norm_2", 0, 8))
        for i in range(4):
            filled(act, "ple", i)
            frees(run(p_gate[:, i // 2, i % 2, :], work_bank("ple", i)[:, :], ACT.Sigmoid), "ple", i)

        def ffn3(n, k, before, i):
            filled(act, before, i)
            high(f"ffn3_{n}", 0)
            squares(k)
            norm_out_split(f"ffnorm{n}", col("ffn1_norm_3" if n % 2 == 0 else "ffn2_norm_3", 8 * (n // 2), 8))
            name = f"ffn3_{n}"

            def gates(name, n_b, it, before, before_it):
                for b in range(n_b):
                    if b % 2 == 0:
                        high(name, 1 + b // 2, it)
                    filled(act, name, b, it)
                    if b < 2:
                        copied(act, before, b + 2, before_it)
                    else:
                        copied(act, name, b - 2, it)
                    run(f_act[b % 2], work_bank(name, b)[:, 0:T], ACT.Silu).then_inc(S["gelu_done"], 1)

            with act.Fori(0, plan.times[name]) as it:
                gates(name, 4, it, name, it - 1)
                high(name, 0, it + 1)
            gates(name + "_end", 2, 0, name, plan.times[name] - 1)

        ffn3(0, 6, "ple", 1)
        squares(7)
        norm_out("nsa_norm", col("mix_norm_3", 0, 8))
        for i in range(4):
            copy_out("nsa_q", i, q3[:, 2 * i:2 * i + 2, :].rearrange("p g t -> p (g t)"))
        copy_out("nsa_kv0", 0, kraw[:, 0:2, :].rearrange("p g t -> p (g t)"))
        copy_out("nsa_kv0", 1, vraw[:, :, :].rearrange("p g t -> p (g t)"))
        for b in range(2):
            copy_out("nsa_kv12", 2 * b, kraw[:, 2 + 2 * b:4 + 2 * b, :].rearrange("p g t -> p (g t)"))
            copy_out("nsa_kv12", 2 * b + 1, v3[:, b, :, :].rearrange("p t n -> p (t n)"))
        filled(act, "nsa_g", 0)
        frees(run(gate3[:, :, :, :].rearrange("p t b h -> p (t b h)"), work_bank("nsa_g", 0)[:, 0:96], ACT.Sigmoid),
              "nsa_g", 0)
        for i in range(2):
            filled(act, "cmp_hid", i)
            frees(run(hid_c[i], work_bank("cmp_hid", i)[:, 0:60], ACT.Gelu_apprx_tanh), "cmp_hid", i)
        filled(act, "cmp_kv", 0)
        act.wait_ge(S["zeroed"], 2)
        for d in range(2):
            half = slice(64 * d, 64 * d + 64)
            ins = run(kc[half, d, :, :].rearrange("p g b -> p (g b)"), work_bank("cmp_kv", 0)[half, 0:60], ACT.Copy)
        frees(ins, "cmp_kv", 0)
        copy_out("cmp_kv", 1, vc, n=T, rows_=NB)
        act.wait_ge(S["cmp_in"], 1)
        run(pc[:, :, :, :], pc[:, :, :, :], ACT.Exp).then_inc(S["cmp_exp"], 1)

        def exps(b, slot, n):
            act.wait_ge(S["max3_ready"], n)
            for d in range(2):
                ins = run(p3[slot][:, d, :], b[:, d * T:(d + 1) * T], ACT.Exp,
                          scale=64 ** -0.5, bias=nm3[slot][:, d:d + 1], accum_out=rs3[slot][:, d:d + 1])
            ins.then_inc(S["exp3_done"], 1)

        for s in range(4):
            exps(bank[s], s, s + 1)
        for m in range(8):
            n = pair_rest(m, 4, 6)
            for s in range(4):
                copy_out("nsa_heads", n + s, pT3[s][:, :], n=384)
            copy_out("nsa_heads", n + 4, pcT, rows_=NB)
            if m < 7:
                for s in range(4):
                    exps(bank[s], 4 * ((m + 1) % 2) + s, 4 * (m + 1) + s + 1)
            copy_out("nsa_heads", n + 5, o3[:, m, :], n=T)
        ffn3(1, 8, "nsa_heads", pair_rest(7, 4, 6) + 5)
        ffn3(2, 9, "ffn3_1_end", 1)
        squares(10)
        norm_out("swa_norm", col("mix_norm_3", 8, 8))
        for i in range(4):
            copy_out("swa_q", i, q3[:, 2 * i:2 * i + 2, :].rearrange("p g t -> p (g t)"))
        filled(act, "swa_kv", 0)
        run(k4, work_bank("swa_kv", 0)[:, 0:T], ACT.Copy)
        frees(run(v4[:, :, :].rearrange("p t n -> p (t n)"), work_bank("swa_kv", 0)[:, T:2 * T], ACT.Copy),
              "swa_kv", 0)
        def swa_exps(m):
            for t in range(TT):
                slot = 2 * (m % 2) + t
                n = 32 + 2 * m + t + 1
                act.wait_ge(S["max3_ready"], n)
                run(sk[slot], sk[slot], ACT.Exp).then_inc(S["sink_exp"], 1)
                exps(bank[slot], slot, n)

        swa_exps(0)
        for m in range(8):
            n = pair_rest(m, 2, 3)
            for d in range(2):
                copy_out("swa_heads", n + d, pT3[d][:, :], n=384)
            if m < 7:
                swa_exps(m + 1)
            copy_out("swa_heads", n + 2, o3[:, m, :], n=T)
        ffn3(3, 11, "swa_heads", pair_rest(7, 2, 3) + 2)
        squares(12)

    @block.gpsimd
    def _(pool):
        loads = [(consts[:, :], dram("consts")), (cols[:, :], dram("cols")),
                 (masks_in, dram("masks")), (x[:, :, :], dram("x").rearrange("(t p) d -> p t d", p=P)),
                 (rows[:, :], wide(dram("rows"), 0, P)),
                 (w_router[:, :, :], dram("w_router").rearrange("(k p) n -> p k n", p=P)),
                 (w_kiwi[:, :, :], dram("w_in_2")[:, 4096:4168].rearrange("(k p) n -> p k n", p=P)),
                 (w_nsa_gate[:, :, :], dram("nsa_w_in_3")[:, 2560:2608].rearrange("(k p) n -> p k n", p=P)),
                 (ck_w2[:, :], dram("nsa_ck_w2_3")), (cv_w2[:, :], dram("nsa_cv_w2_3")),
                 (pT_in[:, :, :], dram("pT").rearrange("(k p) t -> p k t", p=P)),
                 (rel_in[:, :], dram("rel_bias_2"))]
        assert 16 * len(loads) == N_INPUTS
        for dst, src in loads:
            pool.dma_start(dst, src).then_inc(inputs_loaded, 16)
        fills = [(ones[:, :], 1.0), (ones_mean[:, :], 1.0 / P), (zeros[:, :], 0.0), (neg_half[:, :], -0.5),
                 (c_pad[:, :, :], 0.0)]
        assert len(fills) == N_FILLS
        for dst, v in fills:
            nc.gpsimd.memset(dst, v).then_inc(fills_done, 1)
        pool.wait_ge(fills_done, N_FILLS)

        def rsqrt(k):
            pool.wait_ge(S["mean_ready"], k + 1)
            nc.gpsimd.tensor_tensor(out=rstd, in0=ms, in1=neg_half[:, 0:TT], op=ALU.pow).then_inc(S["rstd_ready"], 1)

        rsqrt(0)
        rsqrt(1)
        for c in range(DC):
            copied(pool, "gather", c)
        for i in range(8):
            copied(pool, "scatterT", i)
        with pool.Fori(0, NE) as e:
            body = len(plan.kinds["experts"])
            pool.wait_ge(products_done, plan.done("experts", 7) - body + e * body)
            nc.gpsimd.tensor_copy(xe_now[:, :, :], xeT[:, :, bass.ds(e * CAP, CAP)]).then_inc(S["expert_staged"], 1)
            pool.wait_ge(products_done, plan.batch0["experts"] + e * body)
            nc.gpsimd.tensor_copy(scat_now, AC[:, bass.ds(e * T, T)]).then_inc(S["expert_staged"], 1)
        rsqrt(2)
        rsqrt(3)
        for h in range(8):
            copied(pool, "bias", h)
        pool.dma_start(skew.rearrange("(p n) -> p n", p=P), bias_row[:, :, :].rearrange("p h j -> p (h j)"))\
            .then_inc(S["rows_out"], 16)
        pool.wait_ge(S["rows_out"], 16)
        for t in range(TT):
            src = bass.AP(tensor=skew.tensor, offset=T - 1 - P * t, ap=[[8 * 512 - 1, P], [512, 8], [1, T]])
            pool.dma_start(bias2[:, t, :, :], src).then_inc(S["bias_in"], 16)
        pool.wait_ge(S["x_new"], TT)
        pool.dma_start(row("gate_m"), wide(dram("final_norm"), 0, P)).then_inc(S["final_row_in"], 16)
        for k in range(4, len(NORMS)):
            rsqrt(k)

    @block.vector
    def _(dve):
        v = nc.vector
        link = Chain(dve, "dve")

        def mean(k):
            dve.wait_ge(S["squares_done"], TT * (k + 1))
            v.tensor_scalar(ms, ss, 1.0 / D, EPS, ALU.mult, ALU.add).then_inc(S["mean_ready"], 1)
            dve.wait_ge(S["rstd_ready"], k + 1)

        def normalise(k, rows=False):
            mean(k)
            for t in range(TT):
                dst, src = (xn, x[:, t, :]) if rows else (diag, ident)
                v.tensor_scalar(dst[:, t, :], src, rstd[:, t:t + 1], None, ALU.mult).then_inc(S["xn_ready"], 1)

        def low(name, s, it=0):
            dve.wait_ge(S["high_ready"], split_number(name, s, it))
            slot = (plan.slab0[name] + s) % NSLOT
            for at, area in split_areas(name, s):
                part = slice(at, at + area.shape[1])
                ins = v.tensor_tensor(twins[f"ring{slot}"][:, part], ring[slot][:, part], area[:, :].bitcast(fp32),
                                      ALU.subtract)
            ins.then_inc(S["low_ready"], 1)

        def low_norm(name, n, gain):
            for g in range(4):
                dve.wait_ge(S["high_norm"], 4 * (n - 1) + g + 1)
                for c in range(2):
                    k = 2 * g + c
                    ins = v.scalar_tensor_tensor(h_low[:, k, :], work_bank(name, g)[:, c * T:(c + 1) * T],
                                                 gain[:, k:k + 1], h_high[:, k, :].bitcast(fp32),
                                                 ALU.mult, ALU.subtract)
                frees(ins, name, g)

        def hidden(name, b, it):
            up, f_ = work_bank(name, b)[:, T:2 * T], f_act[b % 2]
            v.tensor_tensor(hid_high[:, b, :], up, f_, ALU.mult)
            frees(v.tensor_tensor(hid[:, b, :], up, f_, ALU.mult), name, b)
            copied(dve, name, b, it)
            v.tensor_tensor(hid_low[:, b, :], hid[:, b, :], hid_high[:, b, :].bitcast(fp32), ALU.subtract)\
                .then_inc(S["hid_split"], 1)

        def x_updated(ins):
            ins.then_inc(S["x_new"], 1)

        dve.wait_ge(inputs_loaded, N_INPUTS)
        dve.wait_ge(fills_done, N_FILLS)
        for dst, src in ((ident16[:, :], ident), (masks16[:, :, :].rearrange("p a s -> p (a s)"), masks_in)):
            v.tensor_copy(dst, src).then_inc(S["masks16_ready"], 1)
        dve.wait_ge(S["c_act_ready"], 1)
        v.tensor_copy(c_pad[:, :, 0:1], c_act[:, :].rearrange("p (k a) -> p k a", a=1)).then_inc(S["c_pad_ready"], 1)
        normalise(0)
        for m in range(12):
            i = 2 * m + 1
            filled(dve, "ada", i)
            b = work_bank("ada", i)
            if m // 2 in (2, 5):
                dst = row("gate_m" if m < 6 else "gate_f")[:, (m % 2) * 512:(m % 2) * 512 + 512]
                frees(v.tensor_tensor(dst, b[:, :], dst, ALU.add), "ada", i)
            else:
                frees(v.tensor_tensor(modc[:, 4 * m:4 * m + 4], b[:, 0:4], col("b_ada", 4 * m, 4), ALU.add), "ada", i)
        for m in range(12):
            copied(dve, "ada", 2 * m + 1)
        for dst, scale_at, g in ((g_mix, 8, "g_norm_mix"), (g_moe, 32, "g_norm_moe")):
            v.scalar_tensor_tensor(dst, modc[:, scale_at:scale_at + 8], 1.0, col(g, 0, 8), ALU.add, ALU.mult)\
                .then_inc(S["mod_ready"], 1)
        for i in range(4):
            filled(dve, "vbc", 8 + i)
            copied(dve, "vbc", i)
            frees(v.tensor_tensor(f_cv[:, 2 * i:2 * i + 2, :].rearrange("p c t -> p (c t)"),
                                  work_bank("vbc", 8 + i)[:, :],
                                  f_v[:, 2 * i:2 * i + 2, :].rearrange("p c t -> p (c t)"), ALU.mult), "vbc", 8 + i)
        for i in range(4):
            copied(dve, "vbc", 8 + i)
            copied(dve, "vbc", 4 + i)
        link(v.tensor_tensor(f_bc[:, :, :], f_cv[:, :, :],
                             wide(col("w_conv", DC, DC).rearrange("p (c a) -> p c a", a=1), 2, T), ALU.mult))
        for c in range(DC):
            ins = v.scalar_tensor_tensor(f_bc[:, c, 1:T], f_cv[:, c, 0:T - 1], col("w_conv", c), f_bc[:, c, 1:T],
                                         ALU.mult, ALU.add)
        link(ins)
        for c in range(DC):
            ins = v.scalar_tensor_tensor(f_bc[:, c, 0:T - 1], f_cv[:, c, 1:T], col("w_conv", 2 * DC + c),
                                         f_bc[:, c, 0:T - 1], ALU.mult, ALU.add)
        link(ins)
        v.tensor_tensor(f_bc[:, :, :], f_bc[:, :, :], f_b[:, :, :], ALU.mult).then_inc(S["conv_ready"], 1)
        for i in range(8):
            copied(dve, "gates", i)
        for i in range(4):
            filled(dve, "fourier_out", i)
            two = slice(2 * i, 2 * i + 2)
            frees(v.tensor_tensor(f_z[:, two, :].rearrange("p c t -> p (c t)"), work_bank("fourier_out", i)[:, :],
                                  f_ga[:, two, :].rearrange("p c t -> p (c t)"), ALU.mult), "fourier_out", i)
        for i in range(4):
            filled(dve, "conv_out", i)
            if i >= 2:
                dve.wait_ge(S["z_ready"], i - 1)
            two = slice(2 * i, 2 * i + 2)
            frees(v.tensor_tensor(tmp[i % 2][:, :], work_bank("conv_out", i)[:, :],
                                  f_gb[:, two, :].rearrange("p c t -> p (c t)"), ALU.mult), "conv_out", i)
            copied(dve, "conv_out", i)
            copied(dve, "fourier_out", i)
            z = f_z[:, two, :].rearrange("p c t -> p (c t)")
            v.tensor_tensor(z, z, tmp[i % 2][:, :], ALU.add).then_inc(S["z_ready"], 1)

        def add_acc(name, gate=None, scale=1.0, batches=(0, 1)):
            for h in range(2):
                filled(dve, name, batches[h])
                for t in range(TT):
                    xs = x[:, t, 512 * h:512 * h + 512]
                    if gate is not None:
                        link(v.tensor_tensor(tmp[t][:, :], acc[t][h][:, :], gate[:, 512 * h:512 * h + 512], ALU.mult))
                        ins = v.tensor_tensor(xs, xs, tmp[t][:, :], ALU.add)
                    else:
                        ins = v.scalar_tensor_tensor(xs, acc[t][h][:, :], scale, xs, ALU.mult, ALU.add)
                    if h == 1:
                        x_updated(ins)
                    elif gate is not None:
                        link(ins)

        add_acc("w_o", gate=row("gate_m"))
        dve.wait_ge(S["x_new"], TT * 1)
        normalise(1, rows=True)
        filled(dve, "router", 0)
        b = work_bank("router", 0)
        for t in range(TT):
            ins = v.tensor_tensor(logit[:, t, :], b[:, t * NE:(t + 1) * NE], row("b_router"), ALU.add)
        frees(ins, "router", 0)
        copied(dve, "router", 0)
        link(v.reduce_max(rmax, logit[:, :, :], AX.X))
        v.tensor_tensor(logit[:, :, :], logit[:, :, :], wide(rmax[:, :].rearrange("p (t a) -> p t a", a=1), 2, NE),
                        ALU.subtract).then_inc(S["logit_ready"], 1)
        dve.wait_ge(S["exp_ready"], 1)
        link(v.reduce_sum(rsum, logit[:, :, :], AX.X))
        link(v.reciprocal(rsum, rsum))
        v.tensor_tensor(prob[:, :, :], logit[:, :, :], wide(rsum[:, :].rearrange("p (t a) -> p t a", a=1), 2, NE),
                        ALU.mult).then_inc(S["prob_ready"], 1)
        filled(dve, "probsT", 0)
        frees(v.tensor_copy(probT, work_bank("probsT", 0)[0:NE, 0:T]), "probsT", 0)
        copied(dve, "probsT", 0)
        src = probT
        for r in range(CAP // 8):
            link(v.max(top8[0:NE, :], src))
            link(v.match_replace(probW, top8[0:NE, :], src, -1.0))
            src = probW
        v.tensor_scalar(mask, probW, 0.0, None, ALU.is_lt).then_inc(S["mask_ready"], 1)
        filled(dve, "maskT", 0)
        frees(v.tensor_copy(maskT[:, :, :].rearrange("p t e -> p (t e)"), work_bank("maskT", 0)[:, 0:2 * NE]),
              "maskT", 0)
        copied(dve, "maskT", 0)
        filled(dve, "slots", 0)
        frees(v.scalar_tensor_tensor(slot_of[:, :, :].rearrange("p t e -> p (t e)"),
                                     work_bank("slots", 0)[:, 0:2 * NE], 1.0,
                                     maskT[:, :, :].rearrange("p t e -> p (t e)"), ALU.add, ALU.mult), "slots", 0)
        copied(dve, "slots", 0)
        link(v.tensor_scalar(slot_of[:, :, :], slot_of[:, :, :], -1.0, None, ALU.add))
        for t in range(TT):
            link(v.tensor_tensor(sel[:, t, :, :], wide(const("iota", "p (a s) -> p a s", a=1), 1, NE),
                                 wide(slot_of[:, t, :].rearrange("p (e a) -> p e a", a=1), 2, CAP), ALU.is_equal))
        dve.wait_ge(S["prob_ready"], 1)
        for t in range(TT):
            for g in range(4):
                ins = v.tensor_tensor(sel_prob[:, t, :, g, :], sel[:, t, :, :],
                                      wide(prob[:, t, :].rearrange("p (e a) -> p e a", a=1), 2, CAP), ALU.mult)
            ins.then_inc(S["sel_prob_ready"], 1)
        with dve.Fori(0, NE) as e:
            filled(dve, "experts", 7, e)
            copied(dve, "experts", 3, e)
            frees(v.tensor_tensor(e_h, work_bank("experts", 7)[:, :], e_act, ALU.mult), "experts", 7)
        add_acc("experts_end", gate=row("gate_f"), batches=(0, 0))
        dve.wait_ge(S["x_new"], TT * 2)
        mean(2)
        x_updated(v.scalar_tensor_tensor(x[:, 0, :], x[:, 0, :], rstd[:, 0:1], row("g_final"), ALU.mult, ALU.mult))
        x_updated(v.scalar_tensor_tensor(x[:, 1, :], x[:, 1, :], rstd[:, 1:2], row("g_final"), ALU.mult, ALU.mult))
        dve.wait_ge(S["x_new"], TT * 3)
        lam = col("lru_lambda_2", 0, 8)
        link(v.tensor_scalar(sp_b, lam, -1.0, 0.0, ALU.mult, ALU.max))
        v.scalar_tensor_tensor(sp_a, sp_b, -2.0, lam, ALU.mult, ALU.subtract)\
            .then_inc(S["lam_exp_in"], 1)
        normalise(3)
        dve.wait_ge(S["lam_exp_out"], 1)
        link(v.tensor_scalar(nsp8, sp_a, 2.0, None, ALU.add))
        link(v.reciprocal(nsp8, nsp8))
        link(v.tensor_tensor(sp_a, sp_a, nsp8, ALU.mult))
        link(v.tensor_tensor(nsp8, sp_a, sp_a, ALU.mult))
        link(v.tensor_scalar(sp8, nsp8, 1.0 / 17, 1.0 / 15, ALU.mult, ALU.add))
        for n in range(13, 0, -2):
            link(v.tensor_tensor(sp8, sp8, nsp8, ALU.mult))
            link(v.tensor_scalar(sp8, sp8, 1.0 / n, None, ALU.add))
        link(v.tensor_tensor(sp8, sp8, sp_a, ALU.mult))
        link(v.scalar_tensor_tensor(sp8, sp8, 2.0, sp_b, ALU.mult, ALU.add))
        link(v.tensor_scalar(nsp8, sp8, -8.0, None, ALU.mult))
        v.tensor_scalar(sp8, sp8, 8.0, None, ALU.mult).then_inc(S["sp_ready"], 1)
        v.memset(ki[:, :, :], 0.0).then_inc(S["zeroed"], 1)
        filled(dve, "norm2", 3)
        for h in range(8):
            ins = v.tensor_copy(rel_rep[:, h, :], wide(rel_in[:, h:h + 1], 1, P))
        ins.then_inc(S["rel_ready"], 1)
        for i in range(4):
            copied(dve, "lru_x", i)
        for c in range(DC):
            ins = v.tensor_scalar(l_ua[:, c, :], l_t[:, c, :], col("lru_conv_w_2", 3 * DC + c),
                                  col("lru_conv_b_2", c), ALU.mult, ALU.add)
        for s in (1, 2, 3):
            link(ins)
            for c in range(DC):
                ins = v.scalar_tensor_tensor(l_ua[:, c, s:T], l_t[:, c, 0:T - s], col("lru_conv_w_2", (3 - s) * DC + c),
                                             l_ua[:, c, s:T], ALU.mult, ALU.add)
        ins.then_inc(S["ua_ready"], 1)
        dve.wait_ge(S["ua_ready"], 1)
        for i in range(4, 8):
            copied(dve, "lru_ri", i)
        link(v.tensor_tensor(l_i[:, :, :], l_i[:, :, :], l_ua[:, :, :], ALU.mult))
        dve.wait_ge(S["tanh_done"], 1)
        link(v.tensor_scalar(l_tmp[:, :, :], l_t[:, :, :], 1.0, None, ALU.add))
        link(v.reciprocal(l_tmp[:, :, :], l_tmp[:, :, :]))
        v.tensor_tensor(l_t[:, :, :], l_t[:, :, :], l_tmp[:, :, :], ALU.mult).then_inc(S["mult_in"], 1)
        dve.wait_ge(S["mult_out"], 1)
        link(v.tensor_tensor(l_i[:, :, :], l_i[:, :, :], l_t[:, :, :], ALU.mult))
        dve.wait_ge(S["decay_done"], 1)
        for c in range(DC):
            ins = v.tensor_tensor_scan(out=l_ua[:, c, :], data0=l_a[:, c, :], data1=l_i[:, c, :], initial=0.0,
                                       op0=ALU.mult, op1=ALU.add)
        ins.then_inc(S["scan_done"], 1)
        dve.wait_ge(S["scan_done"], 1)
        for i in range(4):
            copied(dve, "lru_gate", i)
        v.tensor_tensor(l_ua[:, :, :], l_ua[:, :, :], l_g[:, :, :], ALU.mult).then_inc(S["lru_ready"], 1)
        for i in range(5):
            a, r = (q2[:, 2 * i:2 * i + 2, :] if i < 4 else k2[:, :, :]).rearrange("p c t -> p (c t)"), msq[i % 2]
            filled(dve, "qk_ms", i)
            frees(v.tensor_scalar(r[:, :], work_bank("qk_ms", i)[:, :], EPS, None, ALU.add), "qk_ms", i)
            copied(dve, "qk_ms", i)
            v.reciprocal(r[:, :], r[:, :]).then_inc(S["msq_ready"], 1)
            dve.wait_ge(S["rsq_ready"], i + 1)
            v.scalar_tensor_tensor(a, a, col("q_norm_2" if i < 4 else "k_norm_2"), r[:, :], ALU.mult, ALU.mult)\
                .then_inc(S["qk_ready"], 1)
        copied(dve, "kiwi", 1)
        for t in range(TT):
            for m in range(4):
                copied(dve, "score", 4 * t + m)
                r = relu_s[m % 2]
                for d in range(2):
                    w = wi[:, t, 2 * m + d:2 * m + d + 1]
                    if m == 0 and d == 0:
                        link(v.tensor_scalar(score[:, t, :], r[:, 0:T], w, None, ALU.mult))
                    else:
                        ins = v.scalar_tensor_tensor(score[:, t, :], r[:, d * T:(d + 1) * T], w, score[:, t, :],
                                                     ALU.mult, ALU.add)
                        if d == 0:
                            link(ins)
                ins.then_inc(S["relu_used"], 1)
                dve.wait_ge(S["relu_used"], 4 * t + m + 1)
        link(v.tensor_tensor(score[:, :, :], score[:, :, :], causal16, ALU.add))
        for t in range(TT):
            src = score[:, t, :]
            for r in range(8):
                link(v.max(t8, src))
                link(v.match_replace(score_w[:, t, :], t8, src, -3e38))
                src = score_w[:, t, :]
        link(v.tensor_scalar(score_w[:, :, :], score_w[:, :, :], -2e38, NEG, ALU.is_gt, ALU.mult))
        link(v.tensor_tensor(score_w[:, :, :], score_w[:, :, :], causal16, ALU.add))
        for i in range(4):
            copied(dve, "gate_a", i)
            filled(dve, "lru_out", i)
            two = slice(2 * i, 2 * i + 2)
            frees(v.tensor_tensor(merged[:, two, :].rearrange("p c t -> p (c t)"), work_bank("lru_out", i)[:, :],
                                  l_tmp[:, two, :].rearrange("p c t -> p (c t)"), ALU.mult), "lru_out", i)
        dve.wait_ge(S["bias_in"], 16 * TT)
        for t in range(TT):
            for m in range(4):
                filled(dve, "logits2", 4 * t + m)
                frees(v.scalar_tensor_tensor(att[t][:, 2 * m:2 * m + 2, :].rearrange("p h s -> p (h s)"),
                                             work_bank("logits2", 4 * t + m)[:, :], P ** -0.5,
                                             bias2[:, t, 2 * m:2 * m + 2, :].rearrange("p h s -> p (h s)"),
                                             ALU.mult, ALU.add), "logits2", 4 * t + m)
            for m in range(4):
                copied(dve, "logits2", 4 * t + m)
            link(v.tensor_tensor(att[t][:, :, :], att[t][:, :, :],
                                 wide(score_w[:, t, :].rearrange("p (a s) -> p a s", a=1), 1, 8), ALU.add))
            v.tensor_reduce(nm2[:, t, :], att[t][:, :, :], AX.X, ALU.max, negate=True).then_inc(S["att_in"], 1)
        for t in range(TT):
            dve.wait_ge(S["att_exp"], t + 1)
            link(v.reciprocal(rs2[:, t, :], rs2[:, t, :]))
            v.tensor_tensor(att[t][:, :, :], att[t][:, :, :],
                            wide(rs2[:, t, :].rearrange("p (h a) -> p h a", a=1), 2, T), ALU.mult)\
                .then_inc(S["att_ready"], 1)
        for i in range(4):
            copied(dve, "gate_b", i)
            filled(dve, "attn_out", i)
            two = slice(2 * i, 2 * i + 2)
            frees(v.tensor_tensor(tmp[i % 2][:, :], work_bank("attn_out", i)[:, :],
                                  l_i[:, two, :].rearrange("p c t -> p (c t)"), ALU.mult), "attn_out", i)
            copied(dve, "attn_out", i)
            copied(dve, "lru_out", i)
            a = merged[:, two, :].rearrange("p c t -> p (c t)")
            v.tensor_tensor(a, a, tmp[i % 2][:, :], ALU.add).then_inc(S["merged_ready"], 1)
        low("ffn2", 0)
        add_acc("w_out2")
        dve.wait_ge(S["x_new"], TT * 4)
        normalise(4)
        low_norm("norm3", 1, col("ffn_norm_2", 0, 8))
        n_f = F2 // P
        c0 = col_at["ffn_conv_w_2"][0]
        cb = col_at["ffn_conv_b_2"][0]
        link2 = sem("conv_step")
        with dve.Fori(0, plan.times["ffn2"]) as it:
            for b in range(4):
                if b % 2 == 0:
                    low("ffn2", 1 + b // 2, it)
                filled(dve, "ffn2", b, it)
                g, fc = work_bank("ffn2", b), f_conv[b % 2]
                wc = lambda j: cols[:, bass.ds(c0 + j * n_f + b + 4 * it, 1)]
                v.tensor_scalar(fc, g[:, 0:T], wc(2), cols[:, bass.ds(cb + b + 4 * it, 1)], ALU.mult, ALU.add)\
                    .then_inc(link2, 1)
                dve.wait_ge(link2, 8 * it + 2 * b + 1)
                v.scalar_tensor_tensor(fc[:, 1:T], g[:, 0:T - 1], wc(1), fc[:, 1:T], ALU.mult, ALU.add)\
                    .then_inc(link2, 1)
                dve.wait_ge(link2, 8 * it + 2 * b + 2)
                v.scalar_tensor_tensor(fc[:, 2:T], g[:, 0:T - 2], wc(0), fc[:, 2:T], ALU.mult, ALU.add)\
                    .then_inc(S["conv_in"], 1)
                dve.wait_ge(S["gelu_done"], 4 * it + b + 1)
                hidden("ffn2", b, it)
            low("ffn2", 0, it + 1)
        low("ple", 1)
        add_acc("ffn2_end", batches=(0, 0))
        dve.wait_ge(S["x_new"], TT * 5)
        normalise(5)
        low_norm("norm4", 2, col("ple_norm_2", 0, 8))
        for i in range(4):
            h, t = i // 2, i % 2
            copied(dve, "ple", i)
            filled(dve, "ple", 4 + i)
            frees(v.tensor_tensor(tmp[i][:, :], work_bank("ple", 4 + i)[:, :], p_gate[:, h, t, :], ALU.mult),
                  "ple", 4 + i)
            copied(dve, "ple", 4 + i)
            xs = x[:, t, 512 * h:512 * h + 512]
            ins = v.tensor_tensor(xs, xs, tmp[i][:, :], ALU.add)
            if h == 1:
                x_updated(ins)
            else:
                link(ins)
        dve.wait_ge(S["x_new"], TT * 6)

        low("ffn3_0", 0)
        gelus = [4 * plan.times["ffn2"]]

        def ffn3(n, k):
            normalise(k)
            low_norm(f"ffnorm{n}", 3 + n, col("ffn1_norm_3" if n % 2 == 0 else "ffn2_norm_3", 8 * (n // 2), 8))
            name = f"ffn3_{n}"

            def tiles(name, n_b, base, it, per):
                for b in range(n_b):
                    if b % 2 == 0:
                        low(name, 1 + b // 2, it)
                    dve.wait_ge(S["gelu_done"], base + b + 1 + per * it)
                    hidden(name, b, it)

            with dve.Fori(0, plan.times[name]) as it:
                tiles(name, 4, gelus[0], it, 4)
                low(name, 0, it + 1)
            gelus[0] += 4 * plan.times[name]
            filled(dve, name, 4, plan.times[name] - 1)
            tiles(name + "_end", 2, gelus[0], 0, 0)
            gelus[0] += 2
            if n == 1:
                low("ffn3_2", 0)
            add_acc(name + "_end", scale=0.5, batches=(2, 2))

        def rope(name, i, a, n):
            k = (0 if name == "nsa_rope" else 7) + i
            filled(dve, name, i)
            sin = const("rope_sin", "p (a t) -> p a t", a=1)
            cos = const("rope_cos", "p (a t) -> p a t", a=1)
            if n > 1:
                sin, cos = wide(sin, 1, n), wide(cos, 1, n)
            t_ = tmp[i % 2][:, 0:n * T].rearrange("p (c t) -> p c t", c=n)
            frees(v.tensor_tensor(t_, work_bank(name, i)[:, 0:n * T].rearrange("p (c t) -> p c t", c=n), sin,
                                  ALU.mult), name, i)
            link(v.tensor_tensor(a, a, cos, ALU.mult))
            copied(dve, name, i)
            v.tensor_tensor(a, a, t_, ALU.add).then_inc(S["rope_ready"], 1)

        def row_max(name, i, b, slot):
            filled(dve, name, i)
            link(v.tensor_reduce(nm3[slot], b[:, :].rearrange("p (d s) -> p d s", d=2), AX.X,
                                 ALU.max, negate=True))
            v.tensor_scalar(nm3[slot], nm3[slot], 64 ** -0.5, None, ALU.mult).then_inc(S["max3_ready"], 1)

        def weigh(n, slot, gate):
            dve.wait_ge(S["exp3_done"], n)
            link(v.reciprocal(rw3[slot], rs3[slot]))
            link(v.tensor_tensor(rw3[slot], rw3[slot], gate, ALU.mult))
            v.tensor_tensor(p3[slot][:, :, :], p3[slot][:, :, :],
                            wide(rw3[slot].rearrange("p (d a) -> p d a", a=1), 2, T), ALU.mult)\
                .then_inc(S["p3_ready"], 1)

        ffn3(0, 6)
        dve.wait_ge(S["x_new"], TT * 7)
        normalise(7)
        for i in range(4):
            copied(dve, "nsa_q", i)
            rope("nsa_rope", i, q3[:, 2 * i:2 * i + 2, :], 2)
        for i in range(3):
            rope("nsa_rope", 4 + i, kraw[:, 2 * i:2 * i + 2, :], 2)
        dve.wait_ge(S["rope_ready"], 7)
        v.memset(kc[:, :, :, :], 0.0).then_inc(S["zeroed"], 1)
        for src, dst in ((kraw[:, 0:2, :], kp), (vraw, vp)):
            for half in range(2):
                v.tensor_copy(dst[0:64, half:4:2, :], src[64 * half:64 * half + 64, :, :])
                ins = v.tensor_copy(dst[64:128, half:4:2, 0:T - 1], src[64 * half:64 * half + 64, :, 1:T])
        link(ins)
        for i, (src, pe_) in enumerate(((kp, "nsa_ck_pe_3"), (vp, "nsa_cv_pe_3"))):
            for a in range(2):
                win = src[:, :, BS * a:BS * a + BS * NB].rearrange("p g (b m two) -> p m g b two", b=NB, two=2)
                bias = wide(wide(col(pe_, 8 * a, 8).rearrange("p (m a b) -> p m a b", a=1, b=1), 2, 4), 3, NB)
                for m in range(8):
                    ins = v.tensor_tensor(xb[i][:, 8 * a + m, :, :], win[:, m, :, :, 0], bias[:, m, :, :], ALU.add)
        ins.then_inc(S["cmp_x_ready"], 1)
        dve.wait_ge(S["cmp_x_ready"], 1)
        for br in range(2):
            link(v.memset(A[3 + br][:, :], 0.0))
            for half in range(2):
                for d in range(2):
                    ins = v.tensor_copy(kd[br][64 * d:64 * d + 64, half:4:2, d, :],
                                        kraw[64 * half:64 * half + 64, 2 + 2 * br:4 + 2 * br, :])
        link(ins)
        copied(dve, "nsa_g", 0)
        for t in range(TT):
            filled(dve, "cmp_s", t)
            frees(v.tensor_scalar(pc[:, t, :, :].rearrange("p h b -> p (h b)"), work_bank("cmp_s", t)[:, 0:240],
                                  64 ** -0.5, None, ALU.mult), "cmp_s", t)
        for t in range(TT):
            copied(dve, "cmp_s", t)
        for t in range(TT):
            ins = v.tensor_tensor(pc[:, t, :, :], pc[:, t, :, :],
                                  wide(const("cmp_neg", "p (t a b) -> p t a b", t=TT, a=1)[:, t, :, :], 1, 16),
                                  ALU.add)
        link(ins)
        link(v.reduce_max(cm[:, :, :], pc[:, :, :, :], AX.X))
        v.tensor_tensor(pc[:, :, :, :].rearrange("p t h b -> p (t h) b"), pc[:, :, :, :].rearrange("p t h b -> p (t h) b"),
                        wide(cm[:, :, :].rearrange("p t (h a) -> p (t h) a", a=1), 2, NB),
                        ALU.subtract).then_inc(S["cmp_in"], 1)
        dve.wait_ge(S["cmp_exp"], 1)
        link(v.reduce_sum(cr[:, :, :], pc[:, :, :, :], AX.X))
        link(v.reciprocal(cr[:, :, :], cr[:, :, :]))
        link(v.tensor_tensor(cr[:, :, :], cr[:, :, :], gate3[:, :, 0, :], ALU.mult))
        link(v.tensor_tensor(pc[:, :, :, :].rearrange("p t h b -> p (t h) b"), pc[:, :, :, :].rearrange("p t h b -> p (t h) b"),
                             wide(cr[:, :, :].rearrange("p t (h a) -> p (t h) a", a=1), 2, NB), ALU.mult))
        for t in range(TT):
            ins = v.tensor_tensor(pc[:, t, :, :], pc[:, t, :, :],
                                  wide(const("cmp_one", "p (t a b) -> p t a b", t=TT, a=1)[:, t, :, :], 1, 16),
                                  ALU.mult)
        ins.then_inc(S["cmp_ready"], 1)
        for s in range(4):
            row_max("nsa_heads", s, bank[s], s)
        for m in range(8):
            for s in range(4):
                br, t = s // 2, s % 2
                weigh(4 * m + s + 1, 4 * (m % 2) + s, gate3[:, t, 1 + br, 2 * m:2 * m + 2])
            if m < 7:
                for s in range(4):
                    row_max("nsa_heads", pair_scores(m + 1, 4, 6) + s, bank[s], 4 * ((m + 1) % 2) + s)
        low("ffn3_1", 0)
        add_acc("nsa_out")
        dve.wait_ge(S["x_new"], TT * 8)
        ffn3(1, 8)
        dve.wait_ge(S["x_new"], TT * 9)
        ffn3(2, 9)
        dve.wait_ge(S["x_new"], TT * 10)
        normalise(10)
        for i in range(4):
            copied(dve, "swa_q", i)
            rope("swa_rope", i, q3[:, 2 * i:2 * i + 2, :], 2)
        copied(dve, "swa_kv", 0)
        filled(dve, "swa_rope", 4)
        frees(v.tensor_tensor(tmp[0][:, 0:T], work_bank("swa_rope", 4)[:, 0:T], const("rope_sin"), ALU.mult),
              "swa_rope", 4)
        link(v.tensor_tensor(k4, k4, const("rope_cos"), ALU.mult))
        copied(dve, "swa_rope", 4)
        link(v.tensor_tensor(k4, k4, tmp[0][:, 0:T], ALU.add))
        link(v.memset(kd4[:, :, :, :], 0.0))
        for half in range(2):
            for d in range(2):
                ins = v.tensor_copy(kd4[64 * d:64 * d + 64, half, d, :], k4[64 * half:64 * half + 64, :])
        ins.then_inc(S["rope_ready"], 1)
        def swa_max(m):
            sinks = row("sinks")[:, 2 * m:2 * m + 2]
            for t in range(TT):
                slot = 2 * (m % 2) + t
                filled(dve, "swa_heads", pair_scores(m, 2, 3) + t)
                link(v.tensor_reduce(nm3[slot], bank[slot][:, :].rearrange("p (d s) -> p d s", d=2),
                                     AX.X, ALU.max))
                link(v.scalar_tensor_tensor(nm3[slot], nm3[slot], 64 ** -0.5, sinks, ALU.mult, ALU.max))
                link(v.tensor_tensor(sk[slot], sinks, nm3[slot], ALU.subtract))
                v.tensor_scalar(nm3[slot], nm3[slot], -1.0, None, ALU.mult).then_inc(S["max3_ready"], 1)

        swa_max(0)
        for m in range(8):
            for t in range(TT):
                slot = 2 * (m % 2) + t
                dve.wait_ge(S["exp3_done"], 32 + 2 * m + t + 1)
                link(v.tensor_tensor(rw3[slot], rs3[slot], sk[slot], ALU.add))
                link(v.reciprocal(rw3[slot], rw3[slot]))
                v.tensor_tensor(p3[slot][:, :, :], p3[slot][:, :, :],
                                wide(rw3[slot].rearrange("p (d a) -> p d a", a=1), 2, T), ALU.mult)\
                    .then_inc(S["p3_ready"], 1)
            if m < 7:
                swa_max(m + 1)
        low("ffn3_3", 0)
        add_acc("swa_out")
        dve.wait_ge(S["x_new"], TT * 11)
        ffn3(3, 11)
        dve.wait_ge(S["x_new"], TT * 12)
        mean(12)
        dve.wait_ge(S["final_row_in"], 16)
        for t in range(TT):
            v.scalar_tensor_tensor(xn[:, t, :], x[:, t, :], rstd[:, t:t + 1], row("gate_m"), ALU.mult, ALU.mult)\
                .then_inc(S["out_ready"], 1)

    ctx.close()


OUT_SHAPE = (1, T, D)
WEIGHTS = {
    "w_ada": D, "w_in": D, "w_fourier": 512, "w_conv_out": D, "w_o": D, "w_router": D,
    "w_gate_e": NE * D, "w_up_e": NE * D, "w_down_e": NE * DE, "w_in_2": D, "lru_wa_2": D, "lru_wx_2": D,
    "w_lru_br_2": D, "w_attn_br_2": D, "w_out_2": D, "w_up_2": D, "w_down_2": F2, "w_ple_gate_2": D,
    "w_ple_proj_2": 256, "rel_bias_2": 32, "ffn1_w_gu_3": 2 * D, "ffn1_w_down_3": 2 * F3,
    "ffn2_w_gu_3": 2 * D, "ffn2_w_down_3": 2 * F3, "nsa_w_in_3": D, "nsa_ck_w1_3": 2048, "nsa_ck_w2_3": P,
    "nsa_cv_w1_3": 2048, "nsa_cv_w2_3": P, "nsa_w_out_3": D, "swa_w_in_3": D, "swa_w_out_3": D, "x": T,
}


def kernel(**inputs):
    import numpy as _np
    import concourse.bacc as _bacc
    from concourse import mybir as _mybir
    from concourse.bass_utils import run_bass_kernel_spmd as _run

    def given(name):
        return _np.asarray(inputs[name])

    nc = _bacc.Bacc("TRN2", target_bir_lowering=False, num_devices=1)
    arrays = {name: _np.ascontiguousarray(given(name)).reshape(rows, -1) for name, rows in WEIGHTS.items()}
    (arrays["consts"], const_at), arrays["masks"] = shape_constants()
    arrays["cols"], col_at = column_inputs(given)
    arrays["rows"], row_at = row_inputs(given)
    arrays["final_norm"] = _np.ascontiguousarray(given("final_norm_3").reshape(1, D))
    arrays["pT"] = _np.ascontiguousarray(given("p_2").reshape(T, 256).T)
    handles = {n: nc.dram_tensor(f"in_{n}", a.shape, _mybir.dt.from_np(a.dtype), kind="ExternalInput").ap()
               for n, a in arrays.items()}
    out = nc.dram_tensor("out_0", (T, D), _mybir.dt.float32, kind="ExternalOutput").ap()
    network(nc, lambda name: handles[name], out, const_at, col_at, row_at)
    r = _run(nc, [{f"in_{n}": a for n, a in arrays.items()}], core_ids=[0])
    return r.results[0]["out_0"].reshape(OUT_SHAPE)
```

```python
from contextlib import ExitStack

import numpy as np

import concourse.bass as bass
from concourse import mybir

T, D = 256, 1024
P = 128
TT, DC = T // P, D // P
EPS = 1e-6
NEG = -1e30
NE, CAP, DE = 16, 32, 2048
F2, F3 = 3072, 2816
NSLOT, SLAB = 3, 4096
NB, BL, BS = 15, 32, 16


def shape_constants():
    i128 = np.arange(P)
    tok = np.arange(T)
    parts = {}
    parts["ident"] = np.eye(P)
    parts["tri"] = (i128[:, None] < i128[None, :])
    ang = 2 * np.pi * ((tok[:, None] * tok[None, :]) % T) / T
    norm = 1 / math_sqrt(T * P)
    cs = np.concatenate([np.cos(ang), -np.sin(ang)], 1) * norm
    parts["dft_seq"] = cs.reshape(TT, P, 2 * T).transpose(1, 0, 2).reshape(P, -1)
    angc = 2 * np.pi * ((i128[:, None] * i128[None, :]) % P) / P
    parts["dft_cos"] = np.cos(angc)
    parts["dft_sin"] = np.sin(angc)
    t = tok.reshape(TT, P).T[:, :, None]
    s = tok[None, None, :]
    masks = np.stack([np.where(s <= t, 0.0, NEG), np.where((s <= t) & (t - s < P), 0.0, NEG)], 1)
    n = np.arange(NB)[None, None, :]
    valid = (n * BS + BL - 1 <= t)
    parts["cmp_neg"] = np.where(valid, 0.0, NEG).reshape(P, -1)
    parts["cmp_one"] = valid.reshape(P, -1)
    parts["iota"] = np.broadcast_to(np.arange(CAP), (P, CAP))
    inv = (np.float32(10000.0) ** (-np.arange(0, 64, 2, dtype=np.float32) / np.float32(64)))
    rope = tok.astype(np.float32)[None, :] * inv.astype(np.float32)[:, None]
    parts["rope_cos"] = np.tile(np.cos(rope), (4, 1))
    parts["rope_sin"] = np.tile(np.sin(rope), (4, 1))
    rot = np.zeros((P, P))
    for h in range(0, P, 64):
        for j in range(32):
            rot[h + 32 + j, h + j] = -1.0
            rot[h + j, h + 32 + j] = 1.0
    parts["rope_rot"] = rot
    dist = np.maximum(255 - np.arange(2 * T), 0)
    df = np.maximum(dist, 1).astype(np.float32)
    large = 16 + (np.log(df / np.float32(16)) / np.float32(math_log(128 / 16)) * np.float32(16)).astype(np.int32)
    bucket = np.where(dist < 16, dist, np.minimum(large, 31))
    oh = np.zeros((P, 2 * T))
    oh[bucket, np.arange(2 * T)] = 1.0
    parts["buckets"] = oh
    return pack(parts), masks.astype(np.float32).reshape(P, -1)


def math_sqrt(v):
    return float(np.sqrt(v))


def math_log(v):
    return float(np.log(v))


def pack(parts):
    at, where, cols = 0, {}, []
    for name, a in parts.items():
        a = np.asarray(a, np.float32).reshape(P, -1)
        where[name] = (at, a.shape[1])
        at += a.shape[1]
        cols.append(a)
    return np.ascontiguousarray(np.concatenate(cols, 1)), where


def column_inputs(v):
    def col(a):
        a = a.reshape(-1, P)
        return a.T
    parts = {"c": col(v("c"))}
    for name in ("b_ada", "g_norm_mix", "b_gate", "w_conv", "g_norm_moe", "mix_norm_2", "lru_conv_w_2",
                 "lru_conv_b_2", "lru_ba_2", "lru_bx_2", "lru_lambda_2", "q_norm_2", "k_norm_2", "ffn_norm_2",
                 "ffn_conv_w_2", "ffn_conv_b_2", "ple_norm_2", "ffn1_norm_3", "mix_norm_3", "ffn2_norm_3",
                 "nsa_ck_pe_3", "nsa_cv_pe_3"):
        parts[name] = col(v(name))
    return pack(parts)


def row_inputs(v):
    b_ada = v("b_ada").reshape(-1)
    parts = {"g_final": v("g_final"), "gate_m": b_ada[2 * D:3 * D],
             "gate_f": b_ada[5 * D:6 * D], "b_router": v("b_router"), "sinks": v("swa_sinks_3")}
    at, where, rows = 0, {}, []
    for name, a in parts.items():
        a = a.reshape(1, -1)
        where[name] = (at, a.shape[1])
        at += a.shape[1]
        rows.append(a)
    return np.ascontiguousarray(np.concatenate(rows, 1)), where


class Plan:

    def __init__(self):
        self.split0, self.split_body, self.splits = {}, {}, 0
        self.split_end = []
        self.batch0, self.work0, self.slab0, self.kinds, self.times = {}, {}, {}, {}, {}
        self.slab0_body = {}
        self.batches = self.works = self.slabs = 0
        self.slab_end = []

    def add(self, name, kinds, frees=(), times=1, split=0):
        self.split0[name], self.split_body[name] = self.splits, split
        self.splits += split * times
        for k in range(times):
            self.split_end += [self.batches + k * len(kinds) + f + 1 for f in frees[:split]]
        self.batch0[name], self.work0[name], self.slab0[name] = self.batches, self.works, self.slabs
        self.kinds[name], self.times[name] = kinds, times
        self.slab0_body[name] = len(frees)
        for k in range(times):
            self.slab_end += [self.batches + k * len(kinds) + f + 1 for f in frees]
        self.batches += times * len(kinds)
        self.works += times * kinds.count("W")
        self.slabs += times * len(frees)

    def done(self, name, i):
        return self.batch0[name] + i + 1

    def work(self, name, i):
        return self.work0[name] + self.kinds[name][:i].count("W")


def pair_scores(m, n_s, n_w):
    return 0 if m == 0 else n_s + (n_s + n_w) * (m - 1)


def pair_rest(m, n_s, n_w):
    return n_s + (n_s + n_w) * m + (n_s if m < 7 else 0)


def make_plan():
    p = Plan()
    for m in range(4):
        p.add(f"mod{m}a", "W", [0])
        p.add(f"mod{m}b", "W")
    p.add("norm0", "WWWW")
    p.add("uf", "WW", [1], split=1)
    p.add("dft_a", "WWWW")
    p.add("dft_b", "WW")
    for s in range(10):
        p.add(f"in{s}", "WW", [1], split=1)
        p.add(*((f"mod{4 + s // 2}a", "W", [0]) if s % 2 == 0 else (f"mod{4 + s // 2}b", "W")))
    p.add("fourier_out", "WWWW", [3], split=1)
    p.add("mod9a", "W", [0])
    p.add("conv_out", "WWWW", [1, 3], split=2)
    p.add("mod9b", "W")
    p.add("mod10a", "W", [0])
    p.add("w_o", "AA", [0, 1], split=2)
    p.add("mod10b", "W")
    p.add("mod11a", "W", [0])
    p.add("mod11b", "W")
    p.add("norm1", "WWWW")
    p.add("router", "W")
    p.add("probsT", "W")
    p.add("maskT", "W")
    p.add("slots", "W")
    p.add("scatterT", "W" * 8)
    p.add("gather", "W" * 8)
    p.add("experts", "AAAW" + "AAAW" + "W" + "AAAW" + "A", [0, 1, 2, 3, 4, 5, 6, 7, 9, 10, 11, 12], times=NE)
    p.add("experts_end", "A")
    p.add("norm2", "WWWW")
    p.add("lru_x", "WWWW", [1, 3])
    p.add("lru_gate", "WWWW", [1, 3])
    p.add("q", "WWWW", [1, 3])
    p.add("lru_ri", "W" * 8, [7])
    p.add("kv", "WW", [1])
    p.add("qi", "WW", [1])
    p.add("kiwi", "WW")
    p.add("bias", "W" * 8)
    p.add("qk_ms", "W" * 5)
    p.add("gate_a", "WWWW", [1, 3])
    p.add("score", "W" * 8)
    p.add("gate_b", "WWWW", [1, 3])
    p.add("logits2", "W" * 8)
    p.add("lru_out", "WWWW", [1, 3])
    p.add("pv2", "WWW" * 4)
    p.add("attn_out", "WWWW", [1, 3])
    p.add("w_out2", "AA", [0, 1])
    p.add("norm3", "WWWW")
    p.add("ffn2", "WWWWA", [1, 3, 4], times=F2 // 512, split=3)
    p.add("ffn2_end", "A")
    p.add("norm4", "WWWW")
    p.add("ple", "WW" * 2 + "WWWW", [1, 3, 7], split=2)
    for n in range(4):
        p.add(f"ffnorm{n}", "WWWW")
        p.add(f"ffn3_{n}", "WWWWA", [1, 3, 4], times=5, split=3)
        p.add(f"ffn3_{n}_end", "WWA", [1, 2], split=2)
        if n == 0:
            p.add("nsa_norm", "WWWW")
            p.add("nsa_kv0", "WW", [1], split=1)
            p.add("nsa_kv12", "WW" * 2, [1, 3], split=2)
            p.add("nsa_g", "W")
            p.add("nsa_rope_k", "W" * 3)
            p.add("nsa_q", "WWWW", [1, 3], split=2)
            p.add("nsa_rope", "W" * 4)
            p.add("cmp_hid", "WW", [1])
            p.add("cmp_kv", "WW")
            p.add("cmp_s", "WW")
            p.add("nsa_heads", "AAAA" + ("AAAA" + "WWWWWW") * 7 + "WWWWWW")
            p.add("nsa_out", "AA", [0, 1], split=2)
        if n == 2:
            p.add("swa_norm", "WWWW")
            p.add("swa_kv", "W", [0], split=1)
            p.add("swa_rope_k", "W")
            p.add("swa_q", "WWWW", [1, 3], split=2)
            p.add("swa_rope", "W" * 4)
            p.add("swa_heads", "AA" + ("AA" + "WWW") * 7 + "WWW")
            p.add("swa_out", "AA", [0, 1], split=2)
    return p


def network(nc, dram, out, const_at, col_at, row_at):
    fp32, fp32r, bf16 = mybir.dt.float32, mybir.dt.float32r, mybir.dt.bfloat16
    ALU = mybir.AluOpType
    ACT = mybir.ActivationFunctionType
    AX = mybir.AxisListType
    plan = make_plan()
    ctx = ExitStack()

    def sb(name, shape):
        return ctx.enter_context(nc.sbuf_tensor(name, shape, fp32))

    twins = {}

    def twinned(name, shape):
        with nc.sbuf_tensor(name, shape, fp32) as plain:
            pass
        twins[name] = ctx.enter_context(nc.sbuf_tensor(f"{name}_r", shape, fp32r))
        return plain

    def sem(name):
        return ctx.enter_context(nc.semaphore(name))

    n_const = sum(w for _, w in const_at.values())
    n_col = sum(w for _, w in col_at.values())
    n_row = sum(w for _, w in row_at.values())
    ring = [twinned(f"ring{i}", [P, SLAB]) for i in range(NSLOT)]
    consts = sb("consts", [P, n_const])
    cols = sb("cols", [P, n_col])
    rows = sb("rows", [P, n_row])
    x = sb("x", [P, TT, D])
    xn = twinned("xn", [P, TT, D])
    hT = twinned("hT", [P, DC, T])
    AB, AC = twinned("AB", [P, 4096]), twinned("AC", [P, 4096])
    A = [twinned(f"A{i}", [P, 2048]) for i in range(9) if i not in (1, 2)]
    A[1:1] = [AC[:, 0:2048], AC[:, 2048:4096]]
    w_router = sb("w_router_sb", [P, DC, NE])
    w_kiwi = sb("w_kiwi", [P, DC, 72])
    w_nsa_gate = sb("w_nsa_gate", [P, DC, 48])
    ck_w2 = sb("ck_w2", [P, 64])
    cv_w2 = sb("cv_w2", [P, 64])
    pT_in = sb("pT_in", [P, 2, T])
    rel_in = sb("rel_in", [32, 8])
    ones = sb("ones", [P, P])
    ones_mean = sb("ones_mean", [P, P])
    zeros = ctx.enter_context(nc.sbuf_tensor("zeros", [P, 512], bf16))
    diag = sb("diag", [P, TT, P])
    ident16 = ctx.enter_context(nc.sbuf_tensor("ident16", [P, P], bf16))
    masks16 = ctx.enter_context(nc.sbuf_tensor("masks16", [P, 2 * TT, T], bf16))
    causal16, window16 = masks16[:, 0:TT, :], masks16[:, TT:2 * TT, :]
    neg_half = sb("neg_half", [P, TT])
    tmp = [sb(f"tmp{i}", [P, 512]) for i in range(4)]
    small = sb("small", [P, 640])

    c_pad = tmp[2][:, 0:256].rearrange("p (k m) -> p k m", m=32)

    def const(name, shape=None, **k):
        at, n = const_at[name]
        v = consts[:, at:at + n]
        return v.rearrange(shape, **k) if shape else v

    def col(name, i=0, n=1):
        return cols[:, col_at[name][0] + i:col_at[name][0] + i + n]

    def row(name):
        at, n = row_at[name]
        return rows[:, at:at + n]

    small_at = [0]

    def narrow(n):
        small_at[0] += n
        assert small_at[0] <= 640
        return small[:, small_at[0] - n:small_at[0]]

    ident = const("ident")
    fm = lambda a: a[:, :].rearrange("p (c t) -> p c t", t=T)

    junk = hT[:, :, :].rearrange("p (a c) t -> p a (c t)", a=TT)
    rel_rep = xn[0:32, 0, :].rearrange("p (h n) -> p h n", h=8)

    masks_in = A[8][:, 0:2 * TT * T]
    ss, ms, rstd = narrow(2), narrow(2), narrow(2)
    c_act = narrow(8)
    mod_part = tmp[3]
    modc = narrow(48)
    g_mix, g_moe = narrow(8), narrow(8)
    uf = A[0][:, 0:1024].rearrange("p (t n) -> p t n", t=TT)
    dft_v = A[1][:, :].rearrange("p (g n) -> p g n", g=4)
    f_v, f_b, f_cv, f_ga, f_gb, f_bc, f_z = (fm(A[i]) for i in (2, 3, 4, 5, 6, 1, 4))
    logit = narrow(32).rearrange("p (t e) -> p t e", t=TT)
    prob = narrow(32).rearrange("p (t e) -> p t e", t=TT)
    rmax, rsum = narrow(2), narrow(2)
    probT = tmp[0][0:NE, 0:T]
    probW = tmp[1][0:NE, 0:T]
    mask = tmp[2][0:NE, 0:T]
    top8 = narrow(8)
    maskT = narrow(32).rearrange("p (t e) -> p t e", t=TT)
    slot_of = narrow(32).rearrange("p (t e) -> p t e", t=TT)
    sel = A[0][:, 0:1024].rearrange("p (t e s) -> p t e s", t=TT, e=NE)
    sel_prob = AB[:, :].rearrange("p (t e g s) -> p t e g s", t=TT, e=NE, g=4)
    scat = AC[:, :].rearrange("p (e t) -> p e t", e=NE)
    xeT = AB[:, :].rearrange("p (c s) -> p c s", c=DC)
    xe_now = A[3][:, 0:256].rearrange("p (c s) -> p c s", c=DC)
    scat_now = A[3][:, 256:512]
    e_act, e_h, e_hT, e_y = (A[3][:, 512:1024], A[3][:, 1024:1536], A[3][:, 1536:2048], A[4][:, 0:512])
    l_t, l_ua, l_a, l_i, l_tmp, l_g = (fm(A[i]) for i in (0, 1, 2, 3, 4, 8))
    sp8, nsp8, sp_a, sp_b = narrow(8), narrow(8), narrow(8), narrow(8)
    q2 = fm(A[7])
    sq2 = fm(A[6])
    k2 = A[5][:, 0:512].rearrange("p (g t) -> p g t", g=2)
    v2 = A[5][:, 512:1024].rearrange("p (t n) -> p t n", t=TT)
    qi = A[5][:, 1024:2048].rearrange("p (c t) -> p c t", t=T)
    ki = tmp[0][:, :].rearrange("p (d t) -> p d t", d=2)
    wi = narrow(16).rearrange("p (t h) -> p t h", t=TT)
    sqk = tmp[1]
    bias2 = AB[:, :].rearrange("p (t h s) -> p t h s", t=TT, h=8)
    bias_row = AB[:, :].rearrange("p (h j) -> p h j", h=8)
    msq = [tmp[2], tmp[3]]
    relu_s = [A[6][:, 0:512], A[6][:, 512:1024]]
    score = A[6][:, 1024:1536].rearrange("p (t s) -> p t s", t=TT)
    score_w = A[6][:, 1536:2048].rearrange("p (t s) -> p t s", t=TT)
    t8 = narrow(8)
    att = [fm(A[4]), fm(A[8])]
    nm2 = narrow(16).rearrange("p (t h) -> p t h", t=TT)
    rs2 = narrow(16).rearrange("p (t h) -> p t h", t=TT)
    pT2 = [tmp[2], tmp[3]]
    o2 = fm(A[1])
    merged = fm(A[0])
    h_high = twins["A7"][:, :].rearrange("p (c t) -> p c t", t=T)
    h_low = twins["hT"]
    hid_high = twins["A8"][:, 0:1024].rearrange("p (f t) -> p f t", t=T)
    hid_low = twins["A0"][:, 0:1024].rearrange("p (f t) -> p f t", t=T)

    y_high, y_low = (twins["A0"][:, at:at + 1024].rearrange("p (g t) -> p g t", g=4) for at in (0, 1024))
    bc_high, bc_low = fm(twins["A3"]), fm(twins["AC"][:, 0:2048])
    z_high, z_low = h_high, fm(twins["A4"])
    o_high, o_low = twins["hT"], fm(twins["A8"])

    def halves(name, s):
        pieces = split_areas(name, s)
        if len(pieces) == 1:
            at, area = pieces[0]
            n = area.shape[1] // 2
            pieces = [(at, area[:, 0:n]), (at + n, area[:, n:2 * n])]
        return pieces

    def split_areas(name, s):
        t_ = {n: twins[n][:, :] for n in ("AB", "A3", "A4", "A5", "A6", "A8")}
        if name == "swa_kv":
            return [(0, t_["AB"][:, 0:2048])]
        if name in ("uf", "fourier_out", "conv_out", "w_o") or name.startswith("in"):
            if (plan.split0[name] + s) % 2 == 0:
                return [(0, t_["AB"])]
            return [(0, twins["xn"][:, :, :].rearrange("p t d -> p (t d)")), (2048, t_["A8"])]
        if name in ("nsa_out", "swa_out"):
            a, b = (("A3", "A4"), ("A5", "A6"))[s]
            return [(0, t_[a]), (2048, t_[b])]
        if (name, s) in (("nsa_kv0", 0), ("nsa_kv12", 1), ("nsa_q", 1), ("swa_q", 1)):
            return [(0, t_["AB"])]
        if name in ("nsa_kv12", "nsa_q", "swa_q"):
            return [(0, t_["A6"]), (2048, t_["A8"])]
        if name.endswith("_end") and s == 1:
            return [(0, t_["A5"])]
        return ([(0, twins["AB"])], [(0, twins["AC"])], [(0, twins["A3"]), (2048, twins["A4"])])[s]

    def hidden_tiles(n):
        return (F2 + n * F3) // P

    hid = A[0][:, 0:1024].rearrange("p (f t) -> p f t", t=T)
    f_conv = [tmp[0][:, 0:256], tmp[1][:, 0:256]]
    f_act = [tmp[2][:, 0:256], tmp[3][:, 0:256]]
    p_gate = A[6][:, :].rearrange("p (h t n) -> p h t n", h=2, t=TT)
    q3 = fm(A[0])
    kraw = A[1][:, 0:1536].rearrange("p (c t) -> p c t", t=T)
    vraw = A[1][:, 1536:2048].rearrange("p (c t) -> p c t", t=T)
    v3 = A[2][:, 0:1024].rearrange("p (b t n) -> p b t n", b=2, t=TT)
    kd = [A[i][:, :].rearrange("p (g d t) -> p g d t", g=4, d=2) for i in (3, 4)]
    kp = A[4][:, 0:1024].rearrange("p (g t) -> p g t", g=4)
    vp = A[4][:, 1024:2048].rearrange("p (g t) -> p g t", g=4)
    xb = [A[5][:, 0:960].rearrange("p (m g b) -> p m g b", m=16, g=4),
          A[5][:, 960:1920].rearrange("p (m g b) -> p m g b", m=16, g=4)]
    hid_c = [A[2][:, 1024:1084], A[2][:, 1084:1144]]
    kc = A[2][:, 1144:1264].rearrange("p (d g b) -> p d g b", d=2, g=4)
    vc = A[2][0:NB, 1264:1520]
    gate3 = narrow(96).rearrange("p (t b h) -> p t b h", t=TT, b=3)
    pc = A[6][:, 0:480].rearrange("p (t h b) -> p t h b", t=TT, h=16)
    cm, cr = (narrow(32).rearrange("p (t h) -> p t h", t=TT) for _ in range(2))
    p3 = [A[a][:, 512 * i:512 * i + 512].rearrange("p (d s) -> p d s", d=2) for a in (7, 1) for i in range(4)]
    pT3 = [AB[:, 512 * i:512 * i + 384] for i in range(4)]
    pcT = AB[0:NB, 2048:2560]
    nm3 = [narrow(2) for _ in range(8)]
    rs3 = [narrow(2) for _ in range(8)]
    rw3 = [narrow(2) for _ in range(8)]
    v4 = A[2][:, 0:256].rearrange("p (t n) -> p t n", t=TT)
    k4 = A[1][:, 0:256]
    kd4 = A[3][:, 0:1024].rearrange("p (g d t) -> p g d t", g=2, d=2)
    sk = [narrow(2) for _ in range(4)]

    skew = nc.dram_tensor("bias_rows", [P * 8 * 512], fp32, kind="Internal").ap()

    bank = [ctx.enter_context(nc.psum_tensor(f"bank{i}", [P, 512], fp32)) for i in range(8)]
    acc = [[bank[0], bank[1]], [bank[2], bank[3]]]

    products_done = sem("products_done")
    bank_copied = [sem(f"bank_copied{i}") for i in range(4)]
    slab_loaded = [sem(f"slab_loaded{i}") for i in range(NSLOT)]
    inputs_loaded = sem("inputs_loaded")
    cols_loaded = sem("cols_loaded")
    first_loaded = sem("first_loaded")
    fills_done = sem("fills_done")
    own = {"dve": sem("dve_own")}

    def filled(eng, name, i, it=0):
        eng.wait_ge(products_done, plan.done(name, i) + it * len(plan.kinds[name]))

    def loaded(eng, name, s, it=0):
        n = plan.slab0[name] + s
        per_pass = plan.slab0_body[name] // NSLOT * 32 if plan.times[name] > 1 else 0
        eng.wait_ge(slab_loaded[n % NSLOT], 32 * (n // NSLOT + 1) + it * per_pass)
        return ring[n % NSLOT]

    def split_number(name, s, it=0):
        return plan.split0[name] + s + 1 + it * plan.split_body[name]

    def work_bank(name, i):
        return bank[4 + plan.work(name, i) % 4]

    def copied(eng, name, i, it=0):
        w = plan.work(name, i)
        eng.wait_ge(bank_copied[w % 4], w // 4 + 1 + it * (plan.kinds[name].count("W") // 4))

    def frees(ins, name, i):
        return ins.then_inc(bank_copied[plan.work(name, i) % 4], 1)

    class Chain:

        def __init__(self, eng, which):
            self.eng, self.sem, self.n, self.off = eng, own[which], 0, 0

        def __call__(self, ins):
            ins.then_inc(self.sem, 1)
            self.n += 1
            self.eng.wait_ge(self.sem, self.n + self.off)

    def wide(a, dim, n):
        shape = list(a.shape)
        assert shape[dim] == 1
        shape[dim] = n
        return a.broadcast_to(shape)

    names = ("c_act_ready", "c_pad_ready", "mod_ready", "x_new", "squares_done", "mean_ready", "rstd_ready",
             "xn_ready", "conv_ready", "z_ready", "logit_ready", "exp_ready", "prob_ready", "mask_ready",
             "zeroed", "msq_ready", "sel_prob_ready", "expert_staged", "rel_ready", "rows_out", "bias_in",
             "lam_exp_in", "lam_exp_out", "sp_ready", "ua_ready", "tanh_done", "decay_done", "mult_in",
             "mult_out", "scan_done", "lru_ready", "rsq_ready", "qk_ready", "relu_used", "att_in", "att_exp",
             "att_ready", "merged_ready", "conv_in", "gelu_done", "rope_ready", "final_row_in", "high_ready",
             "low_ready", "high_norm", "h0_split", "y_high", "o_high", "hid_split", "cmp_x_ready", "cmp_in",
             "cmp_exp", "cmp_ready", "max3_ready", "exp3_done", "masks16_ready", "p3_ready", "out_ready",
             "out_stored")
    S = {n: sem(n) for n in names}

    NORMS = ["norm0", "norm1", "g_final", "norm2", "norm3", "norm4", "ffnorm0", "nsa_norm", "ffnorm1",
             "ffnorm2", "swa_norm", "ffnorm3", "final"]
    N_FIRST, N_INPUTS, N_FILLS = 16 * 3, 16 * 8, 5
    dft_seq = const("dft_seq", "p (t n) -> p t n", t=TT)
    block = ctx.enter_context(nc.Block())

    @block.sync
    def _(sp):
        def k_rows(w, c0, n):
            return w[:, c0:c0 + n].rearrange("(k p) n -> p k n", p=P)

        def two_halves(slot, src, n):
            dst = ring[slot][:, 0:8 * n].rearrange("p (k n) -> p k n", k=8)
            return [(dst[:, 4 * a:4 * a + 4, :], src[:, 4 * a:4 * a + 4, :]) for a in range(2)]

        def row_block(slot, w, r0, n):
            dst = ring[slot][:, 0:n * D].rearrange("p (k n) -> p k n", k=n)
            src = w[r0:r0 + n * P, :].rearrange("(k p) n -> p k n", p=P)
            h = n // 2
            return [(dst[:, 0:h, :], src[:, 0:h, :]), (dst[:, h:n, :], src[:, h:n, :])]

        def row_block_at(slot, w, r0, n):
            dst = ring[slot][:, 0:n * D].rearrange("p (k n) -> p k n", k=n)
            src = w[bass.ds(r0, n * P), :].rearrange("(k p) n -> p k n", p=P)
            h = n // 2
            return [(dst[:, 0:h, :], src[:, 0:h, :]), (dst[:, h:n, :], src[:, h:n, :])]

        def gate_up(slot, w, f0, width):
            dst = ring[slot][:, :].rearrange("p (k n) -> p k n", k=8)
            gate = w[:, bass.ds(f0, 256)].rearrange("(k p) n -> p k n", p=P)
            up = w[:, bass.ds(f0 + width, 256)].rearrange("(k p) n -> p k n", p=P)
            return [(dst[:, :, 0:256], gate), (dst[:, :, 256:512], up)]

        def load(name, s, halves, it=0, after=None):
            n = plan.slab0[name] + s
            if n >= NSLOT:
                sp.wait_ge(products_done, (plan.slab_end[n - NSLOT] if after is None else after))
            for dst, src in halves:
                sp.dma_start(dst, src).then_inc(slab_loaded[n % NSLOT], 16)

        def slot(name, s):
            return (plan.slab0[name] + s) % NSLOT

        def dense(name, w, n_slabs, c0=0):
            for s in range(n_slabs):
                load(name, s, two_halves(slot(name, s), k_rows(w, c0 + 512 * s, 512), 512))

        def loop(name, slab):
            body = plan.slab0_body[name]
            for s in range(body):
                load(name, s, slab(s, 0))
            with sp.Fori(1, plan.times[name]) as it:
                for s in range(body):
                    n = plan.slab0[name] + body + s
                    load(name, s, slab(s, it), after=plan.slab_end[n - NSLOT] + (it - 1) * len(plan.kinds[name]))

        def modulation(m):
            load(f"mod{m}a", 0, two_halves(slot(f"mod{m}a", 0), k_rows(dram("w_ada"), 512 * m, 512), 512))

        for m in range(4):
            modulation(m)
        w_in = dram("w_in")
        dense("uf", w_in, 1)
        for s in range(10):
            dense(f"in{s}", w_in, 1, 512 + 512 * s)
            if s % 2 == 0:
                modulation(4 + s // 2)
        load("fourier_out", 0, row_block(slot("fourier_out", 0), dram("w_fourier"), 0, 4))
        modulation(9)
        dense("conv_out", dram("w_conv_out"), 2)
        modulation(10)
        dense("w_o", dram("w_o"), 2)
        modulation(11)

        w_gate_e, w_up_e, w_down_e = dram("w_gate_e"), dram("w_up_e"), dram("w_down_e")

        def expert_slab(s, e):
            sl = slot("experts", s)
            if s < 8:
                w = w_gate_e if s < 4 else w_up_e
                dst = ring[sl][:, :].rearrange("p (k n) -> p k n", k=2)
                src = w[bass.ds(e * D + (s % 4) * 256, 256), :].rearrange("(k p) n -> p k n", p=P)
                return [(dst[:, k:k + 1, :], src[:, k:k + 1, :]) for k in range(2)]
            return row_block_at(sl, w_down_e, e * DE + (s % 4) * 512, 4)

        loop("experts", expert_slab)

        w_in2 = dram("w_in_2")
        dense("lru_x", w_in2, 2, 0)
        dense("lru_gate", w_in2, 2, 1024)
        dense("q", w_in2, 2, 2048)
        sl = slot("lru_ri", 0)
        gate_w = [dram(n).rearrange("(b c) d -> c b d", c=P) for n in ("lru_wa_2", "lru_wx_2")]
        load("lru_ri", 0, [(ring[sl][:, i * D:(i + 1) * D].rearrange("p (b d) -> p b d", b=8), gate_w[i])
                           for i in range(2)])
        dense("kv", w_in2, 1, 3072)
        dense("qi", w_in2, 1, 3584)
        dense("gate_a", w_in2, 2, 4168)
        dense("gate_b", w_in2, 2, 5192)
        dense("lru_out", dram("w_lru_br_2"), 2)
        dense("attn_out", dram("w_attn_br_2"), 2)
        dense("w_out2", dram("w_out_2"), 2)

        def ffn_slab(name, w_up, w_down, width):
            def slab(s, it):
                if s < 2:
                    return gate_up(slot(name, s), w_up, it * 512 + s * 256, width)
                return row_block_at(slot(name, s), w_down, it * 512, 4)
            return slab

        loop("ffn2", ffn_slab("ffn2", dram("w_up_2"), dram("w_down_2"), F2))
        w_ple_gate, w_ple_proj = dram("w_ple_gate_2"), dram("w_ple_proj_2")
        dense("ple", w_ple_gate, 2)
        load("ple", 2, row_block(slot("ple", 2), w_ple_proj, 0, 2))

        def ffn3(n, w_gu, w_down):
            loop(f"ffn3_{n}", ffn_slab(f"ffn3_{n}", w_gu, w_down, F3))
            end = f"ffn3_{n}_end"
            load(end, 0, gate_up(slot(end, 0), w_gu, F3 - 256, F3))
            load(end, 1, row_block(slot(end, 1), w_down, F3 - 256, 2))

        gu1, dn1, gu2, dn2 = (dram(n) for n in ("ffn1_w_gu_3", "ffn1_w_down_3", "ffn2_w_gu_3", "ffn2_w_down_3"))
        ffn3(0, gu1[0:D, :], dn1[0:F3, :])
        w_nsa = dram("nsa_w_in_3")
        dense("nsa_kv0", w_nsa, 1, 1024)
        dense("nsa_kv12", w_nsa, 2, 1536)
        dense("nsa_q", w_nsa, 2)
        sl = slot("cmp_hid", 0)
        load("cmp_hid", 0, [(ring[sl][:, i * 2048:(i + 1) * 2048].rearrange("p (m h) -> p m h", m=16),
                             dram(n).rearrange("(m p) h -> p m h", p=P))
                            for i, n in enumerate(("nsa_ck_w1_3", "nsa_cv_w1_3"))])
        dense("nsa_out", dram("nsa_w_out_3"), 2)
        ffn3(1, gu2[0:D, :], dn2[0:F3, :])
        ffn3(2, gu1[D:2 * D, :], dn1[F3:2 * F3, :])
        w_swa = dram("swa_w_in_3")
        load("swa_kv", 0, two_halves(slot("swa_kv", 0), k_rows(w_swa, 1024, 256), 256))
        dense("swa_q", w_swa, 2)
        dense("swa_out", dram("swa_w_out_3"), 2)
        ffn3(3, gu2[D:2 * D, :], dn2[F3:2 * F3, :])
        sp.wait_ge(S["out_ready"], TT)
        sp.dma_start(out.rearrange("(t p) d -> p t d", p=P), xn[:, :, :]).then_inc(S["out_stored"], 16)
        sp.wait_ge(S["out_stored"], 16)

    @block.tensor
    def _(pe):
        mm = nc.tensor.matmul

        def open_bank(name, i, it=0):
            w = plan.work(name, i)
            if w >= 4:
                pe.wait_ge(bank_copied[w % 4], w // 4 + it * (plan.kinds[name].count("W") // 4))
            return bank[4 + w % 4]

        def slab(name, s, it=0):
            return loaded(pe, name, s, it)

        def split_slab(name, s, it=0):
            pe.wait_ge(S["low_ready"], split_number(name, s, it))
            low = twins[f"ring{(plan.slab0[name] + s) % NSLOT}"]
            areas = split_areas(name, s)

            def at(c, n):
                start, area = [a for a in areas if a[0] <= c][-1]
                return area[:, c - start:c - start + n], low[:, c:c + n]
            return at

        def mm3(out_, lhs, rhs, start, stop):
            mm(out_, lhs[0], rhs[0], start=start, stop=False, skip_group_check=True)
            mm(out_, lhs[0], rhs[1], start=False, stop=False, skip_group_check=True)
            return mm(out_, lhs[1], rhs[0], start=False, stop=stop, skip_group_check=True)

        def h_parts(k, at=0, n=T):
            return h_high[:, k, at:at + n], h_low[:, k, at:at + n]

        def batch(ins):
            ins.then_inc(products_done, 1)

        def all_copied(name, idx):
            for i in idx:
                copied(pe, name, i)

        def normT(k, name):
            pe.wait_ge(S["xn_ready"], TT * k)
            for g in range(4):
                b = open_bank(name, g)
                for c in range(2):
                    for t in range(TT):
                        dst = b[:, c * T + t * P:c * T + (t + 1) * P]
                        chunk = slice((2 * g + c) * P, (2 * g + c + 1) * P)
                        if name == "norm1":
                            last = nc.tensor.transpose(dst, xn[:, t, chunk], ident)
                        else:
                            last = mm(dst, x[:, t, chunk], diag[:, t, :], start=True, stop=True)
                batch(last)

        def feature_major(name, b0, s, src, n_k, n_f=4, stride=512, c0=0):
            w = slab(name, s)
            for g in range(n_f // 2):
                b = open_bank(name, b0 + g)
                for f in range(2):
                    for k in range(n_k):
                        at = k * stride + c0 + (2 * g + f) * P
                        last = mm(b[:, f * T:(f + 1) * T], w[:, at:at + P], src[:, k, :],
                                  start=(k == 0), stop=(k == n_k - 1))
                batch(last)

        def feature_major3(name, b0, s, parts, n_k=DC, n_f=4, stride=512):
            w = split_slab(name, s)
            for g in range(n_f // 2):
                b = open_bank(name, b0 + g)
                for f in range(2):
                    for k in range(n_k):
                        last = mm3(b[:, f * T:(f + 1) * T], w(k * stride + (2 * g + f) * P, P), parts(k),
                                   k == 0, k == n_k - 1)
                batch(last)

        def token_major3(name, i, w, c0=256, n=256, stride=512):
            b = open_bank(name, i)
            for t in range(TT):
                for k in range(DC):
                    last = mm3(b[:, t * n:(t + 1) * n], h_parts(k, t * P, P), w(k * stride + c0, n),
                               k == 0, k == DC - 1)
            batch(last)

        def to_acc3(name, s, high, low):
            w = split_slab(name, s)
            for t in range(TT):
                tile = slice(t * P, (t + 1) * P)
                for k in range(DC):
                    last = mm3(acc[t][s][:, :], (high[:, k, tile], low[:, k, tile]), w(512 * k, 512),
                               k == 0, k == DC - 1)
            batch(last)

        def to_acc(name, s, src):
            w = slab(name, s)
            for t in range(TT):
                for k in range(DC):
                    last = mm(acc[t][s][:, :], src[:, k, t * P:(t + 1) * P], w[:, 512 * k:512 * k + 512],
                              start=(k == 0), stop=(k == DC - 1))
            batch(last)

        def clear_acc():
            for t in range(TT):
                for h in range(2):
                    mm(acc[t][h][:, :], zeros[:, 0:P], zeros[:, :], start=True, stop=False, skip_group_check=True)

        pe.wait_ge(fills_done, N_FILLS)
        pe.wait_ge(S["c_pad_ready"], 1)
        def modulation(m):
            w = slab(f"mod{m}a", 0)
            b = open_bank(f"mod{m}a", 0)
            for k in range(DC):
                j = 32 * (k % 4)
                last = mm(b[j:j + 32, :], c_pad[:, k, :], w[:, 512 * k:512 * k + 512], start=(k < 4),
                          stop=(k >= 4), tile_position=(0, j), skip_group_check=True)
            batch(last)

        def modulation_sum(m):
            copied(pe, f"mod{m}a", 0)
            b = open_bank(f"mod{m}b", 0)
            if m // 2 in (2, 5):
                last = mm(b[:, :], ones[:, :], mod_part[:, :], start=True, stop=True)
            else:
                for c in range(4):
                    last = mm(b[:, c:c + 1], mod_part[:, c * P:(c + 1) * P], ones[:, 0:1],
                              start=True, stop=True)
            batch(last)

        for m in range(4):
            modulation(m)
            modulation_sum(m)
        pe.wait_ge(first_loaded, N_FIRST)
        normT(1, "norm0")
        pe.wait_ge(S["h0_split"], 4)
        w = split_slab("uf", 0)
        for t in range(TT):
            b = open_bank("uf", t)
            for k in range(DC):
                last = mm3(b[:, :], h_parts(k, t * P, P), w(512 * k, 512), k == 0, k == DC - 1)
            batch(last)
        all_copied("uf", range(2))
        for g in range(4):
            b = open_bank("dft_a", g)
            for t in range(TT):
                last = mm(b[:, :], uf[:, t, g * P:(g + 1) * P], dft_seq[:, t, :], start=(t == 0), stop=(t == 1))
            batch(last)
        all_copied("dft_a", range(4))
        for i in range(2):
            b = open_bank("dft_b", i)
            for j in range(2):
                mm(b[:, j * T:(j + 1) * T], const("dft_cos"), dft_v[:, 2 * i + j, 0:T], start=True, stop=False)
                last = mm(b[:, j * T:(j + 1) * T], const("dft_sin"), dft_v[:, 2 * i + j, T:2 * T],
                          start=False, stop=True)
            batch(last)
        pe.wait_ge(inputs_loaded, N_INPUTS)
        for s in range(10):
            feature_major3(f"in{s}", 0, 0, h_parts)
            (modulation if s % 2 == 0 else modulation_sum)(4 + s // 2)
        all_copied("dft_b", range(2))
        feature_major3("fourier_out", 0, 0, lambda k: (y_high[:, k, :], y_low[:, k, :]), 4, n_f=8, stride=D)
        modulation(9)
        pe.wait_ge(S["conv_ready"], 1)
        for s in range(2):
            feature_major3("conv_out", 2 * s, s, lambda k: (bc_high[:, k, :], bc_low[:, k, :]))
        modulation_sum(9)
        modulation(10)
        pe.wait_ge(S["z_ready"], 4)
        for s in range(2):
            to_acc3("w_o", s, z_high, z_low)
        modulation_sum(10)
        modulation(11)
        modulation_sum(11)
        normT(2, "norm1")
        all_copied("norm1", range(4))
        b = open_bank("router", 0)
        for t in range(TT):
            for k in range(DC):
                last = mm(b[:, t * NE:(t + 1) * NE], hT[:, k, t * P:(t + 1) * P], w_router[:, k, :],
                          start=(k == 0), stop=(k == DC - 1))
        batch(last)
        pe.wait_ge(S["prob_ready"], 1)
        b = open_bank("probsT", 0)
        for t in range(TT):
            last = nc.tensor.transpose(b[0:NE, t * P:(t + 1) * P], prob[:, t, :], ident)
        batch(last)
        pe.wait_ge(S["mask_ready"], 1)
        b = open_bank("maskT", 0)
        for t in range(TT):
            last = nc.tensor.transpose(b[:, t * NE:(t + 1) * NE], mask[:, t * P:(t + 1) * P], ident[0:NE, 0:NE])
        batch(last)
        copied(pe, "maskT", 0)
        b = open_bank("slots", 0)
        mm(b[:, 0:NE], const("tri"), maskT[:, 0, :], start=True, stop=True)
        mm(b[:, NE:2 * NE], ones[:, :], maskT[:, 0, :], start=True, stop=False)
        batch(mm(b[:, NE:2 * NE], const("tri"), maskT[:, 1, :], start=False, stop=True))
        pe.wait_ge(S["sel_prob_ready"], TT)
        for i in range(8):
            b = open_bank("scatterT", i)
            for j in range(2):
                for t in range(TT):
                    last = nc.tensor.transpose(b[:, j * T + t * P:j * T + (t + 1) * P],
                                               sel_prob[:, t, 2 * i + j, :, :].rearrange("p g s -> p (g s)"), ident)
            batch(last)
        for c in range(DC):
            b = open_bank("gather", c)
            for t in range(TT):
                last = mm(b[:, :], xn[:, t, c * P:(c + 1) * P], sel[:, t, :, :].rearrange("p e s -> p (e s)"),
                          start=(t == 0), stop=(t == 1))
            batch(last)
        clear_acc()
        with pe.Fori(0, NE) as e:
            for part in range(2):
                b = open_bank("experts", 4 * part + 3, e)
                if part == 0:
                    pe.wait_ge(S["expert_staged"], 2 * e + 1)
                for m in range(4):
                    w = slab("experts", 4 * part + m, e)
                    for kk in range(2):
                        k = 2 * m + kk
                        for j in range(4):
                            last = mm(b[32 * j:32 * j + 32, :], xe_now[:, k, :],
                                      w[:, kk * DE + 512 * j:kk * DE + 512 * j + 512], start=(k == 0),
                                      stop=(k == DC - 1), tile_position=(0, 32 * j), skip_group_check=True)
                    batch(last)
            copied(pe, "experts", 7, e)
            b = open_bank("experts", 8, e)
            for q in range(4):
                last = nc.tensor.transpose(b[:, q * P:(q + 1) * P], e_h[:, q * P:(q + 1) * P], ident)
            batch(last)
            copied(pe, "experts", 8, e)
            b = open_bank("experts", 12, e)
            for m in range(4):
                w = slab("experts", 8 + m, e)
                for q in range(4):
                    for half in range(2):
                        j = 32 * (2 * half + q % 2)
                        last = mm(b[j:j + 32, :], e_hT[:, q * P + 32 * m:q * P + 32 * m + 32],
                                  w[:, q * D + 512 * half:q * D + 512 * half + 512], start=(m == 0 and q < 2),
                                  stop=(m == 3 and q >= 2), tile_position=(0, j), skip_group_check=True)
                batch(last)
            copied(pe, "experts", 12, e)
            pe.wait_ge(S["expert_staged"], 2 * e + 2)
            for t in range(TT):
                for half in range(2):
                    last = mm(acc[t][half][:, :], scat_now[64 * half:64 * half + 64, t * P:(t + 1) * P],
                              e_y[64 * half:64 * half + 64, :], start=False, stop=False,
                              tile_position=(64 * half, 0), skip_group_check=True)
            batch(last)

        def close_acc(name):
            for t in range(TT):
                for h in range(2):
                    last = mm(acc[t][h][:, :], zeros[:, 0:P], zeros[:, :], start=False, stop=True,
                              skip_group_check=True)
            batch(last)

        close_acc("experts_end")
        normT(3, "norm2")
        all_copied("norm2", range(4))
        for s in range(2):
            feature_major("lru_x", 2 * s, s, hT, DC)
        for s in range(2):
            feature_major("lru_gate", 2 * s, s, hT, DC)
        for s in range(2):
            feature_major("q", 2 * s, s, hT, DC)
        pe.wait_ge(S["ua_ready"], 1)
        w = slab("lru_ri", 0)
        for i in range(8):
            b = open_bank("lru_ri", i)
            for j in range(2):
                n = 2 * (i % 4) + j
                at = (i // 4) * D + n * P
                last = mm(b[:, j * T:(j + 1) * T], w[:, at:at + P], l_ua[:, n, :], start=True, stop=True)
            batch(last)
        feature_major("kv", 0, 0, hT, DC, n_f=2)
        w = ring[plan.slab0["kv"] % NSLOT]
        b = open_bank("kv", 1)
        for t in range(TT):
            for k in range(DC):
                last = mm(b[:, t * T:(t + 1) * T], hT[:, k, t * P:(t + 1) * P], w[:, 512 * k + 256:512 * k + 512],
                          start=(k == 0), stop=(k == DC - 1))
        batch(last)
        feature_major("qi", 0, 0, hT, DC)
        b = open_bank("kiwi", 0)
        for d in range(2):
            for k in range(DC):
                last = mm(b[64 * d:64 * d + 64, 0:T], w_kiwi[:, k, 0:64], hT[:, k, :], start=(k == 0),
                          stop=(k == DC - 1), tile_position=(0, 64 * d), skip_group_check=True)
        batch(last)
        b = open_bank("kiwi", 1)
        for t in range(TT):
            for k in range(DC):
                last = mm(b[:, t * 8:(t + 1) * 8], hT[:, k, t * P:(t + 1) * P], w_kiwi[:, k, 64:72],
                          start=(k == 0), stop=(k == DC - 1))
        batch(last)
        pe.wait_ge(S["rel_ready"], 1)
        for h in range(8):
            b = open_bank("bias", h)
            batch(mm(b[:, :], rel_rep[:, h, :], const("buckets")[0:32, :], start=True, stop=True))
        all_copied("q", range(4))
        copied(pe, "kv", 0)
        for i in range(5):
            b = open_bank("qk_ms", i)
            src = sq2[:, 2 * i:2 * i + 2, :].rearrange("p c t -> p (c t)") if i < 4 else sqk[:, :]
            batch(mm(b[:, :], ones_mean[:, :], src, start=True, stop=True))
        for s in range(2):
            feature_major("gate_a", 2 * s, s, hT, DC)
        all_copied("qi", range(2))
        all_copied("kiwi", range(1))
        for t in range(TT):
            for m in range(4):
                b = open_bank("score", 4 * t + m)
                batch(mm(b[:, :].rearrange("p (d s) -> p d s", d=2), qi[:, m, t * P:(t + 1) * P], ki[:, :, :],
                         start=True, stop=True))
        for s in range(2):
            feature_major("gate_b", 2 * s, s, hT, DC)
        pe.wait_ge(S["qk_ready"], 5)
        for t in range(TT):
            for m in range(4):
                b = open_bank("logits2", 4 * t + m)
                for d in range(2):
                    h = 2 * m + d
                    last = mm(b[:, d * T:(d + 1) * T], q2[:, h, t * P:(t + 1) * P], k2[:, h // 4, :],
                              start=True, stop=True)
                batch(last)
        pe.wait_ge(S["lru_ready"], 1)
        for s in range(2):
            feature_major("lru_out", 2 * s, s, l_ua, DC)
        pe.wait_ge(S["att_ready"], TT)

        def causal_blocks(b, p_of_t):
            nc.tensor.transpose(b[:, 0:P], p_of_t(0)[:, 0:P], ident)
            nc.tensor.transpose(b[:, P:2 * P], p_of_t(1)[:, 0:P], ident)
            return nc.tensor.transpose(b[:, 2 * P:3 * P], p_of_t(1)[:, P:2 * P], ident)

        for m in range(4):
            for d in range(2):
                b = open_bank("pv2", 3 * m + d)
                batch(causal_blocks(b, lambda t: att[t][:, 2 * m + d, :]))
            b = open_bank("pv2", 3 * m + 2)
            g = m // 2
            for d in range(2):
                copied(pe, "pv2", 3 * m + d)
                mm(b[:, d * T:(d + 1) * T], v2[:, 0, g * P:(g + 1) * P], pT2[d][:, 0:T], start=True, stop=False)
                last = mm(b[:, d * T + P:(d + 1) * T], v2[:, 1, g * P:(g + 1) * P], pT2[d][:, T:T + P],
                          start=False, stop=True)
            batch(last)
        all_copied("pv2", (2, 5, 8, 11))
        for s in range(2):
            feature_major("attn_out", 2 * s, s, o2, DC)
        pe.wait_ge(S["merged_ready"], 4)
        for s in range(2):
            to_acc("w_out2", s, merged)

        def gate_up_tile(name, i, w, j, it=0):
            b = open_bank(name, i, it)
            for part in range(2):
                for k in range(DC):
                    at = 512 * k + 256 * part + P * j
                    last = mm3(b[:, part * T:(part + 1) * T], w(at, P), h_parts(k), k == 0, k == DC - 1)
            batch(last)

        def down(name, n_f, w, it, stop, hids):
            for f in range(n_f):
                pe.wait_ge(S["hid_split"], hids + f + 1)
                for t in range(TT):
                    tile = slice(t * P, (t + 1) * P)
                    for h in range(2):
                        last = mm3(acc[t][h][:, :], (hid_high[:, f, tile], hid_low[:, f, tile]),
                                   w(f * D + 512 * h, 512), False, stop and f == n_f - 1)
            batch(last)

        def ffn(name, hids):
            with pe.Fori(0, plan.times[name]) as it:
                for s in range(2):
                    w = split_slab(name, s, it)
                    for j in range(2):
                        gate_up_tile(name, 2 * s + j, w, j, it)
                down(name, 4, split_slab(name, 2, it), it, False, hids + 4 * it)

        normT(4, "norm3")
        clear_acc()
        all_copied("norm3", range(4))
        ffn("ffn2", 0)
        close_acc("ffn2_end")
        normT(5, "norm4")
        all_copied("norm4", range(4))
        for h in range(2):
            w = split_slab("ple", h)
            for t in range(TT):
                b = open_bank("ple", 2 * h + t)
                for k in range(DC):
                    last = mm3(b[:, :], h_parts(k, t * P, P), w(512 * k, 512), k == 0, k == DC - 1)
                batch(last)
        w = slab("ple", 2)
        for h in range(2):
            for t in range(TT):
                b = open_bank("ple", 4 + 2 * h + t)
                for k in range(2):
                    last = mm(b[:, :], pT_in[:, k, t * P:(t + 1) * P], w[:, k * D + 512 * h:k * D + 512 * h + 512],
                              start=(k == 0), stop=(k == 1))
                batch(last)
        def ffn3(n, k):
            normT(k, f"ffnorm{n}")
            clear_acc()
            all_copied(f"ffnorm{n}", range(4))
            hids = hidden_tiles(n)
            ffn(f"ffn3_{n}", hids)
            end = f"ffn3_{n}_end"
            w = split_slab(end, 0)
            for j in range(2):
                gate_up_tile(end, j, w, j)
            down(end, 2, split_slab(end, 1), 0, True, hids + 4 * plan.times[f"ffn3_{n}"])

        def rope(name, i, src):
            b = open_bank(name, i)
            batch(mm(b[:, 0:src.shape[1]], const("rope_rot"), src, start=True, stop=True))

        def pairs(a, i, n=2):
            return a[:, 2 * i:2 * i + n, :].rearrange("p c t -> p (c t)")

        ffn3(0, 6)
        normT(7, "nsa_norm")
        all_copied("nsa_norm", range(4))
        feature_major3("nsa_kv0", 0, 0, h_parts)
        for s in range(2):
            feature_major3("nsa_kv12", 2 * s, s, h_parts, n_f=2)
            token_major3("nsa_kv12", 2 * s + 1, split_slab("nsa_kv12", s))
        b = open_bank("nsa_g", 0)
        for t in range(TT):
            for k in range(DC):
                for part in range(2):
                    last = mm(b[:, t * 48:(t + 1) * 48], h_parts(k, t * P, P)[part].bitcast(fp32),
                              w_nsa_gate[:, k, :], start=(k + part == 0), stop=(k + part == DC))
        batch(last)
        all_copied("nsa_kv0", range(2))
        all_copied("nsa_kv12", range(4))
        for i in range(3):
            rope("nsa_rope_k", i, pairs(kraw, i))
        for s in range(2):
            feature_major3("nsa_q", 2 * s, s, h_parts)
        all_copied("nsa_q", range(4))
        for i in range(4):
            rope("nsa_rope", i, pairs(q3, i))
        pe.wait_ge(S["cmp_x_ready"], 1)
        w = slab("cmp_hid", 0)
        for i in range(2):
            b = open_bank("cmp_hid", i)
            for m in range(16):
                at = i * 2048 + m * P
                last = mm(b[:, 0:60], w[:, at:at + P], xb[i][:, m, :, :].rearrange("p g b -> p (g b)"),
                          start=(m == 0), stop=(m == 15))
            batch(last)
        all_copied("cmp_hid", range(2))
        b = open_bank("cmp_kv", 0)
        for d in range(2):
            last = mm(b[64 * d:64 * d + 64, 0:60], ck_w2[:, :], hid_c[0], start=True, stop=True,
                      tile_position=(0, 64 * d), skip_group_check=True)
        batch(last)
        b = open_bank("cmp_kv", 1)
        for g in range(4):
            last = mm(b[0:NB, g * 64:(g + 1) * 64], hid_c[1][:, g * NB:(g + 1) * NB], cv_w2[:, :],
                      start=True, stop=True)
        batch(last)
        all_copied("cmp_kv", range(2))
        pe.wait_ge(S["rope_ready"], 7)
        for t in range(TT):
            b = open_bank("cmp_s", t)
            for m in range(8):
                last = mm(b[:, 2 * m * NB:(2 * m + 2) * NB], q3[:, m, t * P:(t + 1) * P], kc[:, :, m // 2, :],
                          start=True, stop=True)
            batch(last)

        def masked_scores(b, m, t, keys, neg):
            both = b[:, :].rearrange("p (d s) -> p d s", d=2)
            mm(both, q3[:, m, t * P:(t + 1) * P], keys, start=True, stop=False)
            batch(mm(both, ident16[:, :], wide(neg[:, t:t + 1, :], 1, 2), start=False, stop=True))

        def nsa_scores(m):
            for br in range(2):
                for t in range(TT):
                    s = 2 * br + t
                    if m:
                        pe.wait_ge(S["exp3_done"], 4 * (m - 1) + s + 1)
                    masked_scores(bank[s], m, t, kd[br][:, m // 2, :, :], causal16)

        pe.wait_ge(S["masks16_ready"], 2)
        nsa_scores(0)
        for m in range(8):
            g = m // 2
            n = pair_rest(m, 4, 6)
            if m < 7:
                nsa_scores(m + 1)
            for br in range(2):
                pe.wait_ge(S["p3_ready"], 4 * m + 2 * br + 2)
                for d in range(2):
                    b = open_bank("nsa_heads", n + 2 * br + d)
                    batch(causal_blocks(b, lambda t: p3[4 * (m % 2) + 2 * br + t][:, d, :]))
            if m == 0:
                pe.wait_ge(S["cmp_ready"], 1)
            b = open_bank("nsa_heads", n + 4)
            for d in range(2):
                for t in range(TT):
                    last = nc.tensor.transpose(b[0:NB, d * T + t * P:d * T + (t + 1) * P], pc[:, t, 2 * m + d, :],
                                               ident)
            batch(last)
            b = open_bank("nsa_heads", n + 5)
            for i in range(5):
                copied(pe, "nsa_heads", n + i)
            for d in range(2):
                o = b[64 * d:64 * d + 64, 0:T]
                o_late = b[64 * d:64 * d + 64, P:T]
                k = dict(tile_position=(0, 64 * d), skip_group_check=True)
                mm(o, vc[:, g * 64:(g + 1) * 64], pcT[:, d * T:(d + 1) * T], start=True, stop=False, **k)
                for br in range(2):
                    pt = pT3[2 * br + d]
                    mm(o, v3[:, br, 0, g * 64:(g + 1) * 64], pt[:, 0:T], start=False, stop=False, **k)
                    last = mm(o_late, v3[:, br, 1, g * 64:(g + 1) * 64], pt[:, T:T + P], start=False,
                              stop=(br == 1), **k)
            batch(last)
        for m in range(8):
            copied(pe, "nsa_heads", pair_rest(m, 4, 6) + 5)
        for s in range(2):
            to_acc3("nsa_out", s, o_high, o_low)
        ffn3(1, 8)
        ffn3(2, 9)
        normT(10, "swa_norm")
        all_copied("swa_norm", range(4))
        w = split_slab("swa_kv", 0)
        b = open_bank("swa_kv", 0)
        for k in range(DC):
            mm3(b[:, 0:T], w(256 * k, P), h_parts(k), k == 0, k == DC - 1)
        for t in range(TT):
            for k in range(DC):
                last = mm3(b[:, T + t * P:T + (t + 1) * P], h_parts(k, t * P, P), w(256 * k + P, P),
                           k == 0, k == DC - 1)
        batch(last)
        copied(pe, "swa_kv", 0)
        rope("swa_rope_k", 0, k4)
        for s in range(2):
            feature_major3("swa_q", 2 * s, s, h_parts)
        all_copied("swa_q", range(4))
        for i in range(4):
            rope("swa_rope", i, pairs(q3, i))
        pe.wait_ge(S["rope_ready"], 12)
        def swa_scores(m):
            for t in range(TT):
                if m >= 2:
                    pe.wait_ge(S["exp3_done"], 32 + 2 * (m - 2) + t + 1)
                masked_scores(bank[2 * (m % 2) + t], m, t, kd4[:, m // 4, :, :], window16)

        swa_scores(0)
        for m in range(8):
            n, g = pair_rest(m, 2, 3), m // 4
            if m < 7:
                swa_scores(m + 1)
            pe.wait_ge(S["p3_ready"], 32 + 2 * m + 2)
            for d in range(2):
                b = open_bank("swa_heads", n + d)
                batch(causal_blocks(b, lambda t: p3[2 * (m % 2) + t][:, d, :]))
            b = open_bank("swa_heads", n + 2)
            for d in range(2):
                copied(pe, "swa_heads", n + d)
                k = dict(tile_position=(0, 64 * d), skip_group_check=True)
                pt = pT3[d]
                mm(b[64 * d:64 * d + 64, 0:T], v4[:, 0, g * 64:(g + 1) * 64], pt[:, 0:T], start=True, stop=False, **k)
                last = mm(b[64 * d:64 * d + 64, P:T], v4[:, 1, g * 64:(g + 1) * 64], pt[:, T:T + P],
                          start=False, stop=True, **k)
            batch(last)
        for m in range(8):
            copied(pe, "swa_heads", pair_rest(m, 2, 3) + 2)
        for s in range(2):
            to_acc3("swa_out", s, o_high, o_low)
        ffn3(3, 11)

    @block.scalar
    def _(act):
        run = nc.scalar.activation

        def copy_out(name, i, dst, n=512, scale=1.0, rows_=P, it=0):
            filled(act, name, i, it)
            frees(run(dst, work_bank(name, i)[0:rows_, 0:n], ACT.Copy, scale=scale), name, i)

        def squares(k):
            for t in range(TT):
                if k:
                    act.wait_ge(S["x_new"], TT * (k - 1) + t + 1)
                run(junk[:, t, :], x[:, t, :], ACT.Square, accum_out=ss[:, t:t + 1]).then_inc(S["squares_done"], 1)

        def high(name, s, it=0):
            j = split_number(name, s) - 1
            if plan.times[name] == 1 and j >= 2 and not name.startswith("ffn"):
                act.wait_ge(products_done, plan.split_end[j - 2])
            w = loaded(act, name, s, it)
            for at, area in halves(name, s):
                run(area[:, :], w[:, at:at + area.shape[1]], ACT.Copy).then_inc(S["high_ready"], 1)

        def norm_out_split(name, gain):
            for g in range(4):
                filled(act, name, g)
                for c in range(2):
                    k = 2 * g + c
                    ins = run(h_high[:, k, :], work_bank(name, g)[:, c * T:(c + 1) * T], ACT.Identity,
                              scale=gain[:, k:k + 1])
                ins.then_inc(S["high_norm"], 1)

        def norm_out(name, gain, shift=None):
            for g in range(4):
                filled(act, name, g)
                for c in range(2):
                    k = 2 * g + c
                    args = {} if shift is None else {"bias": shift[:, k:k + 1]}
                    ins = run(hT[:, k, :], work_bank(name, g)[:, c * T:(c + 1) * T], ACT.Identity,
                              scale=gain[:, k:k + 1], **args)
                frees(ins, name, g)

        def two(name, i, fn):
            filled(act, name, i)
            for f in range(2):
                ins = fn(f, work_bank(name, i)[:, f * T:(f + 1) * T])
            frees(ins, name, i)

        act.wait_ge(cols_loaded, 16)
        act.wait_ge(fills_done, N_FILLS)
        run(c_act, col("c", 0, 8), ACT.Silu).then_inc(S["c_act_ready"], 1)

        def modulation(m):
            copy_out(f"mod{m}a", 0, mod_part[:, :])

        for m in range(2):
            modulation(m)
        act.wait_ge(first_loaded, N_FIRST)
        squares(0)
        for m in range(2, 4):
            modulation(m)
        high("uf", 0)
        act.wait_ge(S["mod_ready"], 1)
        for g in range(4):
            filled(act, "norm0", g)
            for c in range(2):
                k = 2 * g + c
                for dst in (hT[:, k, :], h_high[:, k, :]):
                    ins = run(dst, work_bank("norm0", g)[:, c * T:(c + 1) * T], ACT.Identity,
                              scale=g_mix[:, k:k + 1], bias=modc[:, k:k + 1])
            frees(ins, "norm0", g)
        act.wait_ge(S["masks16_ready"], 2)
        high("in0", 0)
        for t in range(TT):
            copy_out("uf", t, uf[:, t, :])
        for g in range(4):
            copy_out("dft_a", g, dft_v[:, g, :])
        for i in range(2):
            filled(act, "dft_b", i)
            run(y_high[:, 2 * i:2 * i + 2, :].rearrange("p g t -> p (g t)"), work_bank("dft_b", i)[:, :],
                ACT.Copy).then_inc(S["y_high"], 1)
        act.wait_ge(inputs_loaded, N_INPUTS)
        for s in range(10):
            if s < 9:
                high(f"in{s + 1}", 0)
            else:
                high("fourier_out", 0)
            for half in range(2):
                if s < 4:
                    at = 4 * (s % 2) + 2 * half
                    dst = (f_v, f_b)[s // 2][:, at:at + 2, :]
                    copy_out(f"in{s}", half, dst.rearrange("p g t -> p (g t)"))
                if s >= 6:
                    i = 2 * (s - 6) + half
                    dst = (f_ga, f_gb)[i // 4]
                    two(f"in{s}", half, lambda f, b: run(dst[:, 2 * (i % 4) + f, :], b, ACT.Sigmoid,
                                                         bias=col("b_gate", 2 * i + f)))
            if s % 2 == 0:
                modulation(4 + s // 2)
        high("conv_out", 0)
        modulation(9)
        high("conv_out", 1)
        high("w_o", 0)
        high("w_o", 1)
        modulation(10)
        modulation(11)
        act.wait_ge(S["mod_ready"], 2)
        squares(1)
        norm_out("norm1", g_moe, modc[:, 24:32])
        act.wait_ge(S["logit_ready"], 1)
        run(logit[:, :, :], logit[:, :, :], ACT.Exp).then_inc(S["exp_ready"], 1)
        for i in range(8):
            copy_out("scatterT", i, scat[:, 2 * i:2 * i + 2, :].rearrange("p e t -> p (e t)"))
        for c in range(DC):
            filled(act, "gather", c)
            frees(run(xeT[:, c, :], work_bank("gather", c)[:, :], ACT.Identity, scale=g_moe[:, c:c + 1],
                      bias=modc[:, 24 + c:25 + c]), "gather", c)
        with act.Fori(0, NE) as e:
            filled(act, "experts", 3, e)
            frees(run(e_act, work_bank("experts", 3)[:, :], ACT.Silu), "experts", 3)
            copy_out("experts", 8, e_hT, it=e)
            copy_out("experts", 12, e_y, it=e)
        squares(2)
        squares(3)
        norm_out("norm2", col("mix_norm_2", 0, 8))
        act.wait_ge(S["lam_exp_in"], 1)
        run(sp_a, sp_a, ACT.Exp).then_inc(S["lam_exp_out"], 1)
        for i in range(4):
            copy_out("lru_x", i, l_t[:, 2 * i:2 * i + 2, :].rearrange("p g t -> p (g t)"))
        for i in range(4):
            copy = l_g[:, 2 * i:2 * i + 2, :].rearrange("p g t -> p (g t)")
            filled(act, "lru_gate", i)
            frees(run(copy, work_bank("lru_gate", i)[:, :], ACT.Gelu_apprx_tanh), "lru_gate", i)
        for i in range(4):
            filled(act, "q", i)
            run(q2[:, 2 * i:2 * i + 2, :].rearrange("p g t -> p (g t)"), work_bank("q", i)[:, :], ACT.Copy)
            frees(run(sq2[:, 2 * i:2 * i + 2, :].rearrange("p g t -> p (g t)"), work_bank("q", i)[:, :],
                      ACT.Square), "q", i)
        for i in range(8):
            dst, bias = ((l_a, "lru_ba_2"), (l_i, "lru_bx_2"))[i // 4]
            two("lru_ri", i, lambda f, b: run(dst[:, 2 * (i % 4) + f, :], b, ACT.Sigmoid,
                                              bias=col(bias, 2 * (i % 4) + f)))
        for i in range(4):
            copied(act, "lru_ri", i)
        act.wait_ge(S["sp_ready"], 1)
        for c in range(DC):
            ins = run(l_t[:, c, :], l_a[:, c, :], ACT.Tanh, scale=sp8[:, c:c + 1])
        ins.then_inc(S["tanh_done"], 1)
        for c in range(DC):
            ins = run(l_a[:, c, :], l_a[:, c, :], ACT.Exp, scale=nsp8[:, c:c + 1])
        ins.then_inc(S["decay_done"], 1)
        act.wait_ge(S["mult_in"], 1)
        run(l_t[:, :, :], l_t[:, :, :], ACT.Sqrt, scale=2.0).then_inc(S["mult_out"], 1)
        filled(act, "kv", 0)
        run(k2[:, :, :].rearrange("p g t -> p (g t)"), work_bank("kv", 0)[:, :], ACT.Copy)
        frees(run(sqk[:, :], work_bank("kv", 0)[:, :], ACT.Square), "kv", 0)
        copy_out("kv", 1, v2[:, :, :].rearrange("p t n -> p (t n)"))
        for i in range(2):
            copy_out("qi", i, qi[:, 2 * i:2 * i + 2, :].rearrange("p g t -> p (g t)"))
        filled(act, "kiwi", 0)
        act.wait_ge(S["zeroed"], 1)
        for d in range(2):
            half = slice(64 * d, 64 * d + 64)
            ins = run(ki[half, d, :], work_bank("kiwi", 0)[half, 0:T], ACT.Copy)
        frees(ins, "kiwi", 0)
        copy_out("kiwi", 1, wi[:, :, :].rearrange("p t h -> p (t h)"), n=16, scale=8 ** -0.5)
        for h in range(8):
            copy_out("bias", h, bias_row[:, h, :])
        for i in range(5):
            act.wait_ge(S["msq_ready"], i + 1)
            run(msq[i % 2][:, :], msq[i % 2][:, :], ACT.Sqrt).then_inc(S["rsq_ready"], 1)
        act.wait_ge(S["scan_done"], 1)
        for i in range(4):
            filled(act, "gate_a", i)
            frees(run(l_a[:, 2 * i:2 * i + 2, :].rearrange("p g t -> p (g t)"), work_bank("gate_a", i)[:, :],
                      ACT.Sigmoid), "gate_a", i)
        for i in range(8):
            filled(act, "score", i)
            if i >= 2:
                act.wait_ge(S["relu_used"], i - 1)
            else:
                filled(act, "qk_ms", 3)
            frees(run(relu_s[i % 2], work_bank("score", i)[:, :], ACT.Relu, scale=64 ** -0.5), "score", i)
        for i in range(4):
            filled(act, "gate_b", i)
            frees(run(l_i[:, 2 * i:2 * i + 2, :].rearrange("p g t -> p (g t)"), work_bank("gate_b", i)[:, :],
                      ACT.Sigmoid), "gate_b", i)
        for t in range(TT):
            act.wait_ge(S["att_in"], t + 1)
            for h in range(8):
                ins = run(att[t][:, h, :], att[t][:, h, :], ACT.Exp, bias=nm2[:, t, h:h + 1],
                          accum_out=rs2[:, t, h:h + 1])
            ins.then_inc(S["att_exp"], 1)
        for m in range(4):
            for d in range(2):
                copy_out("pv2", 3 * m + d, pT2[d][:, 0:384], n=384)
            copy_out("pv2", 3 * m + 2, o2[:, 2 * m:2 * m + 2, :].rearrange("p g t -> p (g t)"))
        filled(act, "attn_out", 3)
        high("ffn2", 0)
        squares(4)
        norm_out_split("norm3", col("ffn_norm_2", 0, 8))
        with act.Fori(0, plan.times["ffn2"]) as it:
            for b in range(4):
                if b % 2 == 0:
                    high("ffn2", 1 + b // 2, it)
                act.wait_ge(S["conv_in"], b + 1 + 4 * it)
                run(f_act[b % 2], f_conv[b % 2], ACT.Gelu_apprx_tanh).then_inc(S["gelu_done"], 1)
            high("ffn2", 0, it + 1)
        squares(5)
        norm_out_split("norm4", col("ple_norm_2", 0, 8))
        high("ple", 1)
        for i in range(4):
            filled(act, "ple", i)
            frees(run(p_gate[:, i // 2, i % 2, :], work_bank("ple", i)[:, :], ACT.Sigmoid), "ple", i)

        def ffn3(n, k, before, i):
            filled(act, before, i)
            high(f"ffn3_{n}", 0)
            squares(k)
            norm_out_split(f"ffnorm{n}", col("ffn1_norm_3" if n % 2 == 0 else "ffn2_norm_3", 8 * (n // 2), 8))
            name = f"ffn3_{n}"

            def gates(name, n_b, it, before, before_it):
                for b in range(n_b):
                    if b % 2 == 0:
                        high(name, 1 + b // 2, it)
                    filled(act, name, b, it)
                    if b < 2:
                        copied(act, before, b + 2, before_it)
                    else:
                        copied(act, name, b - 2, it)
                    run(f_act[b % 2], work_bank(name, b)[:, 0:T], ACT.Silu).then_inc(S["gelu_done"], 1)

            with act.Fori(0, plan.times[name]) as it:
                gates(name, 4, it, name, it - 1)
                high(name, 0, it + 1)
            gates(name + "_end", 2, 0, name, plan.times[name] - 1)

        ffn3(0, 6, "ple", 1)
        filled(act, "ffn3_0_end", 1)
        high("nsa_kv0", 0)
        squares(7)
        norm_out_split("nsa_norm", col("mix_norm_3", 0, 8))
        high("nsa_kv12", 0)
        copy_out("nsa_kv0", 0, kraw[:, 0:2, :].rearrange("p g t -> p (g t)"))
        copy_out("nsa_kv0", 1, vraw[:, :, :].rearrange("p g t -> p (g t)"))
        high("nsa_kv12", 1)
        for b in range(2):
            if b:
                high("nsa_q", 0)
            copy_out("nsa_kv12", 2 * b, kraw[:, 2 + 2 * b:4 + 2 * b, :].rearrange("p g t -> p (g t)"))
            copy_out("nsa_kv12", 2 * b + 1, v3[:, b, :, :].rearrange("p t n -> p (t n)"))
        filled(act, "nsa_g", 0)
        frees(run(gate3[:, :, :, :].rearrange("p t b h -> p (t b h)"), work_bank("nsa_g", 0)[:, 0:96], ACT.Sigmoid),
              "nsa_g", 0)
        high("nsa_q", 1)
        for i in range(4):
            copy_out("nsa_q", i, q3[:, 2 * i:2 * i + 2, :].rearrange("p g t -> p (g t)"))
        for i in range(2):
            filled(act, "cmp_hid", i)
            frees(run(hid_c[i], work_bank("cmp_hid", i)[:, 0:60], ACT.Gelu_apprx_tanh), "cmp_hid", i)
        filled(act, "cmp_kv", 0)
        act.wait_ge(S["zeroed"], 2)
        for d in range(2):
            half = slice(64 * d, 64 * d + 64)
            ins = run(kc[half, d, :, :].rearrange("p g b -> p (g b)"), work_bank("cmp_kv", 0)[half, 0:60], ACT.Copy)
        frees(ins, "cmp_kv", 0)
        copy_out("cmp_kv", 1, vc, n=T, rows_=NB)
        act.wait_ge(S["cmp_in"], 1)
        run(pc[:, :, :, :], pc[:, :, :, :], ACT.Exp).then_inc(S["cmp_exp"], 1)

        def exps(b, slot, n):
            act.wait_ge(S["max3_ready"], n)
            for d in range(2):
                ins = run(p3[slot][:, d, :], b[:, d * T:(d + 1) * T], ACT.Exp,
                          scale=64 ** -0.5, bias=nm3[slot][:, d:d + 1], accum_out=rs3[slot][:, d:d + 1])
            ins.then_inc(S["exp3_done"], 1)

        for s in range(4):
            exps(bank[s], s, s + 1)
        for m in range(8):
            n = pair_rest(m, 4, 6)
            for s in range(4):
                copy_out("nsa_heads", n + s, pT3[s][:, :], n=384)
            copy_out("nsa_heads", n + 4, pcT, rows_=NB)
            if m < 7:
                for s in range(4):
                    exps(bank[s], 4 * ((m + 1) % 2) + s, 4 * (m + 1) + s + 1)
            filled(act, "nsa_heads", n + 5)
            run(o_high[:, m, :], work_bank("nsa_heads", n + 5)[:, 0:T], ACT.Copy).then_inc(S["o_high"], 1)
            if m >= 6:
                high("nsa_out", m - 6)
        ffn3(1, 8, "nsa_heads", pair_rest(7, 4, 6) + 5)
        ffn3(2, 9, "ffn3_1_end", 1)
        filled(act, "ffn3_2_end", 1)
        high("swa_kv", 0)
        squares(10)
        norm_out_split("swa_norm", col("mix_norm_3", 8, 8))
        high("swa_q", 0)
        filled(act, "swa_kv", 0)
        run(k4, work_bank("swa_kv", 0)[:, 0:T], ACT.Copy)
        frees(run(v4[:, :, :].rearrange("p t n -> p (t n)"), work_bank("swa_kv", 0)[:, T:2 * T], ACT.Copy),
              "swa_kv", 0)
        high("swa_q", 1)
        for i in range(4):
            copy_out("swa_q", i, q3[:, 2 * i:2 * i + 2, :].rearrange("p g t -> p (g t)"))

        def swa_exps(m):
            for t in range(TT):
                slot = 2 * (m % 2) + t
                n = 32 + 2 * m + t + 1
                act.wait_ge(S["max3_ready"], n)
                run(sk[slot], sk[slot], ACT.Exp)
                exps(bank[slot], slot, n)

        swa_exps(0)
        for m in range(8):
            n = pair_rest(m, 2, 3)
            for d in range(2):
                copy_out("swa_heads", n + d, pT3[d][:, :], n=384)
            if m < 7:
                swa_exps(m + 1)
            filled(act, "swa_heads", n + 2)
            run(o_high[:, m, :], work_bank("swa_heads", n + 2)[:, 0:T], ACT.Copy).then_inc(S["o_high"], 1)
            if m >= 6:
                high("swa_out", m - 6)
        ffn3(3, 11, "swa_heads", pair_rest(7, 2, 3) + 2)
        squares(12)

    @block.gpsimd
    def _(pool):
        pool.dma_start(cols[:, :], dram("cols")).then_inc(cols_loaded, 16)
        fills = [(c_pad[:, :, :], 0.0), (ones[:, :], 1.0), (ones_mean[:, :], 1.0 / P), (zeros[:, :], 0.0),
                 (neg_half[:, :], -0.5)]
        assert len(fills) == N_FILLS
        for dst, v in fills:
            nc.gpsimd.memset(dst, v).then_inc(fills_done, 1)
        first = [(x[:, :, :], dram("x").rearrange("(t p) d -> p t d", p=P)), (consts[:, :], dram("consts")),
                 (masks_in, dram("masks"))]
        assert 16 * len(first) == N_FIRST
        for dst, src in first:
            pool.dma_start(dst, src).then_inc(first_loaded, 16)
        loads = [(rows[:, :], wide(dram("rows"), 0, P)),
                 (w_router[:, :, :], dram("w_router").rearrange("(k p) n -> p k n", p=P)),
                 (w_kiwi[:, :, :], dram("w_in_2")[:, 4096:4168].rearrange("(k p) n -> p k n", p=P)),
                 (w_nsa_gate[:, :, :], dram("nsa_w_in_3")[:, 2560:2608].rearrange("(k p) n -> p k n", p=P)),
                 (ck_w2[:, :], dram("nsa_ck_w2_3")), (cv_w2[:, :], dram("nsa_cv_w2_3")),
                 (pT_in[:, :, :], dram("pT").rearrange("(k p) t -> p k t", p=P)),
                 (rel_in[:, :], dram("rel_bias_2"))]
        assert 16 * len(loads) == N_INPUTS
        for dst, src in loads:
            pool.dma_start(dst, src).then_inc(inputs_loaded, 16)
        pool.wait_ge(fills_done, N_FILLS)

        def rsqrt(k):
            pool.wait_ge(S["mean_ready"], k + 1)
            nc.gpsimd.tensor_tensor(out=rstd, in0=ms, in1=neg_half[:, 0:TT], op=ALU.pow).then_inc(S["rstd_ready"], 1)

        rsqrt(0)
        rsqrt(1)
        for c in range(DC):
            copied(pool, "gather", c)
        for i in range(8):
            copied(pool, "scatterT", i)
        with pool.Fori(0, NE) as e:
            body = len(plan.kinds["experts"])
            pool.wait_ge(products_done, plan.done("experts", 7) - body + e * body)
            nc.gpsimd.tensor_copy(xe_now[:, :, :], xeT[:, :, bass.ds(e * CAP, CAP)]).then_inc(S["expert_staged"], 1)
            pool.wait_ge(products_done, plan.batch0["experts"] + e * body)
            nc.gpsimd.tensor_copy(scat_now, AC[:, bass.ds(e * T, T)]).then_inc(S["expert_staged"], 1)
        rsqrt(2)
        rsqrt(3)
        for h in range(8):
            copied(pool, "bias", h)
        pool.dma_start(skew.rearrange("(p n) -> p n", p=P), bias_row[:, :, :].rearrange("p h j -> p (h j)"))\
            .then_inc(S["rows_out"], 16)
        pool.wait_ge(S["rows_out"], 16)
        for t in range(TT):
            src = bass.AP(tensor=skew.tensor, offset=T - 1 - P * t, ap=[[8 * 512 - 1, P], [512, 8], [1, T]])
            pool.dma_start(bias2[:, t, :, :], src).then_inc(S["bias_in"], 16)
        pool.wait_ge(S["x_new"], TT)
        pool.dma_start(row("gate_m"), wide(dram("final_norm"), 0, P)).then_inc(S["final_row_in"], 16)
        for k in range(4, len(NORMS)):
            rsqrt(k)

    @block.vector
    def _(dve):
        v = nc.vector
        link = Chain(dve, "dve")

        def mean(k):
            dve.wait_ge(S["squares_done"], TT * (k + 1))
            v.tensor_scalar(ms, ss, 1.0 / D, EPS, ALU.mult, ALU.add).then_inc(S["mean_ready"], 1)
            dve.wait_ge(S["rstd_ready"], k + 1)

        def normalise(k, rows=False):
            mean(k)
            for t in range(TT):
                dst, src = (xn, x[:, t, :]) if rows else (diag, ident)
                v.tensor_scalar(dst[:, t, :], src, rstd[:, t:t + 1], None, ALU.mult).then_inc(S["xn_ready"], 1)

        def low(name, s, it=0):
            slot = (plan.slab0[name] + s) % NSLOT
            for half, (at, area) in enumerate(halves(name, s)):
                dve.wait_ge(S["high_ready"], 2 * split_number(name, s, it) - 1 + half)
                part = slice(at, at + area.shape[1])
                ins = v.tensor_tensor(twins[f"ring{slot}"][:, part], ring[slot][:, part], area[:, :].bitcast(fp32),
                                      ALU.subtract)
            ins.then_inc(S["low_ready"], 1)

        def low_norm(name, n, gain):
            for g in range(4):
                dve.wait_ge(S["high_norm"], 4 * (n - 1) + g + 1)
                for c in range(2):
                    k = 2 * g + c
                    ins = v.scalar_tensor_tensor(h_low[:, k, :], work_bank(name, g)[:, c * T:(c + 1) * T],
                                                 gain[:, k:k + 1], h_high[:, k, :].bitcast(fp32),
                                                 ALU.mult, ALU.subtract)
                frees(ins, name, g)

        def hidden(name, b, it):
            up, f_ = work_bank(name, b)[:, T:2 * T], f_act[b % 2]
            v.tensor_tensor(hid_high[:, b, :], up, f_, ALU.mult)
            frees(v.tensor_tensor(hid[:, b, :], up, f_, ALU.mult), name, b)
            copied(dve, name, b, it)
            v.tensor_tensor(hid_low[:, b, :], hid[:, b, :], hid_high[:, b, :].bitcast(fp32), ALU.subtract)\
                .then_inc(S["hid_split"], 1)

        def x_updated(ins):
            ins.then_inc(S["x_new"], 1)

        dve.wait_ge(cols_loaded, 16)
        dve.wait_ge(fills_done, N_FILLS)
        dve.wait_ge(S["c_act_ready"], 1)
        v.tensor_copy(c_pad[:, :, 0:1], c_act[:, :].rearrange("p (k a) -> p k a", a=1)).then_inc(S["c_pad_ready"], 1)
        dve.wait_ge(first_loaded, N_FIRST)
        normalise(0)

        def modulation(m):
            name, i = f"mod{m}b", 0
            filled(dve, name, i)
            b = work_bank(name, i)
            if m // 2 in (2, 5):
                dst = row("gate_m" if m < 6 else "gate_f")[:, (m % 2) * 512:(m % 2) * 512 + 512]
                frees(v.tensor_tensor(dst, b[:, :], dst, ALU.add), name, i)
            else:
                frees(v.tensor_tensor(modc[:, 4 * m:4 * m + 4], b[:, 0:4], col("b_ada", 4 * m, 4), ALU.add), name, i)

        def modulated_gain(dst, ms_, scale_at, g):
            for m in ms_:
                copied(dve, f"mod{m}b", 0)
            v.scalar_tensor_tensor(dst, modc[:, scale_at:scale_at + 8], 1.0, col(g, 0, 8), ALU.add, ALU.mult)\
                .then_inc(S["mod_ready"], 1)

        for m in range(4):
            modulation(m)
        modulated_gain(g_mix, range(4), 8, "g_norm_mix")
        low("uf", 0)
        for dst, src in ((ident16[:, :], ident), (masks16[:, :, :].rearrange("p a s -> p (a s)"), masks_in)):
            v.tensor_copy(dst, src).then_inc(S["masks16_ready"], 1)
        for g in range(4):
            copied(dve, "norm0", g)
            two = slice(2 * g, 2 * g + 2)
            v.tensor_tensor(h_low[:, two, :], hT[:, two, :], h_high[:, two, :].bitcast(fp32), ALU.subtract)\
                .then_inc(S["h0_split"], 1)
        low("in0", 0)
        for i in range(2):
            dve.wait_ge(S["y_high"], i + 1)
            two = slice(2 * i, 2 * i + 2)
            frees(v.tensor_tensor(y_low[:, two, :].rearrange("p g t -> p (g t)"), work_bank("dft_b", i)[:, :],
                                  y_high[:, two, :].rearrange("p g t -> p (g t)").bitcast(fp32), ALU.subtract),
                  "dft_b", i)
        dve.wait_ge(inputs_loaded, N_INPUTS)
        for s in range(8):
            low(f"in{s + 1}", 0)
            if s in (4, 5):
                for half in range(2):
                    i = 2 * (s - 4) + half
                    filled(dve, f"in{s}", half)
                    copied(dve, f"in{s - 4}", half)
                    frees(v.tensor_tensor(f_cv[:, 2 * i:2 * i + 2, :].rearrange("p c t -> p (c t)"),
                                          work_bank(f"in{s}", half)[:, :],
                                          f_v[:, 2 * i:2 * i + 2, :].rearrange("p c t -> p (c t)"), ALU.mult),
                          f"in{s}", half)
            if s % 2:
                modulation(4 + s // 2)
        low("in9", 0)
        for half in range(2):
            for s in (2, 3, 4, 5):
                copied(dve, f"in{s}", half)
        link(v.tensor_tensor(f_bc[:, :, :], f_cv[:, :, :],
                             wide(col("w_conv", DC, DC).rearrange("p (c a) -> p c a", a=1), 2, T), ALU.mult))
        for c in range(DC):
            ins = v.scalar_tensor_tensor(f_bc[:, c, 1:T], f_cv[:, c, 0:T - 1], col("w_conv", c), f_bc[:, c, 1:T],
                                         ALU.mult, ALU.add)
        link(ins)
        for c in range(DC):
            ins = v.scalar_tensor_tensor(f_bc[:, c, 0:T - 1], f_cv[:, c, 1:T], col("w_conv", 2 * DC + c),
                                         f_bc[:, c, 0:T - 1], ALU.mult, ALU.add)
        link(ins)
        link(v.tensor_tensor(f_bc[:, :, :], f_bc[:, :, :], f_b[:, :, :], ALU.mult))
        link(v.tensor_copy(bc_high[:, :, :], f_bc[:, :, :]))
        v.tensor_tensor(bc_low[:, :, :], f_bc[:, :, :], bc_high[:, :, :].bitcast(fp32), ALU.subtract)\
            .then_inc(S["conv_ready"], 1)
        low("fourier_out", 0)
        dve.wait_ge(S["conv_ready"], 1)
        modulation(8)
        low("conv_out", 0)
        for s in range(6, 10):
            for half in range(2):
                copied(dve, f"in{s}", half)
        for i in range(4):
            filled(dve, "fourier_out", i)
            two = slice(2 * i, 2 * i + 2)
            frees(v.tensor_tensor(f_z[:, two, :].rearrange("p c t -> p (c t)"), work_bank("fourier_out", i)[:, :],
                                  f_ga[:, two, :].rearrange("p c t -> p (c t)"), ALU.mult), "fourier_out", i)
        low("conv_out", 1)
        for i in range(4):
            filled(dve, "conv_out", i)
            if i >= 2:
                dve.wait_ge(S["z_ready"], i - 1)
            if i == 2:
                low("w_o", 0)
            two = slice(2 * i, 2 * i + 2)
            frees(v.tensor_tensor(tmp[i % 2][:, :], work_bank("conv_out", i)[:, :],
                                  f_gb[:, two, :].rearrange("p c t -> p (c t)"), ALU.mult), "conv_out", i)
            copied(dve, "conv_out", i)
            copied(dve, "fourier_out", i)
            z = f_z[:, two, :].rearrange("p c t -> p (c t)")
            link(v.tensor_tensor(z, z, tmp[i % 2][:, :], ALU.add))
            zh = z_high[:, two, :].rearrange("p c t -> p (c t)")
            link(v.tensor_copy(zh, z))
            v.tensor_tensor(z_low[:, two, :].rearrange("p c t -> p (c t)"), z, zh.bitcast(fp32), ALU.subtract)\
                .then_inc(S["z_ready"], 1)
        modulation(9)
        modulated_gain(g_moe, range(4, 10), 32, "g_norm_moe")
        low("w_o", 1)

        def add_acc(name, gate=None, scale=1.0, batches=(0, 1)):
            for h in range(2):
                filled(dve, name, batches[h])
                for t in range(TT):
                    xs = x[:, t, 512 * h:512 * h + 512]
                    if gate is not None:
                        link(v.tensor_tensor(tmp[t][:, :], acc[t][h][:, :], gate[:, 512 * h:512 * h + 512], ALU.mult))
                        ins = v.tensor_tensor(xs, xs, tmp[t][:, :], ALU.add)
                    else:
                        ins = v.scalar_tensor_tensor(xs, acc[t][h][:, :], scale, xs, ALU.mult, ALU.add)
                    if h == 1:
                        x_updated(ins)
                    elif gate is not None:
                        link(ins)

        add_acc("w_o", gate=row("gate_m"))
        dve.wait_ge(S["x_new"], TT * 1)
        normalise(1, rows=True)
        modulation(10)
        modulation(11)
        filled(dve, "router", 0)
        b = work_bank("router", 0)
        for t in range(TT):
            ins = v.tensor_tensor(logit[:, t, :], b[:, t * NE:(t + 1) * NE], row("b_router"), ALU.add)
        frees(ins, "router", 0)
        copied(dve, "router", 0)
        link(v.reduce_max(rmax, logit[:, :, :], AX.X))
        v.tensor_tensor(logit[:, :, :], logit[:, :, :], wide(rmax[:, :].rearrange("p (t a) -> p t a", a=1), 2, NE),
                        ALU.subtract).then_inc(S["logit_ready"], 1)
        dve.wait_ge(S["exp_ready"], 1)
        link(v.reduce_sum(rsum, logit[:, :, :], AX.X))
        link(v.reciprocal(rsum, rsum))
        v.tensor_tensor(prob[:, :, :], logit[:, :, :], wide(rsum[:, :].rearrange("p (t a) -> p t a", a=1), 2, NE),
                        ALU.mult).then_inc(S["prob_ready"], 1)
        filled(dve, "probsT", 0)
        frees(v.tensor_copy(probT, work_bank("probsT", 0)[0:NE, 0:T]), "probsT", 0)
        copied(dve, "probsT", 0)
        src = probT
        for r in range(CAP // 8):
            link(v.max(top8[0:NE, :], src))
            link(v.match_replace(probW, top8[0:NE, :], src, -1.0))
            src = probW
        v.tensor_scalar(mask, probW, 0.0, None, ALU.is_lt).then_inc(S["mask_ready"], 1)
        filled(dve, "maskT", 0)
        frees(v.tensor_copy(maskT[:, :, :].rearrange("p t e -> p (t e)"), work_bank("maskT", 0)[:, 0:2 * NE]),
              "maskT", 0)
        copied(dve, "maskT", 0)
        filled(dve, "slots", 0)
        frees(v.scalar_tensor_tensor(slot_of[:, :, :].rearrange("p t e -> p (t e)"),
                                     work_bank("slots", 0)[:, 0:2 * NE], 1.0,
                                     maskT[:, :, :].rearrange("p t e -> p (t e)"), ALU.add, ALU.mult), "slots", 0)
        copied(dve, "slots", 0)
        link(v.tensor_scalar(slot_of[:, :, :], slot_of[:, :, :], -1.0, None, ALU.add))
        for t in range(TT):
            link(v.tensor_tensor(sel[:, t, :, :], wide(const("iota", "p (a s) -> p a s", a=1), 1, NE),
                                 wide(slot_of[:, t, :].rearrange("p (e a) -> p e a", a=1), 2, CAP), ALU.is_equal))
        dve.wait_ge(S["prob_ready"], 1)
        for t in range(TT):
            for g in range(4):
                ins = v.tensor_tensor(sel_prob[:, t, :, g, :], sel[:, t, :, :],
                                      wide(prob[:, t, :].rearrange("p (e a) -> p e a", a=1), 2, CAP), ALU.mult)
            ins.then_inc(S["sel_prob_ready"], 1)
        with dve.Fori(0, NE) as e:
            filled(dve, "experts", 7, e)
            copied(dve, "experts", 3, e)
            frees(v.tensor_tensor(e_h, work_bank("experts", 7)[:, :], e_act, ALU.mult), "experts", 7)
        add_acc("experts_end", gate=row("gate_f"), batches=(0, 0))
        dve.wait_ge(S["x_new"], TT * 2)
        mean(2)
        x_updated(v.scalar_tensor_tensor(x[:, 0, :], x[:, 0, :], rstd[:, 0:1], row("g_final"), ALU.mult, ALU.mult))
        x_updated(v.scalar_tensor_tensor(x[:, 1, :], x[:, 1, :], rstd[:, 1:2], row("g_final"), ALU.mult, ALU.mult))
        dve.wait_ge(S["x_new"], TT * 3)
        lam = col("lru_lambda_2", 0, 8)
        link(v.tensor_scalar(sp_b, lam, -1.0, 0.0, ALU.mult, ALU.max))
        v.scalar_tensor_tensor(sp_a, sp_b, -2.0, lam, ALU.mult, ALU.subtract)\
            .then_inc(S["lam_exp_in"], 1)
        normalise(3)
        dve.wait_ge(S["lam_exp_out"], 1)
        link(v.tensor_scalar(nsp8, sp_a, 2.0, None, ALU.add))
        link(v.reciprocal(nsp8, nsp8))
        link(v.tensor_tensor(sp_a, sp_a, nsp8, ALU.mult))
        link(v.tensor_tensor(nsp8, sp_a, sp_a, ALU.mult))
        link(v.tensor_scalar(sp8, nsp8, 1.0 / 17, 1.0 / 15, ALU.mult, ALU.add))
        for n in range(13, 0, -2):
            link(v.tensor_tensor(sp8, sp8, nsp8, ALU.mult))
            link(v.tensor_scalar(sp8, sp8, 1.0 / n, None, ALU.add))
        link(v.tensor_tensor(sp8, sp8, sp_a, ALU.mult))
        link(v.scalar_tensor_tensor(sp8, sp8, 2.0, sp_b, ALU.mult, ALU.add))
        link(v.tensor_scalar(nsp8, sp8, -8.0, None, ALU.mult))
        v.tensor_scalar(sp8, sp8, 8.0, None, ALU.mult).then_inc(S["sp_ready"], 1)
        v.memset(ki[:, :, :], 0.0).then_inc(S["zeroed"], 1)
        filled(dve, "norm2", 3)
        for h in range(8):
            ins = v.tensor_copy(rel_rep[:, h, :], wide(rel_in[:, h:h + 1], 1, P))
        ins.then_inc(S["rel_ready"], 1)
        for i in range(4):
            copied(dve, "lru_x", i)
        for c in range(DC):
            ins = v.tensor_scalar(l_ua[:, c, :], l_t[:, c, :], col("lru_conv_w_2", 3 * DC + c),
                                  col("lru_conv_b_2", c), ALU.mult, ALU.add)
        for s in (1, 2, 3):
            link(ins)
            for c in range(DC):
                ins = v.scalar_tensor_tensor(l_ua[:, c, s:T], l_t[:, c, 0:T - s], col("lru_conv_w_2", (3 - s) * DC + c),
                                             l_ua[:, c, s:T], ALU.mult, ALU.add)
        ins.then_inc(S["ua_ready"], 1)
        dve.wait_ge(S["ua_ready"], 1)
        for i in range(4, 8):
            copied(dve, "lru_ri", i)
        link(v.tensor_tensor(l_i[:, :, :], l_i[:, :, :], l_ua[:, :, :], ALU.mult))
        dve.wait_ge(S["tanh_done"], 1)
        link(v.tensor_scalar(l_tmp[:, :, :], l_t[:, :, :], 1.0, None, ALU.add))
        link(v.reciprocal(l_tmp[:, :, :], l_tmp[:, :, :]))
        v.tensor_tensor(l_t[:, :, :], l_t[:, :, :], l_tmp[:, :, :], ALU.mult).then_inc(S["mult_in"], 1)
        dve.wait_ge(S["mult_out"], 1)
        link(v.tensor_tensor(l_i[:, :, :], l_i[:, :, :], l_t[:, :, :], ALU.mult))
        dve.wait_ge(S["decay_done"], 1)
        for c in range(DC):
            ins = v.tensor_tensor_scan(out=l_ua[:, c, :], data0=l_a[:, c, :], data1=l_i[:, c, :], initial=0.0,
                                       op0=ALU.mult, op1=ALU.add)
        ins.then_inc(S["scan_done"], 1)
        dve.wait_ge(S["scan_done"], 1)
        for i in range(4):
            copied(dve, "lru_gate", i)
        v.tensor_tensor(l_ua[:, :, :], l_ua[:, :, :], l_g[:, :, :], ALU.mult).then_inc(S["lru_ready"], 1)
        for i in range(5):
            a, r = (q2[:, 2 * i:2 * i + 2, :] if i < 4 else k2[:, :, :]).rearrange("p c t -> p (c t)"), msq[i % 2]
            filled(dve, "qk_ms", i)
            frees(v.tensor_scalar(r[:, :], work_bank("qk_ms", i)[:, :], EPS, None, ALU.add), "qk_ms", i)
            copied(dve, "qk_ms", i)
            v.reciprocal(r[:, :], r[:, :]).then_inc(S["msq_ready"], 1)
            dve.wait_ge(S["rsq_ready"], i + 1)
            v.scalar_tensor_tensor(a, a, col("q_norm_2" if i < 4 else "k_norm_2"), r[:, :], ALU.mult, ALU.mult)\
                .then_inc(S["qk_ready"], 1)
        copied(dve, "kiwi", 1)
        for t in range(TT):
            for m in range(4):
                copied(dve, "score", 4 * t + m)
                r = relu_s[m % 2]
                for d in range(2):
                    w = wi[:, t, 2 * m + d:2 * m + d + 1]
                    if m == 0 and d == 0:
                        link(v.tensor_scalar(score[:, t, :], r[:, 0:T], w, None, ALU.mult))
                    else:
                        ins = v.scalar_tensor_tensor(score[:, t, :], r[:, d * T:(d + 1) * T], w, score[:, t, :],
                                                     ALU.mult, ALU.add)
                        if d == 0:
                            link(ins)
                ins.then_inc(S["relu_used"], 1)
                dve.wait_ge(S["relu_used"], 4 * t + m + 1)
        link(v.tensor_tensor(score[:, :, :], score[:, :, :], causal16, ALU.add))
        for t in range(TT):
            src = score[:, t, :]
            for r in range(8):
                link(v.max(t8, src))
                link(v.match_replace(score_w[:, t, :], t8, src, -3e38))
                src = score_w[:, t, :]
        link(v.tensor_scalar(score_w[:, :, :], score_w[:, :, :], -2e38, NEG, ALU.is_gt, ALU.mult))
        link(v.tensor_tensor(score_w[:, :, :], score_w[:, :, :], causal16, ALU.add))
        dve.wait_ge(S["bias_in"], 16 * TT)
        for t in range(TT):
            for m in range(4):
                filled(dve, "logits2", 4 * t + m)
                frees(v.scalar_tensor_tensor(att[t][:, 2 * m:2 * m + 2, :].rearrange("p h s -> p (h s)"),
                                             work_bank("logits2", 4 * t + m)[:, :], P ** -0.5,
                                             bias2[:, t, 2 * m:2 * m + 2, :].rearrange("p h s -> p (h s)"),
                                             ALU.mult, ALU.add), "logits2", 4 * t + m)
            for m in range(4):
                copied(dve, "logits2", 4 * t + m)
            link(v.tensor_tensor(att[t][:, :, :], att[t][:, :, :],
                                 wide(score_w[:, t, :].rearrange("p (a s) -> p a s", a=1), 1, 8), ALU.add))
            v.tensor_reduce(nm2[:, t, :], att[t][:, :, :], AX.X, ALU.max, negate=True).then_inc(S["att_in"], 1)
        for t in range(TT):
            for i in (2 * t, 2 * t + 1):
                copied(dve, "gate_a", i)
                filled(dve, "lru_out", i)
                two = slice(2 * i, 2 * i + 2)
                frees(v.tensor_tensor(merged[:, two, :].rearrange("p c t -> p (c t)"), work_bank("lru_out", i)[:, :],
                                      l_a[:, two, :].rearrange("p c t -> p (c t)"), ALU.mult), "lru_out", i)
            dve.wait_ge(S["att_exp"], t + 1)
            link(v.reciprocal(rs2[:, t, :], rs2[:, t, :]))
            v.tensor_tensor(att[t][:, :, :], att[t][:, :, :],
                            wide(rs2[:, t, :].rearrange("p (h a) -> p h a", a=1), 2, T), ALU.mult)\
                .then_inc(S["att_ready"], 1)
        for i in range(4):
            copied(dve, "gate_b", i)
            filled(dve, "attn_out", i)
            two = slice(2 * i, 2 * i + 2)
            frees(v.tensor_tensor(tmp[i % 2][:, :], work_bank("attn_out", i)[:, :],
                                  l_i[:, two, :].rearrange("p c t -> p (c t)"), ALU.mult), "attn_out", i)
            copied(dve, "attn_out", i)
            copied(dve, "lru_out", i)
            a = merged[:, two, :].rearrange("p c t -> p (c t)")
            v.tensor_tensor(a, a, tmp[i % 2][:, :], ALU.add).then_inc(S["merged_ready"], 1)
        low("ffn2", 0)
        add_acc("w_out2")
        dve.wait_ge(S["x_new"], TT * 4)
        normalise(4)
        low_norm("norm3", 1, col("ffn_norm_2", 0, 8))
        n_f = F2 // P
        c0 = col_at["ffn_conv_w_2"][0]
        cb = col_at["ffn_conv_b_2"][0]
        link2 = sem("conv_step")
        with dve.Fori(0, plan.times["ffn2"]) as it:
            for b in range(4):
                if b % 2 == 0:
                    low("ffn2", 1 + b // 2, it)
                filled(dve, "ffn2", b, it)
                g, fc = work_bank("ffn2", b), f_conv[b % 2]
                wc = lambda j: cols[:, bass.ds(c0 + j * n_f + b + 4 * it, 1)]
                v.tensor_scalar(fc, g[:, 0:T], wc(2), cols[:, bass.ds(cb + b + 4 * it, 1)], ALU.mult, ALU.add)\
                    .then_inc(link2, 1)
                dve.wait_ge(link2, 8 * it + 2 * b + 1)
                v.scalar_tensor_tensor(fc[:, 1:T], g[:, 0:T - 1], wc(1), fc[:, 1:T], ALU.mult, ALU.add)\
                    .then_inc(link2, 1)
                dve.wait_ge(link2, 8 * it + 2 * b + 2)
                v.scalar_tensor_tensor(fc[:, 2:T], g[:, 0:T - 2], wc(0), fc[:, 2:T], ALU.mult, ALU.add)\
                    .then_inc(S["conv_in"], 1)
                dve.wait_ge(S["gelu_done"], 4 * it + b + 1)
                hidden("ffn2", b, it)
            low("ffn2", 0, it + 1)
        add_acc("ffn2_end", batches=(0, 0))
        dve.wait_ge(S["x_new"], TT * 5)
        normalise(5)
        low_norm("norm4", 2, col("ple_norm_2", 0, 8))
        low("ple", 1)
        low("ffn3_0", 0)
        for i in range(4):
            h, t = i // 2, i % 2
            copied(dve, "ple", i)
            filled(dve, "ple", 4 + i)
            frees(v.tensor_tensor(tmp[i][:, :], work_bank("ple", 4 + i)[:, :], p_gate[:, h, t, :], ALU.mult),
                  "ple", 4 + i)
            copied(dve, "ple", 4 + i)
            xs = x[:, t, 512 * h:512 * h + 512]
            ins = v.tensor_tensor(xs, xs, tmp[i][:, :], ALU.add)
            if h == 1:
                x_updated(ins)
            else:
                link(ins)
        dve.wait_ge(S["x_new"], TT * 6)

        gelus = [4 * plan.times["ffn2"]]

        def ffn3(n, k, following=None):
            normalise(k)
            low_norm(f"ffnorm{n}", (3, 5, 6, 8)[n], col("ffn1_norm_3" if n % 2 == 0 else "ffn2_norm_3", 8 * (n // 2), 8))
            name = f"ffn3_{n}"

            def tiles(name, n_b, base, it, per):
                for b in range(n_b):
                    if b % 2 == 0:
                        low(name, 1 + b // 2, it)
                    dve.wait_ge(S["gelu_done"], base + b + 1 + per * it)
                    hidden(name, b, it)

            with dve.Fori(0, plan.times[name]) as it:
                tiles(name, 4, gelus[0], it, 4)
                low(name, 0, it + 1)
            gelus[0] += 4 * plan.times[name]
            filled(dve, name, 4, plan.times[name] - 1)
            tiles(name + "_end", 2, gelus[0], 0, 0)
            gelus[0] += 2
            if following:
                low(following, 0)
            add_acc(name + "_end", scale=0.5, batches=(2, 2))

        def rope(name, i, a, n):
            filled(dve, name, i)
            sin = const("rope_sin", "p (a t) -> p a t", a=1)
            cos = const("rope_cos", "p (a t) -> p a t", a=1)
            if n > 1:
                sin, cos = wide(sin, 1, n), wide(cos, 1, n)
            t_ = tmp[i % 2][:, 0:n * T].rearrange("p (c t) -> p c t", c=n)
            frees(v.tensor_tensor(t_, work_bank(name, i)[:, 0:n * T].rearrange("p (c t) -> p c t", c=n), sin,
                                  ALU.mult), name, i)
            link(v.tensor_tensor(a, a, cos, ALU.mult))
            copied(dve, name, i)
            v.tensor_tensor(a, a, t_, ALU.add).then_inc(S["rope_ready"], 1)

        def row_max(name, i, b, slot):
            filled(dve, name, i)
            link(v.tensor_reduce(nm3[slot], b[:, :].rearrange("p (d s) -> p d s", d=2), AX.X,
                                 ALU.max, negate=True))
            v.tensor_scalar(nm3[slot], nm3[slot], 64 ** -0.5, None, ALU.mult).then_inc(S["max3_ready"], 1)

        def weigh(n, slot, gate):
            dve.wait_ge(S["exp3_done"], n)
            link(v.reciprocal(rw3[slot], rs3[slot]))
            link(v.tensor_tensor(rw3[slot], rw3[slot], gate, ALU.mult))
            v.tensor_tensor(p3[slot][:, :, :], p3[slot][:, :, :],
                            wide(rw3[slot].rearrange("p (d a) -> p d a", a=1), 2, T), ALU.mult)\
                .then_inc(S["p3_ready"], 1)

        ffn3(0, 6, "nsa_kv0")
        dve.wait_ge(S["x_new"], TT * 7)
        normalise(7)
        low_norm("nsa_norm", 4, col("mix_norm_3", 0, 8))
        low("nsa_kv12", 0)
        low("nsa_kv12", 1)
        low("nsa_q", 0)
        for i in range(3):
            copied(dve, "nsa_kv0" if i == 0 else "nsa_kv12", max(2 * i - 2, 0))
            rope("nsa_rope_k", i, kraw[:, 2 * i:2 * i + 2, :], 2)
        low("nsa_q", 1)
        dve.wait_ge(S["rope_ready"], 3)
        v.memset(kc[:, :, :, :], 0.0).then_inc(S["zeroed"], 1)
        for src, dst in ((kraw[:, 0:2, :], kp), (vraw, vp)):
            for half in range(2):
                v.tensor_copy(dst[0:64, half:4:2, :], src[64 * half:64 * half + 64, :, :])
                ins = v.tensor_copy(dst[64:128, half:4:2, 0:T - 1], src[64 * half:64 * half + 64, :, 1:T])
        link(ins)
        for i, (src, pe_) in enumerate(((kp, "nsa_ck_pe_3"), (vp, "nsa_cv_pe_3"))):
            for a in range(2):
                win = src[:, :, BS * a:BS * a + BS * NB].rearrange("p g (b m two) -> p m g b two", b=NB, two=2)
                bias = wide(wide(col(pe_, 8 * a, 8).rearrange("p (m a b) -> p m a b", a=1, b=1), 2, 4), 3, NB)
                for m in range(8):
                    ins = v.tensor_tensor(xb[i][:, 8 * a + m, :, :], win[:, m, :, :, 0], bias[:, m, :, :], ALU.add)
        ins.then_inc(S["cmp_x_ready"], 1)
        dve.wait_ge(S["cmp_x_ready"], 1)
        for br in range(2):
            link(v.memset(A[3 + br][:, :], 0.0))
            for half in range(2):
                for d in range(2):
                    ins = v.tensor_copy(kd[br][64 * d:64 * d + 64, half:4:2, d, :],
                                        kraw[64 * half:64 * half + 64, 2 + 2 * br:4 + 2 * br, :])
        link(ins)
        for i in range(4):
            copied(dve, "nsa_q", i)
            rope("nsa_rope", i, q3[:, 2 * i:2 * i + 2, :], 2)
        copied(dve, "nsa_g", 0)
        for t in range(TT):
            filled(dve, "cmp_s", t)
            frees(v.tensor_scalar(pc[:, t, :, :].rearrange("p h b -> p (h b)"), work_bank("cmp_s", t)[:, 0:240],
                                  64 ** -0.5, None, ALU.mult), "cmp_s", t)
        for t in range(TT):
            copied(dve, "cmp_s", t)
        for t in range(TT):
            ins = v.tensor_tensor(pc[:, t, :, :], pc[:, t, :, :],
                                  wide(const("cmp_neg", "p (t a b) -> p t a b", t=TT, a=1)[:, t, :, :], 1, 16),
                                  ALU.add)
        link(ins)
        link(v.reduce_max(cm[:, :, :], pc[:, :, :, :], AX.X))
        v.tensor_tensor(pc[:, :, :, :].rearrange("p t h b -> p (t h) b"), pc[:, :, :, :].rearrange("p t h b -> p (t h) b"),
                        wide(cm[:, :, :].rearrange("p t (h a) -> p (t h) a", a=1), 2, NB),
                        ALU.subtract).then_inc(S["cmp_in"], 1)
        for s in range(4):
            row_max("nsa_heads", s, bank[s], s)
        dve.wait_ge(S["cmp_exp"], 1)
        link(v.reduce_sum(cr[:, :, :], pc[:, :, :, :], AX.X))
        link(v.reciprocal(cr[:, :, :], cr[:, :, :]))
        link(v.tensor_tensor(cr[:, :, :], cr[:, :, :], gate3[:, :, 0, :], ALU.mult))
        link(v.tensor_tensor(pc[:, :, :, :].rearrange("p t h b -> p (t h) b"), pc[:, :, :, :].rearrange("p t h b -> p (t h) b"),
                             wide(cr[:, :, :].rearrange("p t (h a) -> p (t h) a", a=1), 2, NB), ALU.mult))
        for t in range(TT):
            ins = v.tensor_tensor(pc[:, t, :, :], pc[:, t, :, :],
                                  wide(const("cmp_one", "p (t a b) -> p t a b", t=TT, a=1)[:, t, :, :], 1, 16),
                                  ALU.mult)
        ins.then_inc(S["cmp_ready"], 1)
        def attention_low(name, i, n, m):
            dve.wait_ge(S["o_high"], n)
            frees(v.tensor_tensor(o_low[:, m, :], work_bank(name, i)[:, 0:T], o_high[:, m, :].bitcast(fp32),
                                  ALU.subtract), name, i)

        for m in range(8):
            for s in range(4):
                br, t = s // 2, s % 2
                weigh(4 * m + s + 1, 4 * (m % 2) + s, gate3[:, t, 1 + br, 2 * m:2 * m + 2])
            if m:
                attention_low("nsa_heads", pair_rest(m - 1, 4, 6) + 5, m, m - 1)
            if m < 7:
                for s in range(4):
                    row_max("nsa_heads", pair_scores(m + 1, 4, 6) + s, bank[s], 4 * ((m + 1) % 2) + s)
        low("nsa_out", 0)
        attention_low("nsa_heads", pair_rest(7, 4, 6) + 5, 8, 7)
        low("nsa_out", 1)
        low("ffn3_1", 0)
        add_acc("nsa_out")
        dve.wait_ge(S["x_new"], TT * 8)
        ffn3(1, 8, "ffn3_2")
        dve.wait_ge(S["x_new"], TT * 9)
        ffn3(2, 9, "swa_kv")
        dve.wait_ge(S["x_new"], TT * 10)
        normalise(10)
        low_norm("swa_norm", 7, col("mix_norm_3", 8, 8))
        low("swa_q", 0)
        low("swa_q", 1)
        copied(dve, "swa_kv", 0)
        filled(dve, "swa_rope_k", 0)
        frees(v.tensor_tensor(tmp[0][:, 0:T], work_bank("swa_rope_k", 0)[:, 0:T], const("rope_sin"), ALU.mult),
              "swa_rope_k", 0)
        link(v.tensor_tensor(k4, k4, const("rope_cos"), ALU.mult))
        copied(dve, "swa_rope_k", 0)
        link(v.tensor_tensor(k4, k4, tmp[0][:, 0:T], ALU.add))
        link(v.memset(kd4[:, :, :, :], 0.0))
        for half in range(2):
            for d in range(2):
                ins = v.tensor_copy(kd4[64 * d:64 * d + 64, half, d, :], k4[64 * half:64 * half + 64, :])
        ins.then_inc(S["rope_ready"], 1)
        for i in range(4):
            copied(dve, "swa_q", i)
            rope("swa_rope", i, q3[:, 2 * i:2 * i + 2, :], 2)

        def swa_max(m):
            sinks = row("sinks")[:, 2 * m:2 * m + 2]
            for t in range(TT):
                slot = 2 * (m % 2) + t
                filled(dve, "swa_heads", pair_scores(m, 2, 3) + t)
                link(v.tensor_reduce(nm3[slot], bank[slot][:, :].rearrange("p (d s) -> p d s", d=2),
                                     AX.X, ALU.max))
                link(v.scalar_tensor_tensor(nm3[slot], nm3[slot], 64 ** -0.5, sinks, ALU.mult, ALU.max))
                link(v.tensor_tensor(sk[slot], sinks, nm3[slot], ALU.subtract))
                v.tensor_scalar(nm3[slot], nm3[slot], -1.0, None, ALU.mult).then_inc(S["max3_ready"], 1)

        swa_max(0)
        for m in range(8):
            for t in range(TT):
                slot = 2 * (m % 2) + t
                dve.wait_ge(S["exp3_done"], 32 + 2 * m + t + 1)
                link(v.tensor_tensor(rw3[slot], rs3[slot], sk[slot], ALU.add))
                link(v.reciprocal(rw3[slot], rw3[slot]))
                v.tensor_tensor(p3[slot][:, :, :], p3[slot][:, :, :],
                                wide(rw3[slot].rearrange("p (d a) -> p d a", a=1), 2, T), ALU.mult)\
                    .then_inc(S["p3_ready"], 1)
            if m:
                attention_low("swa_heads", pair_rest(m - 1, 2, 3) + 2, 8 + m, m - 1)
            if m < 7:
                swa_max(m + 1)
        low("swa_out", 0)
        attention_low("swa_heads", pair_rest(7, 2, 3) + 2, 16, 7)
        low("swa_out", 1)
        low("ffn3_3", 0)
        add_acc("swa_out")
        dve.wait_ge(S["x_new"], TT * 11)
        ffn3(3, 11)
        dve.wait_ge(S["x_new"], TT * 12)
        mean(12)
        dve.wait_ge(S["final_row_in"], 16)
        for t in range(TT):
            v.scalar_tensor_tensor(xn[:, t, :], x[:, t, :], rstd[:, t:t + 1], row("gate_m"), ALU.mult, ALU.mult)\
                .then_inc(S["out_ready"], 1)

    ctx.close()


OUT_SHAPE = (1, T, D)
WEIGHTS = {
    "w_ada": D, "w_in": D, "w_fourier": 512, "w_conv_out": D, "w_o": D, "w_router": D,
    "w_gate_e": NE * D, "w_up_e": NE * D, "w_down_e": NE * DE, "w_in_2": D, "lru_wa_2": D, "lru_wx_2": D,
    "w_lru_br_2": D, "w_attn_br_2": D, "w_out_2": D, "w_up_2": D, "w_down_2": F2, "w_ple_gate_2": D,
    "w_ple_proj_2": 256, "rel_bias_2": 32, "ffn1_w_gu_3": 2 * D, "ffn1_w_down_3": 2 * F3,
    "ffn2_w_gu_3": 2 * D, "ffn2_w_down_3": 2 * F3, "nsa_w_in_3": D, "nsa_ck_w1_3": 2048, "nsa_ck_w2_3": P,
    "nsa_cv_w1_3": 2048, "nsa_cv_w2_3": P, "nsa_w_out_3": D, "swa_w_in_3": D, "swa_w_out_3": D, "x": T,
}


def kernel(**inputs):
    import numpy as _np
    import concourse.bacc as _bacc
    from concourse import mybir as _mybir
    from concourse.bass_utils import run_bass_kernel_spmd as _run

    def given(name):
        return _np.asarray(inputs[name])

    nc = _bacc.Bacc("TRN2", target_bir_lowering=False, num_devices=1)
    arrays = {name: _np.ascontiguousarray(given(name)).reshape(rows, -1) for name, rows in WEIGHTS.items()}
    (arrays["consts"], const_at), arrays["masks"] = shape_constants()
    arrays["cols"], col_at = column_inputs(given)
    arrays["rows"], row_at = row_inputs(given)
    arrays["final_norm"] = _np.ascontiguousarray(given("final_norm_3").reshape(1, D))
    arrays["pT"] = _np.ascontiguousarray(given("p_2").reshape(T, 256).T)
    handles = {n: nc.dram_tensor(f"in_{n}", a.shape, _mybir.dt.from_np(a.dtype), kind="ExternalInput").ap()
               for n, a in arrays.items()}
    out = nc.dram_tensor("out_0", (T, D), _mybir.dt.float32, kind="ExternalOutput").ap()
    network(nc, lambda name: handles[name], out, const_at, col_at, row_at)
    r = _run(nc, [{f"in_{n}": a for n, a in arrays.items()}], core_ids=[0])
    return r.results[0]["out_0"].reshape(OUT_SHAPE)
```
